# Optimizing a Trainium2 kernel written in Bass

```python
import jax, jax.numpy as jnp
from jax import lax
import numpy as np

D_MODEL = 2048
BATCH = 1
SEQ = 512
DEPTH = 1

HEAD_DIM = 64
ATTN_HEADS = 16
ATTN_KV_HEADS = 4
ATTN_GROUP = ATTN_HEADS // ATTN_KV_HEADS
ATTN_WIDTH = ATTN_HEADS * HEAD_DIM
KV_WIDTH = ATTN_KV_HEADS * HEAD_DIM
WINDOW = 128
BLOCK = 128

RWKV_HEADS = 16
RWKV_HEAD_SIZE = 64
RWKV_WIDTH = RWKV_HEADS * RWKV_HEAD_SIZE
DECAY_RANK = 64
ICLR_RANK = 64
VRES_RANK = 32
GATE_RANK = 160
SHIFT_WIDTH = 3 * RWKV_WIDTH + DECAY_RANK + ICLR_RANK + GATE_RANK

FFN_HIDDEN = -(-8 * D_MODEL // (3 * 256)) * 256

IN_SPLITS = (ATTN_WIDTH, KV_WIDTH, KV_WIDTH, SHIFT_WIDTH, D_MODEL, D_MODEL)
N_IN = sum(IN_SPLITS)

NORM_EPS = 1e-5
LNX_EPS = 64e-5

kernel_name = 'hybrid_swa_sink_alibi_rwkv7_gated_swiglu'

def split_last(t, sizes):
    idx = np.cumsum(np.array(sizes))[:-1].tolist()
    return jnp.split(t, idx, axis=-1)

def rms_norm(x, g):
    x32 = x.astype(jnp.float32)
    y = x32 * lax.rsqrt(jnp.mean(x32 * x32, axis=-1, keepdims=True) + NORM_EPS)
    return (y * g.astype(jnp.float32)).astype(x.dtype)

def token_shift_mix(p, mu):
    prev = jnp.pad(p, ((0, 0), (1, 0), (0, 0)))[:, :-1]
    return p + (prev - p) * mu

def alibi_slopes():
    return jnp.exp2(-8.0 * jnp.arange(1, ATTN_HEADS + 1, dtype=jnp.float32) / ATTN_HEADS)

def sliding_window_attention(q, k, v, sinks):
    B, T, _ = q.shape
    nb = T // BLOCK
    qb = q.reshape(B, nb, BLOCK, ATTN_KV_HEADS, ATTN_GROUP, HEAD_DIM)
    kb = k.reshape(B, nb, BLOCK, ATTN_KV_HEADS, HEAD_DIM)
    vb = v.reshape(B, nb, BLOCK, ATTN_KV_HEADS, HEAD_DIM)

    def with_prev(t):
        prev = jnp.concatenate([jnp.zeros_like(t[:, :1]), t[:, :-1]], axis=1)
        return jnp.concatenate([prev, t], axis=2)

    kw, vw = with_prev(kb), with_prev(vb)
    s = jnp.einsum('bnqkgd,bnskd->bnkgqs', qb, kw).astype(jnp.float32) * (HEAD_DIM ** -0.5)
    qi = jnp.arange(BLOCK)[:, None]
    kj = jnp.arange(2 * BLOCK)[None, :]
    dist = BLOCK + qi - kj
    kpos = (jnp.arange(nb)[:, None] - 1) * BLOCK + jnp.arange(2 * BLOCK)[None, :]
    valid = ((dist >= 0) & (dist < WINDOW))[None] & (kpos >= 0)[:, None, :]
    slopes = alibi_slopes().reshape(ATTN_KV_HEADS, ATTN_GROUP)
    s = s - slopes[:, :, None, None] * dist.astype(jnp.float32)
    s = jnp.where(valid[None, :, None, None], s, -jnp.inf)
    sink = jnp.broadcast_to(sinks.astype(jnp.float32).reshape(ATTN_KV_HEADS, ATTN_GROUP, 1, 1),
                            s.shape[:-1] + (1,))
    p = jax.nn.softmax(jnp.concatenate([s, sink], axis=-1), axis=-1)[..., :-1]
    o = jnp.einsum('bnkgqs,bnskd->bnqkgd', p.astype(v.dtype), vw)
    return o.reshape(B, T, ATTN_WIDTH)

def rwkv7_time_mix(r, k, v, dw, da, dg, decay_up, decay_bias, iclr_up, iclr_bias, gate_up,
                   k_k, k_a, r_k, lnx_w, lnx_b):
    B, T, C = r.shape
    H, N = RWKV_HEADS, RWKV_HEAD_SIZE
    f32 = jnp.float32
    w_log = -jax.nn.softplus(-(decay_bias + jnp.tanh(dw) @ decay_up).astype(f32)) - 0.5
    decay = jnp.exp(-jnp.exp(w_log))
    a = jax.nn.sigmoid((iclr_bias + da @ iclr_up).astype(f32))
    g = jax.nn.sigmoid(dg) @ gate_up
    kk = (k * k_k).astype(f32).reshape(B, T, H, N)
    kk = kk / jnp.maximum(jnp.sqrt(jnp.sum(kk * kk, axis=-1, keepdims=True)), 1e-12)
    k_mod = k.astype(f32) * (1.0 + (a - 1.0) * k_a.astype(f32))

    def heads_tm(t):
        return t.astype(f32).reshape(B, T, H, N).transpose(1, 0, 2, 3)

    def step(S, inp):
        r_t, w_t, k_t, v_t, kk_t, a_t = inp
        sa = jnp.einsum('bhij,bhj->bhi', S, -kk_t)
        S = (S * w_t[:, :, None, :] + sa[..., None] * (kk_t * a_t)[:, :, None, :]
             + v_t[..., None] * k_t[:, :, None, :])
        return S, jnp.einsum('bhij,bhj->bhi', S, r_t)

    S0 = jnp.zeros((B, H, N, N), f32)
    _, y = lax.scan(step, S0, (heads_tm(r), heads_tm(decay), heads_tm(k_mod), heads_tm(v),
                               kk.transpose(1, 0, 2, 3), heads_tm(a)))
    y = y.transpose(1, 0, 2, 3)
    mean = jnp.mean(y, axis=-1, keepdims=True)
    var = jnp.mean(jnp.square(y - mean), axis=-1, keepdims=True)
    y = ((y - mean) * lax.rsqrt(var + LNX_EPS)).reshape(B, T, C)
    y = y * lnx_w.astype(f32) + lnx_b.astype(f32)
    r4 = r.astype(f32).reshape(B, T, H, N)
    bonus = jnp.sum(r4 * k_mod.reshape(B, T, H, N) * r_k.astype(f32), axis=-1, keepdims=True)
    y = y + (bonus * v.astype(f32).reshape(B, T, H, N)).reshape(B, T, C)
    return y.astype(r.dtype) * g

def setup_inputs(seed: int = 0) -> dict:
    key = jax.random.key(seed)
    ks = jax.random.split(key, 32)
    L, D, C = DEPTH, D_MODEL, RWKV_WIDTH

    def nrm(k, shape, scale):
        return jax.random.normal(k, shape, jnp.float32) * scale

    def uni(k, shape, lo, hi):
        return jax.random.uniform(k, shape, jnp.float32, lo, hi)

    return {
        'x': nrm(ks[0], (BATCH, SEQ, D), 1.0),
        'norm_mix': 1.0 + nrm(ks[1], (L, D), 0.02),
        'norm_ffn': 1.0 + nrm(ks[2], (L, D), 0.02),
        'norm_final': 1.0 + nrm(ks[3], (D,), 0.02),
        'w_in': nrm(ks[4], (L, D, N_IN), D ** -0.5),
        'attn_sinks': nrm(ks[5], (L, ATTN_HEADS), 0.5),
        'tshift_mix': uni(ks[6], (L, SHIFT_WIDTH), 0.0, 1.0),
        'decay_up': nrm(ks[7], (L, DECAY_RANK, C), 0.1 * DECAY_RANK ** -0.5),
        'decay_bias': uni(ks[8], (L, C), -5.0, 1.0),
        'iclr_up': nrm(ks[9], (L, ICLR_RANK, C), 0.1 * ICLR_RANK ** -0.5),
        'iclr_bias': nrm(ks[10], (L, C), 0.1),
        'gate_up': nrm(ks[11], (L, GATE_RANK, C), GATE_RANK ** -0.5),
        'k_k': 0.85 + nrm(ks[12], (L, C), 0.05),
        'k_a': 1.0 + nrm(ks[13], (L, C), 0.05),
        'r_k': nrm(ks[14], (L, RWKV_HEADS, RWKV_HEAD_SIZE), 0.1),
        'lnx_w': 1.0 + nrm(ks[15], (L, C), 0.02),
        'lnx_b': nrm(ks[16], (L, C), 0.02),
        'vres_down': nrm(ks[17], (L - 1, D, VRES_RANK), D ** -0.5),
        'vres_mix': uni(ks[18], (L - 1, VRES_RANK), 0.0, 1.0),
        'vres_up': nrm(ks[19], (L - 1, VRES_RANK, C), VRES_RANK ** -0.5),
        'vres_bias': 1.0 + nrm(ks[20], (L - 1, C), 0.1),
        'w_branch_attn': nrm(ks[21], (L, ATTN_WIDTH, D), ATTN_WIDTH ** -0.5),
        'w_branch_rwkv': nrm(ks[22], (L, C, D), C ** -0.5),
        'w_out': nrm(ks[23], (L, D, D), D ** -0.5),
        'ffn_gate': nrm(ks[24], (L, D, FFN_HIDDEN), D ** -0.5),
        'ffn_up': nrm(ks[25], (L, D, FFN_HIDDEN), D ** -0.5),
        'ffn_down': nrm(ks[26], (L, FFN_HIDDEN, D), FFN_HIDDEN ** -0.5),
    }

def reference(x, norm_mix, norm_ffn, norm_final, w_in, attn_sinks, tshift_mix, decay_up,
              decay_bias, iclr_up, iclr_bias, gate_up, k_k, k_a, r_k, lnx_w, lnx_b,
              vres_down, vres_mix, vres_up, vres_bias, w_branch_attn, w_branch_rwkv, w_out,
              ffn_gate, ffn_up, ffn_down):
    v_first = None
    for l in range(DEPTH):
        h = rms_norm(x, norm_mix[l])
        p = h @ w_in[l]
        q, k_att, v_att, rw, gate_a, gate_b = split_last(p, IN_SPLITS)
        rw = token_shift_mix(rw, tshift_mix[l])
        r, k, v, dw, da, dg = split_last(
            rw, (RWKV_WIDTH, RWKV_WIDTH, RWKV_WIDTH, DECAY_RANK, ICLR_RANK, GATE_RANK))
        if l == 0:
            v_first = v
        else:
            dv = token_shift_mix(h @ vres_down[l - 1], vres_mix[l - 1])
            v = v + (v_first - v) * jax.nn.sigmoid(vres_bias[l - 1] + dv @ vres_up[l - 1])
        y_attn = sliding_window_attention(q, k_att, v_att, attn_sinks[l])
        y_rwkv = rwkv7_time_mix(r, k, v, dw, da, dg, decay_up[l], decay_bias[l], iclr_up[l],
                                iclr_bias[l], gate_up[l], k_k[l], k_a[l], r_k[l],
                                lnx_w[l], lnx_b[l])
        merged = (jax.nn.sigmoid(gate_a) * (y_attn @ w_branch_attn[l])
                  + jax.nn.sigmoid(gate_b) * (y_rwkv @ w_branch_rwkv[l]))
        x = x + merged @ w_out[l]
        h = rms_norm(x, norm_ffn[l])
        x = x + (jax.nn.silu(h @ ffn_gate[l]) * (h @ ffn_up[l])) @ ffn_down[l]
    return rms_norm(x, norm_final)


_drawn_inputs = setup_inputs


def setup_inputs(seed=0):
    import zlib

    import numpy as np

    out = dict(_drawn_inputs(seed))
    spreads = {}
    factors = {'norm_mix': 4.288,
     'norm_ffn': 13.488,
     'norm_final': 25.405,
     'attn_sinks': 154.244,
     'decay_up': 22.786,
     'iclr_up': 4.41,
     'iclr_bias': 4.307,
     'k_k': 45.403,
     'k_a': 3.442,
     'lnx_w': 64.0,
     'lnx_b': 64.0}
    for name, (base, spread) in spreads.items():
        noise = np.random.default_rng([zlib.crc32(name.encode()), seed]).standard_normal(out[name].shape)
        drawn = base * np.exp(spread * noise) if base else spread * noise
        out[name] = __import__('jax').numpy.asarray(drawn.astype(out[name].dtype))
    for name, factor in factors.items():
        out[name] = (out[name] * factor).astype(out[name].dtype)
    return out
```

```python
import math
from contextlib import ExitStack

import numpy as np
import concourse.bass as bass
from concourse import mybir

P = 128
D_MODEL, T_SEQ = 2048, 512
KD = D_MODEL // P
HEADS, HD = 16, 64
KV_HEADS = 4
GROUP = HEADS // KV_HEADS
WIDTH = HEADS * HD
KV_WIDTH = KV_HEADS * HD
PAIRS = WIDTH // P
BLOCK = 128
NB = T_SEQ // BLOCK
CHUNK = 64
CHUNKS = T_SEQ // CHUNK
LEVELS = 5
LAMBDA = math.exp(-0.5)
DECAY_RANK, ICLR_RANK, GATE_RANK = 64, 64, 160
FFN_HIDDEN = -(-8 * D_MODEL // (3 * 256)) * 256
GROUPS_F = 4
FG = FFN_HIDDEN // P // GROUPS_F
NORM_EPS, LNX_EPS = 1e-5, 64e-5
SLOT = KD * P
DSLOT = FG * P

N_LOW = 3
ATT0 = N_LOW
ATT_TILES = 2 + GROUP
RW0 = ATT0 + KV_HEADS // 2 * ATT_TILES
RW_TILES = 7
MERGE0 = RW0 + PAIRS * RW_TILES
OUT0 = MERGE0 + KD
FFN0 = OUT0 + KD
FGRP = 2 * FG + KD
C_MUK, C_MUR, C_MUV, C_DB, C_IB, C_KK, C_KA, C_RK, C_LW, C_LB = range(10)
NCST = 10

FILL = {"prep": 4, "solve": 2, "level_a": 2, "level_b": 1, "rhs": 2, "u": 2, "state": 1,
        "y": 1, "center": 2}
assert (FILL["prep"] + FILL["solve"] + LEVELS * (FILL["level_a"] + FILL["level_b"])
        + CHUNKS * (FILL["rhs"] + FILL["u"] + FILL["state"]) + FILL["y"] + FILL["center"]) == 4 * KD


def index(i, per, off):
    return i * per + off, off % 2, i * (per // 2) + off // 2


def ffn_index(g, i, off):
    off += FFN0
    return g * FGRP + i * 2 + off, off % 2, g * (FGRP // 2) + i + off // 2


class Arena:

    def __init__(self, nc, at):
        self.nc, self.at = nc, at

    def __call__(self, name, shape, dt=mybir.dt.float32):
        size = int(np.prod(shape)) * (1 if dt == mybir.dt.uint8 else 4)
        t = self.nc.alloc_sbuf_tensor_at(name, [P] + list(shape), dt, offset=self.at)
        self.at += -(-size // 32) * 32
        return t


def build_layer(nc, xT, w_slots, w_ups, w_gu, w_down, norms, pair_cst, low_mu,
                sinks, consts, scan_lq, level_masks, att_cst, out):
    f32, f32r, u8 = mybir.dt.float32, mybir.dt.float32r, mybir.dt.uint8
    ALU, ACT = mybir.AluOpType, mybir.ActivationFunctionType
    AX = mybir.AxisListType.X
    MUL, ADD, SUB = ALU.mult, ALU.add, ALU.subtract
    V, A, PE = nc.vector, nc.scalar, nc.tensor

    gates_dram = nc.dram_tensor("gates_dram", (4 * PAIRS, P, T_SEQ), f32, kind="Internal").ap()
    y_dram = nc.dram_tensor("y_dram", (2 * PAIRS, P, T_SEQ), f32, kind="Internal").ap()
    x2_dram = nc.dram_tensor("x2_dram", (KD, P, T_SEQ), f32, kind="Internal").ap()

    keep = Arena(nc, -(-nc.sbuf_base // 64) * 64)
    raw = [keep(f"raw{s}", [SLOT]) for s in range(2)]
    whi = [keep(f"whi{s}", [SLOT], f32r) for s in range(2)]
    wlo = [keep(f"wlo{s}", [SLOT], f32r) for s in range(2)]
    H_hi = keep("H_hi", [KD, T_SEQ], f32r)
    H_lo = keep("H_lo", [KD, T_SEQ], f32r)
    cst = keep("cst", [5, P])
    ident, ones, head_ones, head_mean, head_center = (cst[:, i, :] for i in range(5))
    norm_g = keep("norm_g", [3, KD])

    front = Arena(nc, keep.at)
    low = [front(f"low{i}", [T_SEQ]) for i in range(3)]
    lowmu = front("lowmu", [3])
    proj = [front(f"proj{i}", [T_SEQ + 1]) for i in range(2)]
    tmp1 = front("tmp1", [T_SEQ])
    ups = [front(f"ups{i}", [3, P]) for i in range(2)]

    start = Arena(nc, front.at)
    X = start("X", [KD, T_SEQ])
    sq = [start(f"sq{i}", [T_SEQ]) for i in range(2)]
    rstd1 = start("rstd1", [T_SEQ])

    att = Arena(nc, start.at)
    qT = att("qT", [GROUP, T_SEQ])
    kT = att("kT", [BLOCK + T_SEQ])
    vT = att("vT", [T_SEQ])
    vtok = att("vtok", [NB + 1, P])
    probs = [att(f"probs{i}", [GROUP, 2 * BLOCK]) for i in range(2)]
    pT = att("pT", [2, T_SEQ])
    yatt = att("yatt", [GROUP, T_SEQ])
    att_const = att("att_const", [2 * 2 * BLOCK + HEADS])
    dist = att_const[:, 0:4 * BLOCK].rearrange("p (v k) -> p v k", v=2)
    slopes = att_const[:, 4 * BLOCK:4 * BLOCK + HEADS]
    sink = att("sink", [HEADS])
    slope_g, sink_g = att("slope_g", [2 * GROUP]), att("sink_g", [2 * GROUP])
    rowmax, negmax, rowsum, sinkexp, rowinv = (
        [att(f"{n}{i}", [GROUP]) for i in range(2)]
        for n in ("rowmax", "negmax", "rowsum", "sinkexp", "rowinv"))

    rw = Arena(nc, front.at)
    scanlq = rw("scanlq", [T_SEQ + 3 * P])
    scan_mask = scanlq[:, 0:T_SEQ]
    lq_mask = scanlq[:, T_SEQ:T_SEQ + 3 * P]
    masks = rw("masks", [LEVELS + 1, P], u8)
    cp_all = rw("cp_all", [PAIRS, NCST])
    cp = [rw(f"cp{i}", [NCST]) for i in range(2)]
    kbuf, rbuf, vbuf = (rw(n, [T_SEQ]) for n in ("kbuf", "rbuf", "vbuf"))
    grow, csum, a_in, icl = (rw(n, [T_SEQ]) for n in ("grow", "csum", "a_in", "icl"))
    kkbuf, kap, tmp2, gbuf, bonus = (
        rw(n, [T_SEQ]) for n in ("kkbuf", "kap", "tmp2", "gbuf", "bonus"))
    zq = rw("zq", [NB, 2, P])
    lq = rw("lq", [2, NB, 3, P])
    Ln = rw("Ln", [2, NB, P])
    Y = rw("Y", [2, NB, P])
    masks_f32 = Y[:].rearrange("p e t n -> p (e t n)")[:, 0:(LEVELS + 1) * P]
    Xi = rw("Xi", [2, NB, P])
    W1 = rw("W1", [2, NB, P])
    btok, ktok, vtk = (rw(n, [NB, P]) for n in ("btok", "ktok", "vtk"))
    lv, rhs, utok = (rw(n, [NB, P]) for n in ("lv", "rhs", "utok"))
    S, SA = rw("S", [P]), rw("SA", [P])
    gout = [rw(f"gout{i}", [T_SEQ]) for i in range(2)]

    back = Arena(nc, keep.at)
    M_hi, M_lo = back("M_hi", [KD, T_SEQ], f32r), back("M_lo", [KD, T_SEQ], f32r)
    late = Arena(nc, back.at)
    rstd = late("rstd", [T_SEQ])
    gin = [back(f"gin{i}", [2, T_SEQ]) for i in range(2)]
    ystage = [back(f"ystage{i}", [2, T_SEQ]) for i in range(2)]
    mrg = [back(f"mrg{i}", [T_SEQ]) for i in range(2)]
    mtmp = back("mtmp", [T_SEQ])
    xin = [late(f"xin{i}", [T_SEQ]) for i in range(2)]
    x2 = [late(f"x2_{i}", [T_SEQ]) for i in range(2)]
    sqacc, sqx = late("sqacc", [T_SEQ]), late("sqx", [T_SEQ])

    ffn = Arena(nc, keep.at)
    resid = ffn("resid", [KD, T_SEQ])
    G_hi = ffn("G_hi", [FG, T_SEQ], f32r)
    gate_n, gate_s, hid = (ffn(n, [T_SEQ]) for n in ("gate_n", "gate_s", "hid"))
    merged_end = keep.at + 2 * KD * T_SEQ * 4
    fend = Arena(nc, merged_end + T_SEQ * 4)
    G_lo = fend("G_lo", [FG, T_SEQ], f32r)
    facc, fsq = fend("facc", [T_SEQ]), fend("fsq", [T_SEQ])
    assert ffn.at <= merged_end
    assert max(rw.at, att.at, back.at, late.at, fend.at) <= nc.sbuf_usable_end

    with ExitStack() as ctx:
        def sem(name):
            return ctx.enter_context(nc.semaphore(name))

        dense = [ctx.enter_context(nc.psum_tensor(f"dense{i}", [P, T_SEQ], f32)) for i in range(2)]
        R = [ctx.enter_context(nc.psum_tensor(f"work{i}", [P, T_SEQ], f32)) for i in range(6)]
        RA, RB = (R[3], R[5]), (R[4], R[0])

        raw_loaded = [sem(f"raw_loaded{s}") for s in range(2)]
        hi_ready, lo_ready = sem("hi_ready"), sem("lo_ready")
        tile_done = sem("tile_done")
        evacuated = sem("evacuated")
        cst_loaded, att_loaded, rw_loaded = sem("cst_loaded"), sem("att_loaded"), sem("rw_loaded")
        x_loaded = [sem(f"x_loaded{g}") for g in range(4)]
        sq_ready, sq_used, ss_done = sem("sq_ready"), sem("sq_used"), sem("ss_done")
        ms_ready, rms_ready = sem("ms_ready"), sem("rms_ready")
        xn_ready, h_hi_ready, h_lo_ready = sem("xn_ready"), sem("h_hi_ready"), sem("h_lo_ready")
        low_ready, shifted = sem("low_ready"), sem("shifted")
        zeroed = sem("zeroed")
        vt_done, vtok_ready = sem("vt_done"), sem("vtok_ready")
        scores_done, stats_ready, exp_done = sem("scores_done"), sem("stats_ready"), sem("exp_done")
        probs_ready, pt_done, pt_read = sem("probs_ready"), sem("pt_done"), sem("pt_read")
        pv_done, pv_read = sem("pv_done"), sem("pv_read")
        yatt_stored = sem("yatt_stored")
        ups_loaded = [sem(f"ups_loaded{s}") for s in range(2)]
        cp_ready, ups_done, up_read = sem("cp_ready"), sem("ups_done"), sem("up_read")
        cum_ready, exps_ready = sem("cum_ready"), sem("exps_ready")
        ksq_ready, kn_done, kn_read, kn_root = (
            sem("ksq_ready"), sem("kn_done"), sem("kn_read"), sem("kn_root"))
        prep_ready, bonus_done, bonus_read = sem("prep_ready"), sem("bonus_done"), sem("bonus_read")
        tok_done, tok_read, g_done, g_read = (
            sem("tok_done"), sem("tok_read"), sem("g_done"), sem("g_read"))
        ln_done, ln_read, lv_done, lv_read = (
            sem("ln_done"), sem("ln_read"), sem("lv_done"), sem("lv_read"))
        x_done, x_read, w1_done, w1_read = (
            sem("x_done"), sem("x_read"), sem("w1_done"), sem("w1_read"))
        p2_done, p2_seen, p2_read = sem("p2_done"), sem("p2_seen"), sem("p2_read")
        m1_done, rhs_ready, m2_done, u_ready = (
            sem("m1_done"), sem("rhs_ready"), sem("m2_done"), sem("u_ready"))
        m3_done, s_ready, sa_ready = sem("m3_done"), sem("s_ready"), sem("sa_ready")
        y_done, y_ready = sem("y_done"), sem("y_ready")
        cen_done, cen_read = sem("cen_done"), sem("cen_read")
        var_done, var_read, var_root = sem("var_done"), sem("var_read"), sem("var_root")
        y_fin, y_stored = sem("y_fin"), sem("y_stored")
        gate_ready, gate_stored = sem("gate_ready"), [sem(f"gate_stored{s}") for s in range(2)]
        ystage_loaded = [sem(f"ystage_loaded{s}") for s in range(2)]
        yb_hi, yb_lo = sem("yb_hi"), sem("yb_lo")
        gin_loaded = [sem(f"gin_loaded{s}") for s in range(2)]
        attn_half, merge_read = sem("attn_half"), sem("merge_read")
        mrg_ready, m_hi_ready, m_lo_ready = sem("mrg_ready"), sem("m_hi_ready"), sem("m_lo_ready")
        xin_loaded = [sem(f"xin_loaded{s}") for s in range(2)]
        bank_read = sem("bank_read")
        x2_ready, x2sq_ready, x2_hi, x2_lo, acc_ready = (
            sem("x2_ready"), sem("x2sq_ready"), sem("x2_hi"), sem("x2_lo"), sem("acc_ready"))
        x2_stored = [sem(f"x2_stored{s}") for s in range(2)]
        ss2_done, ms2_ready, rms2_ready, rstd_ready = (
            sem("ss2_done"), sem("ms2_ready"), sem("rms2_ready"), sem("rstd_ready"))
        resid_loaded = sem("resid_loaded")
        gate_n_ready, silu_ready, hid_ready, g_hi_ready, g_lo_ready = (
            sem("gate_n_ready"), sem("silu_ready"), sem("hid_ready"), sem("g_hi_ready"),
            sem("g_lo_ready"))
        fin_ready, fsq_ready, out_ready, out_stored = (
            sem("fin_ready"), sem("fsq_ready"), sem("out_ready"), sem("out_stored"))

        def by_block(ap):
            return ap.rearrange("p (t n) -> p t n", t=NB)

        def wide(ap, n):
            return ap.unsqueeze(1).to_broadcast([P, n, ap.shape[-1]])

        def tile_of(buf, m):
            return buf[:, m, :] if isinstance(m, int) else buf[:, bass.ds(m, 1), :].rearrange(
                "p a n -> p (a n)")

        class Fill:

            def __init__(self, step):
                self.pos, self.step = 0, step

            def __call__(self, place):
                for _ in range(FILL[place]):
                    self.step(self.pos // KD, self.pos % KD)
                    self.pos += 1

        block = ctx.enter_context(nc.Block())

        @block.sync
        def _(sp):
            def load(ix, src=None, cols=SLOT):
                n, s, _ = ix
                src = w_slots[n] if src is None else src
                if not (isinstance(n, int) and n < 2):
                    sp.wait_ge(lo_ready, n - 1)
                sp.dma_start(raw[s][:, 0:cols], src).then_inc(raw_loaded[s], 16)

            sp.dma_start(cst[:], consts).then_inc(cst_loaded, 16)
            sp.dma_start(norm_g[:], norms).then_inc(cst_loaded, 16)
            for g in range(4):
                if g == 1:
                    load(index(0, 2, 0))
                sp.dma_start(X[:, 4 * g:4 * g + 4, :],
                             xT[4 * g:4 * g + 4].rearrange("k p t -> p k t")).then_inc(x_loaded[g], 16)
            load(index(0, 2, 1))
            sp.dma_start(lowmu[:], low_mu).then_inc(att_loaded, 16)
            sp.dma_start(att_const[:], att_cst).then_inc(att_loaded, 16)
            sp.dma_start(sink[:], sinks).then_inc(att_loaded, 16)
            load(index(0, 2, 2))
            with sp.Fori(0, KV_HEADS // 2) as gp:
                for j in range(ATT_TILES):
                    load(index(gp, ATT_TILES, ATT0 + j))
            for s in range(2):
                load(index(0, 2, RW0 + s))

            sp.wait_ge(pv_read, 2 + 2 * NB * KV_HEADS // 2)
            sp.wait_ge(yatt_stored, 16 * (KV_HEADS // 2 + 1))
            sp.dma_start(scanlq[:], scan_lq).then_inc(rw_loaded, 16)
            sp.dma_start(masks_f32, level_masks).then_inc(rw_loaded, 16)
            sp.dma_start(cp_all[:], pair_cst).then_inc(rw_loaded, 16)
            with sp.Fori(0, PAIRS // 2) as i:
                for u in range(2):
                    p = i * 2 + u
                    sp.wait_ge(ups_done, p + 1)
                    sp.dma_start(ups[u][:], w_ups[p]).then_inc(ups_loaded[u], 16)
                    for j in range(RW_TILES):
                        load(index(i, 2 * RW_TILES, RW0 + 2 + u * RW_TILES + j))

            sp.wait_ge(yatt_stored, 16 * (KV_HEADS // 2 + 1))
            sp.wait_ge(y_fin, PAIRS)
            for h in range(PAIRS):
                if h == PAIRS // 2:
                    sp.wait_ge(y_stored, 16 * (PAIRS + 1))
                if h >= 2:
                    sp.wait_ge(yb_lo, h - 1)
                sp.dma_start(ystage[h % 2][:],
                             y_dram[2 * h:2 * h + 2].rearrange("k p t -> p k t")
                             ).then_inc(ystage_loaded[h % 2], 16)
            for s in range(2):
                sp.wait_ge(gate_stored[s], 16 * (2 * PAIRS + 1))
            for m in range(2):
                sp.dma_start(gin[m][:], gates_dram[2 * m:2 * m + 2].rearrange("k p t -> p k t")
                             ).then_inc(gin_loaded[m], 16)
            with sp.Fori(1, KD // 2) as i:
                for u in range(2):
                    m = i * 2 + u
                    load(index(i, 2, MERGE0 + u))
                    sp.wait_ge(merge_read, m - 1)
                    sp.dma_start(gin[u][:], gates_dram[bass.ds(m * 2, 2)].rearrange("k p t -> p k t")
                                 ).then_inc(gin_loaded[u], 16)

            for s in range(2):
                load(index(0, 2, OUT0 + s))
            sp.wait_ge(m_lo_ready, KD)
            for m in range(2):
                sp.dma_start(xin[m][:], xT[m]).then_inc(xin_loaded[m], 16)
            with sp.Fori(1, KD // 2) as i:
                for u in range(2):
                    m = i * 2 + u
                    load(index(i, 2, OUT0 + u))
                    sp.wait_ge(x2_ready, m - 1)
                    sp.dma_start(xin[u][:], xT[m]).then_inc(xin_loaded[u], 16)

            for s in range(2):
                load(ffn_index(0, 0, s), w_gu[s])
            sp.wait_ge(tile_done, FFN0)
            for s in range(2):
                sp.wait_ge(x2_stored[s], 16 * (KD // 2 + 1))
            for g in range(4):
                sp.dma_start(resid[:, 4 * g:4 * g + 4, :],
                             x2_dram[4 * g:4 * g + 4].rearrange("k p t -> p k t")
                             ).then_inc(resid_loaded, 16)

            def load_down(g):
                with sp.Fori(0, KD // 2) as i:
                    for u in range(2):
                        load(ffn_index(g, i, 2 * FG + u), w_down[g * KD + i * 2 + u], DSLOT)

            with sp.Fori(1, FG) as t:
                for u in range(2):
                    load(ffn_index(0, t, u), w_gu[t * 2 + u])
            load_down(0)
            with sp.Fori(1, GROUPS_F) as g:
                with sp.Fori(0, FG) as t:
                    for u in range(2):
                        load(ffn_index(g, t, u), w_gu[g * (2 * FG) + t * 2 + u])
                load_down(g)

            for g in range(4):
                sp.wait_ge(out_ready, 4 * g + 4)
                sp.dma_start(out[4 * g:4 * g + 4].rearrange("k p t -> p k t"),
                             resid[:, 4 * g:4 * g + 4, :]).then_inc(out_stored, 16)
            sp.wait_ge(out_stored, 64)

        @block.gpsimd
        def _(pool):
            def low_part(ix, cols=SLOT):
                n, s, _ = ix
                pool.wait_ge(hi_ready, n + 1)
                nc.gpsimd.tensor_tensor(wlo[s][:, 0:cols], raw[s][:, 0:cols],
                                        whi[s][:, 0:cols].bitcast(f32), SUB).then_inc(lo_ready, 1)

            low_part(index(0, 2, 0))
            with pool.Fori(0, FFN0 // 2) as i:
                for u in range(2):
                    low_part(index(i, 2, 1 + u))
            with pool.Fori(0, GROUPS_F) as g:
                with pool.Fori(0, FG) as t:
                    for u in range(2):
                        low_part(ffn_index(g, t, u))
                with pool.Fori(0, KD // 2) as i:
                    for u in range(2):
                        low_part(ffn_index(g, i, 2 * FG + u), DSLOT)

        @block.scalar
        def _(act):
            act.sem_inc(evacuated, 2)
            act.sem_inc(pt_read, 1)
            act.sem_inc(pv_read, 2)
            act.sem_inc(cen_read, 1)
            act.sem_inc(yatt_stored, 16)
            act.sem_inc(y_stored, 16)
            for s in range(2):
                act.sem_inc(gate_stored[s], 16)
                act.sem_inc(x2_stored[s], 16)

            def copy(dst, src, scale=1.0):
                return A.activation(dst, src, ACT.Copy, scale=scale)

            def split(ix, cols=SLOT):
                n, s, h = ix
                act.wait_ge(raw_loaded[s], h * 16 + 16)
                if not (isinstance(n, int) and n < 2):
                    act.wait_ge(tile_done, n - 1)
                copy(whi[s][:, 0:cols], raw[s][:, 0:cols]).then_inc(hi_ready, 1)

            split(index(0, 2, 0))
            for k in range(KD):
                if k % 4 == 0:
                    act.wait_ge(x_loaded[k // 4], 16)
                if k >= 2:
                    act.wait_ge(sq_used, k - 1)
                A.activation(sq[k % 2][:], X[:, k, :], ACT.Square).then_inc(sq_ready, 1)
            split(index(0, 2, 1))
            act.wait_ge(ms_ready, 1)
            A.activation(rstd1[:], rstd1[:], ACT.Sqrt).then_inc(rms_ready, 1)
            act.wait_ge(cst_loaded, 32)
            for k in range(KD):
                act.wait_ge(xn_ready, k + 1)
                copy(H_hi[:, k, :], X[:, k, :], norm_g[:, 0, k:k + 1]).then_inc(h_hi_ready, 1)

            def evacuate_proj(n, s, w, which):
                act.wait_ge(tile_done, n + 1)
                if not (isinstance(w, int) and w < 2):
                    act.wait_ge(shifted, w - 1)
                copy(proj[which][:, 1:T_SEQ + 1], dense[s][:]).then_inc(evacuated, 1)

            act.wait_ge(zeroed, 1)
            for n in range(N_LOW):
                evacuate_proj(n, n % 2, n, n % 2)
                split(index(0, 2, n + 2))
            act.wait_ge(shifted, 1)
            A.activation(low[0][0:DECAY_RANK, :], low[0][0:DECAY_RANK, :], ACT.Tanh)
            act.wait_ge(shifted, 3)
            A.activation(low[1][:], low[1][:], ACT.Sigmoid)
            A.activation(low[2][:], low[2][:], ACT.Sigmoid).then_inc(low_ready, 1)

            with act.Fori(0, KV_HEADS // 2) as gp:
                for j in range(ATT_TILES):
                    n, s, _ = index(gp, ATT_TILES, ATT0 + j)
                    act.wait_ge(tile_done, n + 1)
                    if j == 0:
                        copy(kT[:, BLOCK:BLOCK + T_SEQ], dense[s][:]).then_inc(evacuated, 1)
                    elif j == 1:
                        copy(vT[:], dense[s][:]).then_inc(evacuated, 1)
                    else:
                        copy(qT[:, j - 2, :], dense[s][:], HD ** -0.5).then_inc(evacuated, 1)
                    split(index(gp, ATT_TILES, ATT0 + j + 2))
                    if j == 3:
                        act.wait_ge(vt_done, gp + 1)
                        copy(vtok[:, 1:NB + 1, :], by_block(R[0][:])).then_inc(vtok_ready, 1)

                def exps(w):
                    act.wait_ge(stats_ready, gp * (2 * NB) + w + 1)
                    for h in range(GROUP):
                        A.activation(probs[w % 2][:, h, :], probs[w % 2][:, h, :], ACT.Exp,
                                     bias=negmax[w % 2][:, h:h + 1],
                                     accum_out=rowsum[w % 2][:, h:h + 1])
                    A.activation(sinkexp[w % 2][:], sinkexp[w % 2][:], ACT.Exp).then_inc(exp_done, 1)

                def read_out(w):
                    e, b = w // NB, w % NB
                    W = gp * (2 * NB) + w
                    act.wait_ge(pt_done, W + 3)
                    act.wait_ge(pv_done, W + 1)
                    copy(pT[:, 0, :], R[5][:])
                    copy(pT[:, 1, :], R[0][:]).then_inc(pt_read, 1)
                    if w == 0:
                        act.wait_ge(yatt_stored, gp * 16 + 16)
                    act.wait_ge(pv_done, W + 2)
                    copy(yatt[e * HD:e * HD + HD, :, b * BLOCK:(b + 1) * BLOCK],
                         R[1 + 2 * (w % 2)][e * HD:e * HD + HD, :].rearrange(
                             "p (h t) -> p h t", h=GROUP)).then_inc(pv_read, 1)

                exps(0)
                for w in range(2 * NB):
                    if w + 1 < 2 * NB:
                        exps(w + 1)
                    read_out(w)
                act.wait_ge(pv_read, gp * (2 * NB) + 2 * NB + 2)
                act.dma_start(y_dram[bass.ds(gp * GROUP, GROUP)].rearrange("k p t -> p k t"),
                              yatt[:]).then_inc(yatt_stored, 16)

            act.wait_ge(rw_loaded, 48)
            with act.Fori(0, PAIRS // 2) as i:
                for u in range(2):
                    p = i * 2 + u
                    c = cp[u]

                    def front_tile(j):
                        n, s, _ = index(i, 2 * RW_TILES, RW0 + u * RW_TILES + j)
                        w = N_LOW + 3 * u + j
                        evacuate_proj(n, s, i * 6 + w, w % 2)
                        split(index(i, 2 * RW_TILES, RW0 + u * RW_TILES + j + 2))

                    def gate_step(tile, k):
                        if k < KD - 1:
                            return
                        n, s, _ = index(i, 2 * RW_TILES, RW0 + u * RW_TILES + 3 + tile)
                        act.wait_ge(tile_done, n + 1)
                        act.wait_ge(gate_stored[tile % 2], (p * 2 + tile // 2) * 16 + 16)
                        A.activation(gout[tile % 2][:], dense[s][:], ACT.Sigmoid).then_inc(evacuated, 1)
                        split(index(i, 2 * RW_TILES, RW0 + u * RW_TILES + 3 + tile + 2))
                        act.wait_ge(evacuated, n + 3)
                        act.dma_start(gates_dram[p * 4 + tile], gout[tile % 2][:]
                                      ).then_inc(gate_stored[tile % 2], 16)

                    fill = Fill(gate_step)
                    front_tile(0)
                    act.wait_ge(cp_ready, p + 1)
                    act.wait_ge(ups_done, p + 3)
                    A.activation(grow[:], R[0][:], ACT.Sigmoid, bias=c[:, C_DB:C_DB + 1]
                                 ).then_inc(up_read, 1)
                    A.activation(icl[:], R[1][:], ACT.Sigmoid, bias=c[:, C_IB:C_IB + 1]
                                 ).then_inc(up_read, 1)
                    copy(gbuf[:], R[2][:]).then_inc(up_read, 1)
                    act.wait_ge(cum_ready, p + 1)
                    A.activation(a_in[:], csum[:], ACT.Exp, scale=-LAMBDA)
                    A.activation(zq[:, :, 0, :], zq[:, :, 0, :], ACT.Exp, scale=-LAMBDA)
                    A.activation(grow[:], csum[:], ACT.Exp, scale=LAMBDA).then_inc(exps_ready, 1)
                    front_tile(1)
                    act.wait_ge(kn_read, p + 1)
                    A.activation(tmp1[:], tmp1[:], ACT.Sqrt).then_inc(kn_root, 1)
                    front_tile(2)
                    fill("prep")
                    for bank, dst, count in ((R[1], btok, 1), (R[2], ktok, 2), (R[0], vtk, 3)):
                        act.wait_ge(tok_done, p * 3 + count)
                        copy(dst[:], by_block(bank[:])).then_inc(tok_read, 1)
                    for e in range(2):
                        act.wait_ge(ln_done, p * 2 + e + 1)
                        copy(Ln[:, e], by_block(R[1 + e][:])).then_inc(ln_read, 1)
                    fill("solve")
                    act.wait_ge(lv_done, p + 1)
                    copy(lv[:], by_block(R[1][:])).then_inc(lv_read, 1)
                    for level in range(LEVELS):
                        for e in range(2):
                            act.wait_ge(x_done, p * (2 * LEVELS) + 2 * level + e + 1)
                            copy(Xi[:, e], by_block(RA[e][:])).then_inc(x_read, 1)
                            act.wait_ge(w1_done, p * (2 * LEVELS) + 2 * level + e + 1)
                            copy(W1[:, e], by_block(RB[e][:])).then_inc(w1_read, 1)
                        fill("level_a")
                        fill("level_b")
                    for n in range(CHUNKS):
                        t, lo = n // 2, CHUNK * (n % 2)
                        if n + 1 < CHUNKS:
                            end = n * CHUNK + CHUNK - 1
                            act.wait_ge(s_ready, p * CHUNKS + n + 1)
                            copy(SA[:], S[:], a_in[:, end:end + 1]).then_inc(sa_ready, 1)
                        fill("rhs")
                        act.wait_ge(m2_done, p * CHUNKS + n + 1)
                        copy(utok[lo:lo + CHUNK, t, :], R[3][lo:lo + CHUNK, 0:P]).then_inc(u_ready, 1)
                        fill("u")
                        fill("state")
                    act.wait_ge(y_done, p + 1)
                    copy(csum[:], R[5][:]).then_inc(y_ready, 1)
                    fill("y")
                    act.wait_ge(cen_done, p + 1)
                    copy(kkbuf[:], R[0][:])
                    A.activation(tmp1[:], R[0][:], ACT.Square).then_inc(cen_read, 1)
                    fill("center")
                    act.wait_ge(var_read, p + 2)
                    A.activation(tmp2[:], tmp2[:], ACT.Sqrt).then_inc(var_root, 1)
                    act.wait_ge(y_fin, p + 1)
                    act.dma_start(y_dram[p + PAIRS], bonus[:]).then_inc(y_stored, 16)

            for h in range(PAIRS):
                act.wait_ge(ystage_loaded[h % 2], 16 * (h // 2 + 1))
                copy(H_hi[:, 2 * h:2 * h + 2, :], ystage[h % 2][:]).then_inc(yb_hi, 1)

            with act.Fori(0, KD // 2) as i:
                for u in range(2):
                    m = i * 2 + u
                    split(index(i, 2, MERGE0 + u + 2))
                    act.wait_ge(mrg_ready, m + 1)
                    copy(tile_of(M_hi, m), mrg[u][:]).then_inc(m_hi_ready, 1)

            with act.Fori(0, KD // 2) as i:
                for u in range(2):
                    m = i * 2 + u
                    split(index(i, 2, OUT0 + u + 2))
                    act.wait_ge(x2_ready, m + 1)
                    act.dma_start(x2_dram[m], x2[u][:]).then_inc(x2_stored[u], 16)
                    act.wait_ge(acc_ready, m + 1)
                    A.activation(sqx[:], x2[u][:], ACT.Square).then_inc(x2sq_ready, 1)
                    copy(tile_of(H_hi, m), x2[u][:], norm_g[:, 1, bass.ds(m, 1)]).then_inc(x2_hi, 1)
            act.wait_ge(ms2_ready, 1)
            A.activation(rstd[:], rstd[:], ACT.Sqrt).then_inc(rms2_ready, 1)

            def hidden(g, t, cols):
                for u in range(2):
                    if u == 1:
                        hn = g * FG + t
                        act.wait_ge(gate_n_ready, hn + 1)
                        A.activation(gate_s[:], gate_n[:], ACT.Silu).then_inc(silu_ready, 1)
                    split(ffn_index(g, t, u + 2), cols)
                    if u == 1:
                        act.wait_ge(hid_ready, hn + 1)
                        copy(tile_of(G_hi, t), hid[:]).then_inc(g_hi_ready, 1)

            def last_square(m):
                act.wait_ge(fin_ready, m + 1)
                act.wait_ge(acc_ready, m + KD + 1)
                A.activation(fsq[:], tile_of(resid, m), ACT.Square).then_inc(fsq_ready, 1)

            def hidden_tiles(g):
                with act.Fori(0, FG - 1) as t:
                    hidden(g, t, SLOT)
                hidden(g, FG - 1, DSLOT)

            with act.Fori(0, GROUPS_F - 1) as g:
                hidden_tiles(g)
                with act.Fori(0, KD // 2 - 1) as i:
                    for u in range(2):
                        split(ffn_index(g, i, 2 * FG + u + 2), DSLOT)
                for u in range(2):
                    split(ffn_index(g, 0, FGRP + u))
            hidden_tiles(GROUPS_F - 1)
            with act.Fori(0, KD // 2 - 1) as i:
                for u in range(2):
                    split(ffn_index(GROUPS_F - 1, i, 2 * FG + u + 2), DSLOT)
                    last_square(i * 2 + u)
            for m in (KD - 2, KD - 1):
                last_square(m)
            act.wait_ge(ms2_ready, 2)
            A.activation(rstd[:], rstd[:], ACT.Sqrt).then_inc(rms2_ready, 1)

        @block.vector
        def _(dve):
            dve.sem_inc(var_read, 1)
            dve.sem_inc(bank_read, 2)
            dve.sem_inc(acc_ready, 1)

            def fence():
                V.drain()

            for i in range(2):
                V.memset(proj[i][:, 0:1], 0.0)
            V.drain().then_inc(zeroed, 1)

            dve.wait_ge(ss_done, 1)
            V.tensor_scalar(rstd1[:], R[0][:], 1.0 / D_MODEL, NORM_EPS, MUL, ADD).then_inc(ms_ready, 1)
            dve.wait_ge(rms_ready, 1)
            V.reciprocal(rstd1[:], rstd1[:])
            fence()
            dve.wait_ge(cst_loaded, 32)
            for k in range(KD + 1):
                if k < KD:
                    V.tensor_tensor(X[:, k, :], X[:, k, :], rstd1[:], MUL).then_inc(xn_ready, 1)
                if k >= 1:
                    dve.wait_ge(h_hi_ready, k)
                    V.scalar_tensor_tensor(H_lo[:, k - 1, :], X[:, k - 1, :], norm_g[:, 0, k - 1:k],
                                           H_hi[:, k - 1, :].bitcast(f32), MUL, SUB
                                           ).then_inc(h_lo_ready, 1)

            def shift(dst, which, mu, n):
                dve.wait_ge(evacuated, n + 3)
                cur, prev = proj[which][:, 1:T_SEQ + 1], proj[which][:, 0:T_SEQ]
                V.tensor_tensor(tmp1[:], prev, cur, SUB)
                fence()
                V.scalar_tensor_tensor(dst, tmp1[:], mu, cur, MUL, ADD).then_inc(shifted, 1)

            dve.wait_ge(att_loaded, 48)
            for n in range(N_LOW):
                shift(low[n][:], n % 2, lowmu[:, n:n + 1], n)
                fence()

            V.memset(kT[:, 0:BLOCK], 0.0)
            V.memset(vtok[:, 0, :], 0.0)
            V.drain().then_inc(zeroed, 1)
            with dve.Fori(0, KV_HEADS // 2) as gp:
                V.tensor_copy(slope_g[:], slopes[:, bass.ds(gp * (2 * GROUP), 2 * GROUP)])
                V.tensor_copy(sink_g[:], sink[:, bass.ds(gp * (2 * GROUP), 2 * GROUP)])
                fence()

                def stats(w):
                    e, b = w // NB, w % NB
                    W = gp * (2 * NB) + w
                    s = w % 2
                    dve.wait_ge(scores_done, W + 1)
                    dve.wait_ge(pt_done, W + 1)
                    for h in range(GROUP):
                        V.scalar_tensor_tensor(
                            probs[s][:, h, :], dist[:, min(b, 1), :],
                            slope_g[:, e * GROUP + h:e * GROUP + h + 1],
                            R[1 + 2 * s + h // 2][:, (h % 2) * 2 * BLOCK:(h % 2 + 1) * 2 * BLOCK],
                            MUL, ADD)
                    fence()
                    V.tensor_reduce(rowmax[s][:], probs[s][:], AX, ALU.max)
                    fence()
                    g = sink_g[:, e * GROUP:(e + 1) * GROUP]
                    V.tensor_tensor(rowmax[s][:], rowmax[s][:], g, ALU.max)
                    fence()
                    V.tensor_scalar(negmax[s][:], rowmax[s][:], -1.0, None, MUL)
                    V.tensor_tensor(sinkexp[s][:], g, rowmax[s][:], SUB).then_inc(stats_ready, 1)

                def normalise(w):
                    s = w % 2
                    dve.wait_ge(exp_done, gp * (2 * NB) + w + 1)
                    V.tensor_tensor(rowsum[s][:], rowsum[s][:], sinkexp[s][:], ADD)
                    fence()
                    V.reciprocal(rowinv[s][:], rowsum[s][:])
                    fence()
                    for h in range(GROUP):
                        last = V.tensor_scalar(probs[s][:, h, :], probs[s][:, h, :],
                                               rowinv[s][:, h:h + 1], None, MUL)
                    last.then_inc(probs_ready, 1)

                stats(0)
                for w in range(2 * NB):
                    if w + 1 < 2 * NB:
                        stats(w + 1)
                    normalise(w)

            dve.wait_ge(rw_loaded, 48)
            V.tensor_copy(masks[:].rearrange("p l n -> p (l n)"), masks_f32)
            V.memset(rhs[:], 0.0)
            V.memset(utok[:], 0.0)
            fence()
            with dve.Fori(0, PAIRS // 2) as i:
                for u in range(2):
                    p = i * 2 + u
                    n0 = i * (2 * RW_TILES) + RW0 + u * RW_TILES
                    c = cp[u]
                    col = lambda k: c[:, k:k + 1]
                    which = (N_LOW + 3 * u) % 2
                    zn, q = zq[:, :, 0, :], zq[:, :, 1, :]

                    V.tensor_copy(c[:], tile_of(cp_all, p))
                    V.drain().then_inc(cp_ready, 1)
                    shift(kbuf[:], which, col(C_MUK), n0)
                    fence()
                    V.tensor_scalar(kkbuf[:], kbuf[:], col(C_KK), None, MUL)
                    fence()
                    V.tensor_tensor(tmp1[:], kkbuf[:], kkbuf[:], MUL).then_inc(ksq_ready, 1)
                    dve.wait_ge(up_read, p * 3 + 3)
                    V.tensor_tensor_scan(csum[:], scan_mask, grow[:], 0.0, MUL, ADD)
                    fence()
                    V.tensor_tensor(zn, by_block(csum[:]), by_block(grow[:]), SUB).then_inc(cum_ready, 1)
                    V.tensor_scalar(tmp2[:], icl[:], 1.0, col(C_KA), SUB, MUL)
                    fence()
                    V.scalar_tensor_tensor(kbuf[:], tmp2[:], 1.0, kbuf[:], ADD, MUL)
                    dve.wait_ge(kn_done, p + 1)
                    V.tensor_scalar(tmp1[:], R[3][:], 1e-24, None, ALU.max).then_inc(kn_read, 1)
                    dve.wait_ge(kn_root, p + 1)
                    V.reciprocal(tmp2[:], tmp1[:])
                    fence()
                    V.scalar_tensor_tensor(kkbuf[:], kkbuf[:], -1.0, tmp2[:], MUL, MUL)
                    fence()
                    dve.wait_ge(exps_ready, p + 1)
                    V.tensor_tensor(zn, zn, by_block(kkbuf[:]), MUL)
                    V.scalar_tensor_tensor(tmp1[:], icl[:], -1.0, kkbuf[:], MUL, MUL)
                    V.tensor_tensor(kap[:], kbuf[:], grow[:], MUL)
                    fence()
                    V.tensor_tensor(icl[:], tmp1[:], grow[:], MUL)
                    fence()
                    shift(rbuf[:], 1 - which, col(C_MUR), n0 + 1)
                    fence()
                    V.tensor_tensor(q, by_block(rbuf[:]), by_block(a_in[:]), MUL)
                    V.scalar_tensor_tensor(tmp2[:], rbuf[:], col(C_RK), kbuf[:], MUL, MUL
                                           ).then_inc(prep_ready, 1)
                    V.tensor_copy(Y[:].rearrange("p e t n -> p (e t) n"), wide(ident, 2 * NB))
                    fence()
                    shift(vbuf[:], which, col(C_MUV), n0 + 2)
                    fence()
                    dve.wait_ge(bonus_done, p + 1)
                    dve.wait_ge(y_stored, p * 16 + 16)
                    V.tensor_tensor(bonus[:], vbuf[:], R[3][:], MUL).then_inc(bonus_read, 1)
                    for t in range(NB):
                        for e in range(2):
                            bank = ((R[3], R[4]), (R[5], R[0]))[e][t % 2]
                            dve.wait_ge(g_done, p * (2 * NB) + 2 * t + e + 1)
                            V.tensor_tensor(lq[:, e, t].rearrange("p a b -> p (a b)"),
                                            bank[:, P:4 * P], lq_mask, MUL)
                            V.copy_predicated(Y[:, e, t, :], masks[:, 0, :], bank[:, 0:P]
                                              ).then_inc(g_read, 1)
                    for level in range(LEVELS):
                        for e in range(2):
                            dve.wait_ge(p2_done, p * (2 * LEVELS) + 2 * level + e + 1)
                            dve.sem_inc(p2_seen, 1)
                            V.copy_predicated(Y[:, e], wide(masks[:, level + 1, :], NB),
                                              by_block(RA[e][:])).then_inc(p2_read, 1)
                    V.memset(S[:], 0.0).then_inc(s_ready, 1)
                    for n in range(CHUNKS):
                        t, lo = n // 2, CHUNK * (n % 2)
                        dve.wait_ge(m1_done, p * CHUNKS + n + 1)
                        if n == 0:
                            dve.wait_ge(lv_read, p + 1)
                        V.tensor_tensor(rhs[lo:lo + CHUNK, t, :], lv[lo:lo + CHUNK, t, :],
                                        R[2][lo:lo + CHUNK, 0:P], ADD).then_inc(rhs_ready, 1)
                        if n + 1 < CHUNKS:
                            end = n * CHUNK + CHUNK - 1
                            dve.wait_ge(m3_done, p * (CHUNKS - 1) + n + 1)
                            dve.wait_ge(sa_ready, p * (CHUNKS - 1) + n + 1)
                            for e in range(2):
                                d = slice(e * HD, e * HD + HD)
                                last = V.scalar_tensor_tensor(S[d, d], R[4][d, d], a_in[d, end:end + 1],
                                                              SA[d, d], MUL, ADD)
                            last.then_inc(s_ready, 1)
                    dve.wait_ge(var_done, p + 1)
                    V.tensor_scalar(tmp2[:], R[1][:], LNX_EPS, None, ADD).then_inc(var_read, 1)
                    dve.wait_ge(var_root, p + 1)
                    V.reciprocal(tmp1[:], tmp2[:])
                    fence()
                    V.tensor_tensor(kkbuf[:], kkbuf[:], tmp1[:], MUL)
                    fence()
                    V.tensor_scalar(kkbuf[:], kkbuf[:], col(C_LW), col(C_LB), MUL, ADD)
                    fence()
                    V.tensor_tensor(kkbuf[:], kkbuf[:], bonus[:], ADD)
                    fence()
                    V.tensor_tensor(bonus[:], kkbuf[:], gbuf[:], MUL).then_inc(y_fin, 1)

            for h in range(PAIRS):
                dve.wait_ge(yb_hi, h + 1)
                V.tensor_tensor(H_lo[:, 2 * h:2 * h + 2, :], ystage[h % 2][:],
                                H_hi[:, 2 * h:2 * h + 2, :].bitcast(f32), SUB).then_inc(yb_lo, 1)

            with dve.Fori(0, KD // 2) as i:
                for u in range(2):
                    m = i * 2 + u
                    a_bank, b_bank = (dense[1], dense[0]) if u == 0 else (R[0], R[1])
                    dve.wait_ge(gin_loaded[u], i * 16 + 16)
                    dve.wait_ge(attn_half, m + 1)
                    V.tensor_tensor(mtmp[:], gin[u][:, 0, :], a_bank[:], MUL)
                    dve.wait_ge(tile_done, m + MERGE0 + 1)
                    V.tensor_tensor(mrg[u][:], gin[u][:, 1, :], b_bank[:], MUL).then_inc(merge_read, 1)
                    fence()
                    V.tensor_tensor(mrg[u][:], mrg[u][:], mtmp[:], ADD).then_inc(mrg_ready, 1)
                    dve.wait_ge(m_hi_ready, m + 1)
                    V.tensor_tensor(tile_of(M_lo, m), mrg[u][:], tile_of(M_hi, m).bitcast(f32), SUB
                                    ).then_inc(m_lo_ready, 1)

            V.memset(sqacc[:], 0.0)
            with dve.Fori(0, KD // 2) as i:
                for u in range(2):
                    m = i * 2 + u
                    bank = dense[(OUT0 + u) % 2]
                    dve.wait_ge(xin_loaded[u], i * 16 + 16)
                    dve.wait_ge(x2_stored[u], i * 16 + 16)
                    dve.wait_ge(tile_done, m + OUT0 + 1)
                    V.tensor_tensor(x2[u][:], xin[u][:], bank[:], ADD).then_inc(bank_read, 1)
                    V.drain().then_inc(x2_ready, 1)
                    dve.wait_ge(x2sq_ready, m + 1)
                    V.tensor_tensor(sqacc[:], sqacc[:], sqx[:], ADD).then_inc(acc_ready, 1)
                    dve.wait_ge(x2_hi, m + 1)
                    V.scalar_tensor_tensor(tile_of(H_lo, m), x2[u][:], norm_g[:, 1, bass.ds(m, 1)],
                                           tile_of(H_hi, m).bitcast(f32), MUL, SUB
                                           ).then_inc(x2_lo, 1)
            dve.wait_ge(ss2_done, 1)
            V.tensor_scalar(rstd[:], R[2][:], 1.0 / D_MODEL, NORM_EPS, MUL, ADD).then_inc(ms2_ready, 1)
            dve.wait_ge(rms2_ready, 1)
            V.reciprocal(rstd[:], rstd[:])
            fence()

            def hidden_tiles(g):
                with dve.Fori(0, FG) as t:
                    n, s, _ = ffn_index(g, t, 0)
                    hn = g * FG + t
                    dve.wait_ge(tile_done, n + 1)
                    V.tensor_tensor(gate_n[:], rstd[:], dense[s][:], MUL).then_inc(bank_read, 1)
                    V.drain().then_inc(gate_n_ready, 1)
                    dve.wait_ge(tile_done, n + 2)
                    V.tensor_tensor(hid[:], rstd[:], dense[1 - s][:], MUL).then_inc(bank_read, 1)
                    fence()
                    dve.wait_ge(silu_ready, hn + 1)
                    V.tensor_tensor(hid[:], hid[:], gate_s[:], MUL).then_inc(hid_ready, 1)
                    dve.wait_ge(g_hi_ready, hn + 1)
                    V.tensor_tensor(tile_of(G_lo, t), hid[:], tile_of(G_hi, t).bitcast(f32), SUB
                                    ).then_inc(g_lo_ready, 1)

            def down_tile(g, i, u):
                n, s, _ = ffn_index(g, i, 2 * FG + u)
                m = i * 2 + u
                dve.wait_ge(tile_done, n + 1)
                V.tensor_tensor(tile_of(resid, m), tile_of(resid, m), dense[s][:], ADD
                                ).then_inc(bank_read, 1)

            with dve.Fori(0, GROUPS_F - 1) as g:
                hidden_tiles(g)
                dve.wait_ge(resid_loaded, 64)
                with dve.Fori(0, KD // 2) as i:
                    for u in range(2):
                        down_tile(g, i, u)
            hidden_tiles(GROUPS_F - 1)
            V.memset(facc[:], 0.0)
            fence()
            with dve.Fori(0, KD // 2) as i:
                for u in range(2):
                    m = i * 2 + u
                    down_tile(GROUPS_F - 1, i, u)
                    V.drain().then_inc(fin_ready, 1)
                    dve.wait_ge(fsq_ready, m + 1)
                    V.tensor_tensor(facc[:], facc[:], fsq[:], ADD).then_inc(acc_ready, 1)
            dve.wait_ge(ss2_done, 2)
            V.tensor_scalar(rstd[:], R[2][:], 1.0 / D_MODEL, NORM_EPS, MUL, ADD).then_inc(ms2_ready, 1)
            dve.wait_ge(rms2_ready, 2)
            V.reciprocal(rstd[:], rstd[:])
            fence()
            for m in range(KD):
                V.scalar_tensor_tensor(resid[:, m, :], resid[:, m, :], norm_g[:, 2, m:m + 1], rstd[:],
                                       MUL, MUL).then_inc(out_ready, 1)

        @block.tensor
        def _(pe):
            pe.sem_inc(pt_done, 2)
            pe.sem_inc(pv_done, 1)
            pe.sem_inc(ups_done, 2)

            def steps(s, bank, ks, first, last, hi=H_hi, lo=H_lo, w0=0):
                for k in ks:
                    wk = slice((k - w0) * P, (k - w0 + 1) * P)
                    PE.matmul(bank[:], whi[s][:, wk], hi[:, k, :], start=(k == first), stop=False)
                    PE.matmul(bank[:], whi[s][:, wk], lo[:, k, :], start=False, stop=False)
                    done = PE.matmul(bank[:], wlo[s][:, wk], hi[:, k, :], start=False, stop=(k == last))
                return done

            def front_tile(ix):
                n, s, _ = ix
                pe.wait_ge(lo_ready, n + 1)
                pe.wait_ge(evacuated, n + 1)
                steps(s, dense[s], range(KD), 0, KD - 1).then_inc(tile_done, 1)

            pe.wait_ge(cst_loaded, 32)
            for k in range(KD):
                pe.wait_ge(sq_ready, k + 1)
                PE.matmul(R[0][:], ones, sq[k % 2][:], start=(k == 0), stop=(k == KD - 1)
                          ).then_inc(sq_used, 1)
            PE.drain().then_inc(ss_done, 1)

            pe.wait_ge(lo_ready, 1)
            for k in range(KD):
                pe.wait_ge(h_lo_ready, k + 1)
                done = steps(0, dense[0], [k], 0, KD - 1)
            done.then_inc(tile_done, 1)
            for n in range(1, N_LOW):
                front_tile(index(0, 2, n))

            pe.wait_ge(zeroed, 2)
            with pe.Fori(0, KV_HEADS // 2) as gp:
                for j in range(ATT_TILES):
                    front_tile(index(gp, ATT_TILES, ATT0 + j))
                    if j == 3:
                        pe.wait_ge(pt_read, gp * (2 * NB) + 1)
                        for t in range(NB):
                            done = PE.transpose(R[0][:, t * P:(t + 1) * P], vT[:, t * P:(t + 1) * P],
                                                ident)
                        done.then_inc(vt_done, 1)
                pe.wait_ge(evacuated, gp * ATT_TILES + ATT0 + ATT_TILES + 2)

                def scores(w):
                    e, b = w // NB, w % NB
                    pe.wait_ge(pv_read, gp * (2 * NB) + w + 1)
                    rows = slice(e * HD, e * HD + HD)
                    for h in range(GROUP):
                        done = PE.matmul(
                            R[1 + 2 * (w % 2) + h // 2][:, (h % 2) * 2 * BLOCK:(h % 2 + 1) * 2 * BLOCK],
                            qT[rows, h, b * BLOCK:(b + 1) * BLOCK],
                            kT[rows, b * BLOCK:(b + 2) * BLOCK], start=True, stop=True)
                    done.then_inc(scores_done, 1)

                def outputs(w):
                    e, b = w // NB, w % NB
                    W = gp * (2 * NB) + w
                    pe.wait_ge(probs_ready, W + 1)
                    pe.wait_ge(pt_read, W + 1)
                    for half, bank in enumerate((R[5], R[0])):
                        for h in range(GROUP):
                            done = PE.transpose(bank[:, h * BLOCK:(h + 1) * BLOCK],
                                                probs[w % 2][:, h, half * BLOCK:(half + 1) * BLOCK],
                                                ident)
                    done.then_inc(pt_done, 1)
                    pe.wait_ge(pt_read, W + 2)
                    cols = slice(e * HD, e * HD + HD)
                    for half in range(2):
                        done = PE.matmul(R[1 + 2 * (w % 2)][cols, :], vtok[:, b + half, cols],
                                         pT[:, half, :], start=(half == 0), stop=(half == 1))
                    done.then_inc(pv_done, 1)

                scores(0)
                pe.wait_ge(vtok_ready, gp + 1)
                for w in range(2 * NB):
                    if w + 1 < 2 * NB:
                        scores(w + 1)
                    outputs(w)

            pe.wait_ge(low_ready, 1)
            pe.wait_ge(pv_read, 2 + NB * KV_HEADS)
            with pe.Fori(0, PAIRS // 2) as i:
                for u in range(2):
                    p = i * 2 + u
                    heads = [slice(e * HD, e * HD + HD) for e in range(2)]

                    def tile_ix(j):
                        return index(i, 2 * RW_TILES, RW0 + u * RW_TILES + j)

                    def gate_step(tile, k):
                        n, s, _ = tile_ix(3 + tile)
                        if k == 0:
                            pe.wait_ge(lo_ready, n + 1)
                            pe.wait_ge(evacuated, n + 1)
                        done = steps(s, dense[s], [k], 0, KD - 1)
                        if k == KD - 1:
                            done.then_inc(tile_done, 1)

                    fill = Fill(gate_step)
                    front_tile(tile_ix(0))
                    pe.wait_ge(ups_loaded[u], i * 16 + 16)
                    pe.wait_ge(cen_read, p + 1)
                    pe.wait_ge(var_read, p + 1)
                    up = ups[u]
                    PE.matmul(R[0][:], up[0:64, 0, :], low[0][0:64, :], start=True, stop=True)
                    PE.matmul(R[1][:], up[64:128, 0, :], low[0][64:128, :], start=True, stop=True)
                    PE.matmul(R[2][:], up[:, 1, :], low[1][:], start=True, stop=False)
                    rest = GATE_RANK - P
                    PE.matmul(R[2][:], up[0:rest, 2, :], low[2][0:rest, :], start=False, stop=True
                              ).then_inc(ups_done, 1)
                    front_tile(tile_ix(1))
                    pe.wait_ge(ksq_ready, p + 1)
                    PE.matmul(R[3][:], head_ones, tmp1[:], start=True, stop=True).then_inc(kn_done, 1)
                    front_tile(tile_ix(2))
                    fill("prep")
                    pe.wait_ge(prep_ready, p + 1)
                    PE.matmul(R[3][:], head_ones, tmp2[:], start=True, stop=True).then_inc(bonus_done, 1)
                    for bank, src in ((R[1], icl), (R[2], kap), (R[0], vbuf)):
                        if src is vbuf:
                            pe.wait_ge(shifted, p * 3 + N_LOW + 3)
                        for t in range(NB):
                            done = PE.transpose(bank[:, t * P:(t + 1) * P], src[:, t * P:(t + 1) * P],
                                                ident)
                        done.then_inc(tok_done, 1)
                    pe.wait_ge(bonus_read, p + 1)
                    pe.wait_ge(tok_read, p * 3 + 3)
                    for t in range(NB):
                        for e in range(2):
                            w = 2 * t + e
                            bank = ((R[3], R[4]), (R[5], R[0]))[e][t % 2]
                            if w >= 4:
                                pe.wait_ge(g_read, p * (2 * NB) + w - 3)
                            tok = slice(t * P, (t + 1) * P)
                            both = zq[heads[e], t].rearrange("p a n -> p (a n)")
                            PE.matmul(bank[:, 0:2 * P], icl[heads[e], tok], both, start=True, stop=True)
                            PE.matmul(bank[:, 2 * P:4 * P], kap[heads[e], tok], both,
                                      start=True, stop=True).then_inc(g_done, 1)
                    for e in range(2):
                        for t in range(NB):
                            tok = slice(t * P, (t + 1) * P)
                            done = PE.matmul(R[1 + e][:, tok], zq[heads[e], t, 0, :], icl[heads[e], tok],
                                             start=True, stop=True)
                        done.then_inc(ln_done, 1)
                    fill("solve")
                    pe.wait_ge(g_read, (p + 1) * (2 * NB))
                    pe.wait_ge(ln_read, p * 2 + 2)
                    for t in range(NB):
                        for e in range(2):
                            done = PE.matmul(R[1][:, t * P + e * HD:t * P + e * HD + HD],
                                             lq[:, e, t, 1, :], vtk[:, t, heads[e]],
                                             start=True, stop=True)
                    done.then_inc(lv_done, 1)
                    for level in range(LEVELS):
                        done_l = p * (2 * LEVELS) + 2 * level
                        for e in range(2):
                            if level:
                                pe.wait_ge(p2_read, done_l - 2 + e + 1)
                            for t in range(NB):
                                done = PE.transpose(RA[e][:, t * P:(t + 1) * P], Y[:, e, t, :], ident)
                            done.then_inc(x_done, 1)
                            for t in range(NB):
                                done = PE.matmul(RB[e][:, t * P:(t + 1) * P], Ln[:, e, t, :],
                                                 Y[:, e, t, :], start=True, stop=True)
                            done.then_inc(w1_done, 1)
                        fill("level_a")
                        for e in range(2):
                            pe.wait_ge(x_read, done_l + e + 1)
                            pe.wait_ge(w1_read, done_l + e + 1)
                            for t in range(NB):
                                done = PE.matmul(RA[e][:, t * P:(t + 1) * P], Xi[:, e, t, :],
                                                 W1[:, e, t, :], start=True, stop=True)
                            done.then_inc(p2_done, 1)
                        fill("level_b")
                    pe.wait_ge(p2_read, (p + 1) * (2 * LEVELS))
                    for n in range(CHUNKS):
                        t, lo = n // 2, CHUNK * (n % 2)
                        here = slice(lo, lo + CHUNK)
                        pe.wait_ge(s_ready, p * CHUNKS + n + 1)
                        PE.matmul(R[2][:, 0:P], zq[:, t, 0, :], S[:], start=True, stop=True
                                  ).then_inc(m1_done, 1)
                        PE.matmul(R[5][:, t * P + lo:t * P + lo + CHUNK], S[:], zq[:, t, 1, here],
                                  start=(n % 2 == 0), stop=False, skip_group_check=True)
                        fill("rhs")
                        pe.wait_ge(rhs_ready, p * CHUNKS + n + 1)
                        for e in range(2):
                            done = PE.matmul(R[3][:, heads[e]], Y[:, e, t, :], rhs[:, t, heads[e]],
                                             start=True, stop=True)
                        done.then_inc(m2_done, 1)
                        fill("u")
                        pe.wait_ge(u_ready, p * CHUNKS + n + 1)
                        if n + 1 < CHUNKS:
                            PE.matmul(R[4][:, 0:P], btok[here, t, :], utok[here, t, :],
                                      start=True, stop=False)
                            PE.matmul(R[4][:, 0:P], ktok[here, t, :], vtk[here, t, :],
                                      start=False, stop=True).then_inc(m3_done, 1)
                        if n % 2:
                            for e in range(2):
                                dst = R[5][heads[e], t * P:(t + 1) * P]
                                PE.matmul(dst, utok[:, t, heads[e]], lq[:, e, t, 0, :],
                                          start=False, stop=False, skip_group_check=True)
                                done = PE.matmul(dst, vtk[:, t, heads[e]], lq[:, e, t, 2, :],
                                                 start=False, stop=True, skip_group_check=True)
                            if n + 1 == CHUNKS:
                                done.then_inc(y_done, 1)
                        fill("state")
                    fill("y")
                    pe.wait_ge(y_ready, p + 1)
                    PE.matmul(R[0][:], head_center, csum[:], start=True, stop=True).then_inc(cen_done, 1)
                    fill("center")
                    pe.wait_ge(cen_read, p + 2)
                    PE.matmul(R[1][:], head_mean, tmp1[:], start=True, stop=True).then_inc(var_done, 1)

            pe.wait_ge(evacuated, MERGE0 + 2)
            pe.wait_ge(cen_read, PAIRS + 1)
            pe.wait_ge(var_read, PAIRS + 1)

            def merge_tile(i, u, first):
                n, s, _ = index(i, 2, MERGE0 + u)
                a_bank, b_bank = (dense[1], dense[0]) if u == 0 else (R[0], R[1])
                pe.wait_ge(lo_ready, n + 1)
                if not first:
                    pe.wait_ge(merge_read, n - MERGE0 - 1)
                for half, bank, flag in ((0, a_bank, attn_half), (1, b_bank, tile_done)):
                    ks = range(half * PAIRS, (half + 1) * PAIRS)
                    for k in ks:
                        if first and k % 2 == 0:
                            pe.wait_ge(yb_lo, k // 2 + 1)
                        done = steps(s, bank, [k], ks[0], ks[-1])
                    done.then_inc(flag, 1)

            for u in range(2):
                merge_tile(0, u, True)
            with pe.Fori(1, KD // 2) as i:
                for u in range(2):
                    merge_tile(i, u, False)

            def later_tile(ix, ks=KD, hi=H_hi, lo=H_lo):
                n, s, _ = ix
                pe.wait_ge(lo_ready, n + 1)
                pe.wait_ge(bank_read, n - OUT0 + 1)
                steps(s, dense[s], range(ks), 0, ks - 1, hi, lo).then_inc(tile_done, 1)

            pe.wait_ge(m_lo_ready, KD)
            with pe.Fori(0, KD // 2) as i:
                for u in range(2):
                    later_tile(index(i, 2, OUT0 + u), KD, M_hi, M_lo)
            pe.wait_ge(x2_lo, KD)
            PE.matmul(R[2][:], ones, sqacc[:], start=True, stop=True).then_inc(ss2_done, 1)
            with pe.Fori(0, GROUPS_F) as g:
                with pe.Fori(0, FG) as t:
                    for u in range(2):
                        later_tile(ffn_index(g, t, u))
                for u in range(2):
                    n, s, _ = ffn_index(g, 0, 2 * FG + u)
                    if u == 0:
                        pe.wait_ge(lo_ready, n + 1)
                        pe.wait_ge(bank_read, n - OUT0 + 1)
                        steps(s, dense[s], range(FG - 1), 0, FG - 1, G_hi, G_lo)
                        pe.wait_ge(g_lo_ready, g * FG + FG)
                        steps(s, dense[s], [FG - 1], 0, FG - 1, G_hi, G_lo).then_inc(tile_done, 1)
                    else:
                        later_tile((n, s, None), FG, G_hi, G_lo)
                with pe.Fori(1, KD // 2) as i:
                    for u in range(2):
                        later_tile(ffn_index(g, i, 2 * FG + u), FG, G_hi, G_lo)
            pe.wait_ge(acc_ready, 2 * KD + 1)
            PE.matmul(R[2][:], ones, facc[:], start=True, stop=True).then_inc(ss2_done, 1)


def _tiles(w):
    k, n = w.shape
    return np.ascontiguousarray(w.reshape(k // P, P, n // P, P).transpose(2, 1, 0, 3)).reshape(n // P, P, k)


def _shape_constants():
    i = np.arange(P)
    eye = np.eye(P, dtype=np.float32)
    head = (i[:, None] // HD == i[None, :] // HD).astype(np.float32)
    consts = np.stack([eye, np.ones((P, P), np.float32), head, head / HD, eye - head / HD], 1)
    s, t = i[:, None], i[None, :]
    same = s // CHUNK == t // CHUNK
    lq_mask = np.stack([same & (t >= s), same & (t > s), same & (t >= s)], 1).astype(np.float32)
    scan = np.broadcast_to((np.arange(T_SEQ) % CHUNK != 0).astype(np.float32), (P, T_SEQ))
    scan_lq = np.concatenate([scan, lq_mask.reshape(P, 3 * P)], 1)
    levels = np.stack([(s // (2 << l) == t // (2 << l)) & (s // (1 << l) % 2 == 0)
                       & (t // (1 << l) % 2 == 1) for l in range(LEVELS + 1)], 1).astype(np.float32).reshape(P, (LEVELS + 1) * P)
    q, k = np.arange(BLOCK)[:, None], np.arange(2 * BLOCK)[None, :]
    d = BLOCK + q - k
    valid = (d >= 0) & (d < BLOCK)
    masked = np.float32(-1e30)
    dist = np.stack([np.where(valid & (k >= BLOCK), -d, masked), np.where(valid, -d, masked)], 1)
    slopes = np.broadcast_to(2.0 ** (-8.0 * np.arange(1, HEADS + 1) / HEADS), (P, HEADS))
    att = np.concatenate([dist.reshape(P, -1), slopes], 1).astype(np.float32)
    return consts, np.ascontiguousarray(scan_lq), levels, np.ascontiguousarray(att)


def kernel(**inputs):
    import concourse.bacc as _bacc
    from concourse.bass_utils import run_bass_kernel_spmd as _run

    a = {k: np.asarray(v) for k, v in inputs.items()}
    w_in = a["w_in"][0]
    at = np.cumsum([0, WIDTH, KV_WIDTH, KV_WIDTH, WIDTH, WIDTH, WIDTH, DECAY_RANK, ICLR_RANK,
                    GATE_RANK, D_MODEL, D_MODEL])
    wq, wk, wv, wr, wrk, wrv, wdw, wda, wdg, wga, wgb = (
        w_in[:, at[j]:at[j + 1]] for j in range(11))
    order = [wdw, wda, wdg, np.zeros((D_MODEL, 2 * P - GATE_RANK), np.float32)]
    for gp in range(KV_HEADS // 2):
        order += [wk[:, gp * P:(gp + 1) * P], wv[:, gp * P:(gp + 1) * P]]
        for h in range(GROUP):
            for e in range(2):
                head = (2 * gp + e) * GROUP + h
                order.append(wq[:, head * HD:(head + 1) * HD])
    for p in range(PAIRS):
        c = slice(p * P, (p + 1) * P)
        order += [wrk[:, c], wr[:, c], wrv[:, c]]
        for m in (2 * p, 2 * p + 1):
            order += [wga[:, m * P:(m + 1) * P], wgb[:, m * P:(m + 1) * P]]
    w_front = _tiles(np.concatenate(order, 1))

    gate_up = np.concatenate([a["gate_up"][0], np.zeros((2 * P - GATE_RANK, WIDTH), np.float32)], 0)
    ups = np.concatenate([a["decay_up"][0], a["iclr_up"][0], gate_up], 0)
    w_ups = np.ascontiguousarray(ups.reshape(3, P, PAIRS, P).transpose(2, 1, 0, 3))

    wba = a["w_branch_attn"][0].reshape(KV_HEADS // 2, 2, GROUP, HD, D_MODEL).transpose(0, 2, 1, 3, 4)
    w_branch = _tiles(np.concatenate([wba.reshape(WIDTH, D_MODEL), a["w_branch_rwkv"][0]], 0))
    w_slots = np.concatenate([w_front, w_branch, _tiles(a["w_out"][0])], 0)
    gt, ut = _tiles(a["ffn_gate"][0]), _tiles(a["ffn_up"][0])
    w_gu = np.ascontiguousarray(np.stack([gt, ut], 1)).reshape(2 * gt.shape[0], P, SLOT)
    down = a["ffn_down"][0].reshape(GROUPS_F, DSLOT, D_MODEL)
    w_down = np.concatenate([_tiles(down[g]) for g in range(GROUPS_F)], 0)

    norms = np.ascontiguousarray(np.stack(
        [a["norm_mix"][0], a["norm_ffn"][0], a["norm_final"]], 0).reshape(3, KD, P).transpose(2, 0, 1))
    mu = a["tshift_mix"][0]
    mu_r, mu_k, mu_v, mu_low = mu[:WIDTH], mu[WIDTH:2 * WIDTH], mu[2 * WIDTH:3 * WIDTH], mu[3 * WIDTH:]
    pair_cst = np.stack([mu_k, mu_r, mu_v, a["decay_bias"][0], a["iclr_bias"][0], a["k_k"][0],
                         a["k_a"][0], a["r_k"][0].reshape(WIDTH), a["lnx_w"][0], a["lnx_b"][0]], 0)
    pair_cst = np.ascontiguousarray(pair_cst.reshape(NCST, PAIRS, P).transpose(2, 1, 0))
    low_mu = np.concatenate([mu_low, np.zeros(3 * P - mu_low.shape[0], np.float32)])
    low_mu = np.ascontiguousarray(low_mu.reshape(3, P).T)
    sinks = np.ascontiguousarray(np.broadcast_to(a["attn_sinks"][0], (P, HEADS)))
    consts, scan_lq, levels, att_cst = _shape_constants()

    arrays = {
        "xT": np.ascontiguousarray(a["x"][0].T).reshape(KD, P, T_SEQ), "w_slots": w_slots,
        "w_ups": w_ups, "w_gu": w_gu, "w_down": w_down,
        "norms": norms, "pair_cst": pair_cst, "low_mu": low_mu, "sinks": sinks, "consts": consts,
        "scan_lq": scan_lq, "level_masks": levels, "att_cst": att_cst}
    nc = _bacc.Bacc("TRN2", target_bir_lowering=False, num_devices=1)
    args = {n: nc.dram_tensor(n, v.shape, mybir.dt.from_np(v.dtype), kind="ExternalInput").ap()
            for n, v in arrays.items()}
    out = nc.dram_tensor("out", (KD, P, T_SEQ), mybir.dt.float32, kind="ExternalOutput").ap()
    build_layer(nc, out=out, **args)
    r = _run(nc, [arrays], core_ids=[0])
    return np.ascontiguousarray(r.results[0]["out"].reshape(D_MODEL, T_SEQ).T)[None]
```

```python
import math
from contextlib import ExitStack

import numpy as np
import concourse.bass as bass
from concourse import mybir

P = 128
D_MODEL, T_SEQ = 2048, 512
KD = D_MODEL // P
HEADS, HD = 16, 64
KV_HEADS = 4
GROUP = HEADS // KV_HEADS
WIDTH = HEADS * HD
KV_WIDTH = KV_HEADS * HD
PAIRS = WIDTH // P
BLOCK = 128
NB = T_SEQ // BLOCK
CHUNK = 64
CHUNKS = T_SEQ // CHUNK
LEVELS = 5
HALF = P // 2
LAMBDA = math.exp(-0.5)
DECAY_RANK, ICLR_RANK, GATE_RANK = 64, 64, 160
FFN_HIDDEN = -(-8 * D_MODEL // (3 * 256)) * 256
GROUPS_F = 4
FG = FFN_HIDDEN // P // GROUPS_F
NORM_EPS, LNX_EPS = 1e-5, 64e-5
SLOT = KD * P
DSLOT = FG * P

STAGES = KV_HEADS // 2
ATT_TILES = 2 + GROUP
LOW0 = STAGES * ATT_TILES
N_LOW = 3
RW0 = LOW0 + N_LOW
RW_TILES = 7
MERGE0 = RW0 + PAIRS * RW_TILES
OUT0 = MERGE0 + KD
FFN0 = OUT0 + KD
FGRP = 2 * FG + KD
C_MUK, C_MUR, C_MUV, C_DB, C_IB, C_KK, C_KA, C_RK, C_LW, C_LB = range(10)
NCST = 10

UNITS = 2 * NB
ATT_FILL = ({"scores": 8, "probs": 4}, {"scores": 4, "probs": 2})
FILL_TILE0 = (ATT_TILES, LOW0, RW0)
for _g in range(STAGES):
    assert UNITS * sum(ATT_FILL[_g].values()) == (FILL_TILE0[_g + 1] - FILL_TILE0[_g]) * KD
FILL = {"prep": 2, "tok": 2, "solve": 2, "level_a": 2, "level_b": 1, "rhs": 2, "u": 2, "state": 1,
        "y": 1, "center": 2}
assert (FILL["prep"] + FILL["tok"] + FILL["solve"] + LEVELS * (FILL["level_a"] + FILL["level_b"])
        + CHUNKS * (FILL["rhs"] + FILL["u"] + FILL["state"]) + FILL["y"] + FILL["center"]) == 4 * KD


def index(i, per, off):
    return i * per + off, off % 2, i * (per // 2) + off // 2


def ffn_index(g, i, off):
    off += FFN0
    return g * FGRP + i * 2 + off, off % 2, g * (FGRP // 2) + i + off // 2


class Arena:

    def __init__(self, nc, at):
        self.nc, self.at = nc, at

    def __call__(self, name, shape, dt=mybir.dt.float32):
        size = int(np.prod(shape)) * (1 if dt == mybir.dt.uint8 else 4)
        t = self.nc.alloc_sbuf_tensor_at(name, [P] + list(shape), dt, offset=self.at)
        self.at += -(-size // 32) * 32
        return t


def build_layer(nc, xT, w_slots, w_ups, w_gu, w_down, norms, pair_cst, low_mu,
                sinks, consts, scan_lq, level_masks, att_cst, out):
    f32, f32r, u8 = mybir.dt.float32, mybir.dt.float32r, mybir.dt.uint8
    ALU, ACT = mybir.AluOpType, mybir.ActivationFunctionType
    AX = mybir.AxisListType.X
    MUL, ADD, SUB = ALU.mult, ALU.add, ALU.subtract
    V, A, PE = nc.vector, nc.scalar, nc.tensor

    gates_dram = nc.dram_tensor("gates_dram", (4 * PAIRS, P, T_SEQ), f32, kind="Internal").ap()
    y_dram = nc.dram_tensor("y_dram", (2 * PAIRS, P, T_SEQ), f32, kind="Internal").ap()
    x2_dram = nc.dram_tensor("x2_dram", (KD, P, T_SEQ), f32, kind="Internal").ap()

    keep = Arena(nc, -(-nc.sbuf_base // 64) * 64)
    raw = [keep(f"raw{s}", [SLOT]) for s in range(2)]
    whi = [keep(f"whi{s}", [SLOT], f32r) for s in range(2)]
    wlo = [keep(f"wlo{s}", [SLOT], f32r) for s in range(2)]
    H_hi = keep("H_hi", [KD, T_SEQ], f32r)
    H_lo = keep("H_lo", [KD, T_SEQ], f32r)
    cst = keep("cst", [5, P])
    ident, ones, head_ones, head_mean, head_center = (cst[:, i, :] for i in range(5))
    norm_g = keep("norm_g", [3, KD])

    front = Arena(nc, keep.at)
    low = [front(f"low{i}", [T_SEQ]) for i in range(3)]
    lowmu = front("lowmu", [3])
    rstd1 = front("rstd1", [T_SEQ])
    proj = front("proj", [T_SEQ + 1])
    tmp1 = front("tmp1", [T_SEQ])
    ups = [front(f"ups{i}", [3, P]) for i in range(2)]

    start = Arena(nc, front.at)
    X = start("X", [KD, T_SEQ])
    sq = [start(f"sq{i}", [T_SEQ]) for i in range(4)]
    sqsum = [start(f"sqsum{i}", [T_SEQ]) for i in range(2)]

    qkv = Arena(nc, front.at)
    qT = [qkv(f"qT{g}", [GROUP, T_SEQ]) for g in range(STAGES)]
    kT = [qkv(f"kT{g}", [BLOCK + T_SEQ]) for g in range(STAGES)]
    vT = [qkv(f"vT{g}", [T_SEQ]) for g in range(STAGES)]
    vtok = [qkv(f"vtok{g}", [NB + 1, P]) for g in range(STAGES)]
    assert qkv.at <= start.at
    att = Arena(nc, start.at)
    probs = [att(f"probs{i}", [GROUP, 2 * BLOCK]) for i in range(2)]
    pT = att("pT", [2, T_SEQ])
    yatt = [att(f"yatt{g}", [GROUP, T_SEQ]) for g in range(STAGES)]
    att_const = att("att_const", [2 * 2 * BLOCK + HEADS])
    dist = att_const[:, 0:4 * BLOCK].rearrange("p (v k) -> p v k", v=2)
    slopes = att_const[:, 4 * BLOCK:4 * BLOCK + HEADS]
    sink = att("sink", [HEADS])
    rowmax, negmax, rowsum, sinkexp, rowinv = (
        [att(f"{n}{i}", [GROUP]) for i in range(2)]
        for n in ("rowmax", "negmax", "rowsum", "sinkexp", "rowinv"))

    rw = Arena(nc, front.at)
    scanlq = rw("scanlq", [T_SEQ + 3 * P])
    scan_mask = scanlq[:, 0:T_SEQ]
    lq_mask = scanlq[:, T_SEQ:T_SEQ + 3 * P]
    masks = rw("masks", [P + LEVELS * HALF], u8)
    cp_all = rw("cp_all", [PAIRS, NCST])
    cp = [rw(f"cp{i}", [NCST]) for i in range(2)]
    kbuf, rbuf, vbuf = (rw(n, [T_SEQ]) for n in ("kbuf", "rbuf", "vbuf"))
    grow, csum, a_in, icl = (rw(n, [T_SEQ]) for n in ("grow", "csum", "a_in", "icl"))
    kkbuf, kap, tmp2, gbuf, bonus = (
        rw(n, [T_SEQ]) for n in ("kkbuf", "kap", "tmp2", "gbuf", "bonus"))
    zq = rw("zq", [NB, 2, P])
    lq = rw("lq", [2, NB, 3, P])
    Ln = rw("Ln", [2, NB, P])
    Y = rw("Y", [2, NB, P])
    masks_f32 = Y[:].rearrange("p e t n -> p (e t n)")[:, 0:P + LEVELS * HALF]
    Xi = rw("Xi", [2, NB, P])
    W1 = rw("W1", [2, NB, HALF])
    btok, ktok, vtk = (rw(n, [NB, P]) for n in ("btok", "ktok", "vtk"))
    lv, rhs, utok = (rw(n, [NB, P]) for n in ("lv", "rhs", "utok"))
    S, SA = rw("S", [P]), rw("SA", [P])
    gout = [rw(f"gout{i}", [T_SEQ]) for i in range(2)]

    back = Arena(nc, keep.at)
    M_hi, M_lo = back("M_hi", [KD, T_SEQ], f32r), back("M_lo", [KD, T_SEQ], f32r)
    late = Arena(nc, back.at)
    rstd = late("rstd", [T_SEQ])
    gin = [back(f"gin{i}", [2, T_SEQ]) for i in range(2)]
    ystage = [back(f"ystage{i}", [2, T_SEQ]) for i in range(2)]
    mrg = [back(f"mrg{i}", [T_SEQ]) for i in range(2)]
    mtmp = back("mtmp", [T_SEQ])
    xin = [late(f"xin{i}", [T_SEQ]) for i in range(2)]
    x2 = [late(f"x2_{i}", [T_SEQ]) for i in range(2)]
    sqacc, sqx = late("sqacc", [T_SEQ]), late("sqx", [T_SEQ])

    ffn = Arena(nc, keep.at)
    resid = ffn("resid", [KD, T_SEQ])
    G_hi = ffn("G_hi", [FG, T_SEQ], f32r)
    gate_n, gate_s, hid = (ffn(n, [T_SEQ]) for n in ("gate_n", "gate_s", "hid"))
    merged_end = keep.at + 2 * KD * T_SEQ * 4
    fend = Arena(nc, merged_end + T_SEQ * 4)
    G_lo = fend("G_lo", [FG, T_SEQ], f32r)
    facc, fsq = fend("facc", [T_SEQ]), fend("fsq", [T_SEQ])
    assert ffn.at <= merged_end
    assert max(rw.at, att.at, back.at, late.at, fend.at) <= nc.sbuf_usable_end

    with ExitStack() as ctx:
        def sem(name):
            return ctx.enter_context(nc.semaphore(name))

        dense = [ctx.enter_context(nc.psum_tensor(f"dense{i}", [P, T_SEQ], f32)) for i in range(2)]
        R = [ctx.enter_context(nc.psum_tensor(f"work{i}", [P, T_SEQ], f32)) for i in range(6)]
        RA, RB = (R[3], R[5]), (R[4], R[0])

        raw_loaded = [sem(f"raw_loaded{s}") for s in range(2)]
        hi_ready, lo_ready = sem("hi_ready"), sem("lo_ready")
        tile_done = sem("tile_done")
        evacuated = sem("evacuated")
        cst_loaded, att_loaded, rw_loaded = sem("cst_loaded"), sem("att_loaded"), sem("rw_loaded")
        norms_loaded = sem("norms_loaded")
        x_loaded = [sem(f"x_loaded{g}") for g in range(KD // 2)]
        sq_ready, ss_done = sem("sq_ready"), sem("ss_done")
        sq_used = [sem("sq_used_even"), sem("sq_used_odd")]
        ms_ready, rms_ready = sem("ms_ready"), sem("rms_ready")
        h_hi_ready, h_lo_ready = sem("h_hi_ready"), sem("h_lo_ready")
        low_ready, shifted = sem("low_ready"), sem("shifted")
        zeroed = sem("zeroed")
        vt_done, vtok_ready = sem("vt_done"), sem("vtok_ready")
        scores_done, stats_ready, exp_done = sem("scores_done"), sem("stats_ready"), sem("exp_done")
        probs_ready, pt_done, pt_read = sem("probs_ready"), sem("pt_done"), sem("pt_read")
        pv_done, pv_read = sem("pv_done"), sem("pv_read")
        yatt_stored = sem("yatt_stored")
        ups_loaded = [sem(f"ups_loaded{s}") for s in range(2)]
        cp_ready, ups_done, up_read = sem("cp_ready"), sem("ups_done"), sem("up_read")
        cum_ready, exps_ready = sem("cum_ready"), sem("exps_ready")
        ksq_ready, kn_done, kn_read, kn_root = (
            sem("ksq_ready"), sem("kn_done"), sem("kn_read"), sem("kn_root"))
        prep_ready, bonus_done, bonus_read = sem("prep_ready"), sem("bonus_done"), sem("bonus_read")
        tok_done, tok_read, g_done, g_read = (
            sem("tok_done"), sem("tok_read"), sem("g_done"), sem("g_read"))
        ln_done, ln_read, lv_done, lv_read = (
            sem("ln_done"), sem("ln_read"), sem("lv_done"), sem("lv_read"))
        x_done, x_read, w1_done, w1_read = (
            sem("x_done"), sem("x_read"), sem("w1_done"), sem("w1_read"))
        p2_done, p2_seen, p2_read = sem("p2_done"), sem("p2_seen"), sem("p2_read")
        m1_done, rhs_ready, m2_done, u_ready = (
            sem("m1_done"), sem("rhs_ready"), sem("m2_done"), sem("u_ready"))
        m3_done, s_ready, sa_ready = sem("m3_done"), sem("s_ready"), sem("sa_ready")
        y_done, y_ready = sem("y_done"), sem("y_ready")
        cen_done, cen_read = sem("cen_done"), sem("cen_read")
        var_done, var_read, var_root = sem("var_done"), sem("var_read"), sem("var_root")
        y_fin, y_stored = sem("y_fin"), sem("y_stored")
        gate_ready, gate_stored = sem("gate_ready"), [sem(f"gate_stored{s}") for s in range(2)]
        ystage_loaded = [sem(f"ystage_loaded{s}") for s in range(2)]
        yb_hi, yb_lo = sem("yb_hi"), sem("yb_lo")
        gin_loaded = [sem(f"gin_loaded{s}") for s in range(2)]
        attn_half, merge_read = sem("attn_half"), sem("merge_read")
        mrg_ready, m_hi_ready, m_lo_ready = sem("mrg_ready"), sem("m_hi_ready"), sem("m_lo_ready")
        xin_loaded = [sem(f"xin_loaded{s}") for s in range(2)]
        bank_read = sem("bank_read")
        x2_ready, x2sq_ready, x2_hi, x2_lo, acc_ready = (
            sem("x2_ready"), sem("x2sq_ready"), sem("x2_hi"), sem("x2_lo"), sem("acc_ready"))
        x2_stored = [sem(f"x2_stored{s}") for s in range(2)]
        ss2_done, ms2_ready, rms2_ready, rstd_ready = (
            sem("ss2_done"), sem("ms2_ready"), sem("rms2_ready"), sem("rstd_ready"))
        resid_loaded = sem("resid_loaded")
        gate_n_ready, silu_ready, hid_ready, g_hi_ready, g_lo_ready = (
            sem("gate_n_ready"), sem("silu_ready"), sem("hid_ready"), sem("g_hi_ready"),
            sem("g_lo_ready"))
        fin_ready, fsq_ready, out_ready, out_stored = (
            sem("fin_ready"), sem("fsq_ready"), sem("out_ready"), sem("out_stored"))

        def by_block(ap):
            return ap.rearrange("p (t n) -> p t n", t=NB)

        def R_half(bank):
            return bank[:, 0:NB * HALF].rearrange("p (t n) -> p t n", t=NB)

        def second_halves(ap, level):
            dims = "p t" if len(ap.shape) == 3 else "p"
            split = ap.rearrange(f"{dims} (g two n) -> {dims} g two n", two=2, n=2 << level)
            return split[:, :, :, 1, :] if len(ap.shape) == 3 else split[:, :, 1, :]

        def wide(ap, n):
            return ap.unsqueeze(1).to_broadcast([P, n, ap.shape[-1]])

        def tile_of(buf, m):
            return buf[:, m, :] if isinstance(m, int) else buf[:, bass.ds(m, 1), :].rearrange(
                "p a n -> p (a n)")

        class Fill:

            def __init__(self, step, counts=FILL):
                self.pos, self.step, self.counts = 0, step, counts

            def __call__(self, place):
                for _ in range(self.counts[place]):
                    self.step(self.pos // KD, self.pos % KD)
                    self.pos += 1

        block = ctx.enter_context(nc.Block())

        @block.sync
        def _(sp):
            def load(ix, src=None, cols=SLOT):
                n, s, _ = ix
                src = w_slots[n] if src is None else src
                if not (isinstance(n, int) and n < 2):
                    sp.wait_ge(lo_ready, n - 1)
                sp.dma_start(raw[s][:, 0:cols], src).then_inc(raw_loaded[s], 16)

            sp.dma_start(norm_g[:], norms).then_inc(norms_loaded, 16)
            for g in range(KD // 2):
                if g == 1:
                    load(index(0, 2, 0))
                    load(index(0, 2, 1))
                sp.dma_start(X[:, 2 * g:2 * g + 2, :],
                             xT[2 * g:2 * g + 2].rearrange("k p t -> p k t")).then_inc(x_loaded[g], 16)
            sp.dma_start(cst[:], consts).then_inc(cst_loaded, 16)
            load(index(0, 2, 2))
            sp.dma_start(lowmu[:], low_mu).then_inc(att_loaded, 16)
            sp.dma_start(att_const[:], att_cst).then_inc(att_loaded, 16)
            sp.dma_start(sink[:], sinks).then_inc(att_loaded, 16)
            for n in range(3, RW0 + 2):
                load(index(0, 2, n))

            sp.wait_ge(pv_read, 2 + STAGES * UNITS)
            sp.wait_ge(yatt_stored, 16 * STAGES)
            sp.dma_start(scanlq[:], scan_lq).then_inc(rw_loaded, 16)
            sp.dma_start(masks_f32, level_masks).then_inc(rw_loaded, 16)
            sp.dma_start(cp_all[:], pair_cst).then_inc(rw_loaded, 16)
            with sp.Fori(0, PAIRS // 2) as i:
                for u in range(2):
                    p = i * 2 + u
                    sp.wait_ge(ups_done, p + 1)
                    sp.dma_start(ups[u][:], w_ups[p]).then_inc(ups_loaded[u], 16)
                    for j in range(RW_TILES):
                        load(index(i, 2 * RW_TILES, RW0 + 2 + u * RW_TILES + j))

            sp.wait_ge(y_fin, PAIRS)
            for h in range(PAIRS):
                if h == PAIRS // 2:
                    sp.wait_ge(y_stored, 16 * (PAIRS + 1))
                if h >= 2:
                    sp.wait_ge(yb_lo, h - 1)
                sp.dma_start(ystage[h % 2][:],
                             y_dram[2 * h:2 * h + 2].rearrange("k p t -> p k t")
                             ).then_inc(ystage_loaded[h % 2], 16)
            for s in range(2):
                sp.wait_ge(gate_stored[s], 16 * (2 * PAIRS + 1))
            for m in range(2):
                sp.dma_start(gin[m][:], gates_dram[2 * m:2 * m + 2].rearrange("k p t -> p k t")
                             ).then_inc(gin_loaded[m], 16)
            with sp.Fori(1, KD // 2) as i:
                for u in range(2):
                    m = i * 2 + u
                    load(index(i, 2, MERGE0 + u))
                    sp.wait_ge(merge_read, m - 1)
                    sp.dma_start(gin[u][:], gates_dram[bass.ds(m * 2, 2)].rearrange("k p t -> p k t")
                                 ).then_inc(gin_loaded[u], 16)

            for s in range(2):
                load(index(0, 2, OUT0 + s))
            sp.wait_ge(m_lo_ready, KD)
            for m in range(2):
                sp.dma_start(xin[m][:], xT[m]).then_inc(xin_loaded[m], 16)
            with sp.Fori(1, KD // 2) as i:
                for u in range(2):
                    m = i * 2 + u
                    load(index(i, 2, OUT0 + u))
                    sp.wait_ge(x2_ready, m - 1)
                    sp.dma_start(xin[u][:], xT[m]).then_inc(xin_loaded[u], 16)

            for s in range(2):
                load(ffn_index(0, 0, s), w_gu[s])
            sp.wait_ge(tile_done, FFN0)
            for s in range(2):
                sp.wait_ge(x2_stored[s], 16 * (KD // 2 + 1))
            for g in range(4):
                sp.dma_start(resid[:, 4 * g:4 * g + 4, :],
                             x2_dram[4 * g:4 * g + 4].rearrange("k p t -> p k t")
                             ).then_inc(resid_loaded, 16)

            def load_down(g):
                with sp.Fori(0, KD // 2) as i:
                    for u in range(2):
                        load(ffn_index(g, i, 2 * FG + u), w_down[g * KD + i * 2 + u], DSLOT)

            with sp.Fori(1, FG) as t:
                for u in range(2):
                    load(ffn_index(0, t, u), w_gu[t * 2 + u])
            load_down(0)
            with sp.Fori(1, GROUPS_F) as g:
                with sp.Fori(0, FG) as t:
                    for u in range(2):
                        load(ffn_index(g, t, u), w_gu[g * (2 * FG) + t * 2 + u])
                load_down(g)

            for g in range(4):
                sp.wait_ge(out_ready, 4 * g + 4)
                sp.dma_start(out[4 * g:4 * g + 4].rearrange("k p t -> p k t"),
                             resid[:, 4 * g:4 * g + 4, :]).then_inc(out_stored, 16)
            sp.wait_ge(out_stored, 64)

        @block.gpsimd
        def _(pool):
            def low_part(ix, cols=SLOT):
                n, s, _ = ix
                pool.wait_ge(hi_ready, n + 1)
                nc.gpsimd.tensor_tensor(wlo[s][:, 0:cols], raw[s][:, 0:cols],
                                        whi[s][:, 0:cols].bitcast(f32), SUB).then_inc(lo_ready, 1)

            pool.wait_ge(lo_ready, 1)
            low_part(index(0, 2, 1))
            nc.gpsimd.memset(sqsum[1][:], 0.0)
            for k in range(1, KD, 2):
                pool.wait_ge(sq_ready, k + 1)
                nc.gpsimd.drain()
                nc.gpsimd.tensor_tensor(sqsum[1][:], sqsum[1][:], sq[k % 4][:], ADD
                                        ).then_inc(sq_used[1], 1)
            low_part(index(0, 2, 2))
            with pool.Fori(1, FFN0 // 2) as i:
                for u in range(2):
                    low_part(index(i, 2, 1 + u))
            with pool.Fori(0, GROUPS_F) as g:
                with pool.Fori(0, FG) as t:
                    for u in range(2):
                        low_part(ffn_index(g, t, u))
                with pool.Fori(0, KD // 2) as i:
                    for u in range(2):
                        low_part(ffn_index(g, i, 2 * FG + u), DSLOT)

        @block.scalar
        def _(act):
            act.sem_inc(evacuated, 2)
            act.sem_inc(pt_read, 1)
            act.sem_inc(pv_read, 2)
            act.sem_inc(cen_read, 1)
            act.sem_inc(y_stored, 16)
            for s in range(2):
                act.sem_inc(gate_stored[s], 16)
                act.sem_inc(x2_stored[s], 16)

            def copy(dst, src, scale=1.0):
                return A.activation(dst, src, ACT.Copy, scale=scale)

            def split(ix, cols=SLOT):
                n, s, h = ix
                act.wait_ge(raw_loaded[s], h * 16 + 16)
                if not (isinstance(n, int) and n < 2):
                    act.wait_ge(tile_done, n - 1)
                copy(whi[s][:, 0:cols], raw[s][:, 0:cols]).then_inc(hi_ready, 1)

            act.wait_ge(norms_loaded, 16)
            def hi_part(k):
                act.wait_ge(x_loaded[k // 2], 16)
                copy(H_hi[:, k, :], X[:, k, :], norm_g[:, 0, k:k + 1]).then_inc(h_hi_ready, 1)

            def square(k):
                if k >= 4:
                    act.wait_ge(sq_used[k % 2], k // 2 - 1)
                A.activation(sq[k % 4][:], X[:, k, :], ACT.Square).then_inc(sq_ready, 1)

            hi_part(0)
            hi_part(1)
            split(index(0, 2, 0))
            square(0)
            square(1)
            split(index(0, 2, 1))
            for k in range(2, KD):
                hi_part(k)
                square(k)

            act.wait_ge(tile_done, 1)
            copy(kT[0][:, BLOCK:BLOCK + T_SEQ], dense[0][:]).then_inc(evacuated, 1)
            act.wait_ge(tile_done, 2)
            copy(vT[0][:], dense[1][:]).then_inc(evacuated, 1)
            for n in range(ATT_TILES):
                split(index(0, 2, n + 2))
                if n == 0:
                    act.wait_ge(ms_ready, 1)
                    A.activation(rstd1[:], rstd1[:], ACT.Sqrt).then_inc(rms_ready, 1)

            for g in range(STAGES):
                def next_tile(tile, k):
                    if k == KD - 1:
                        split(index(0, 2, FILL_TILE0[g] + tile + 2))

                fill = Fill(next_tile, ATT_FILL[g])

                def exps(w):
                    act.wait_ge(stats_ready, g * UNITS + w + 1)
                    for h in range(GROUP):
                        A.activation(probs[w % 2][:, h, :], probs[w % 2][:, h, :], ACT.Exp,
                                     bias=negmax[w % 2][:, h:h + 1],
                                     accum_out=rowsum[w % 2][:, h:h + 1])
                    A.activation(sinkexp[w % 2][:], sinkexp[w % 2][:], ACT.Exp).then_inc(exp_done, 1)

                act.wait_ge(vt_done, g + 1)
                act.wait_ge(zeroed, 2)
                copy(vtok[g][:, 1:NB + 1, :], by_block(R[0][:])).then_inc(vtok_ready, 1)
                exps(0)
                for w in range(UNITS):
                    e, b = w // NB, w % NB
                    W = g * UNITS + w
                    if w + 1 < UNITS:
                        exps(w + 1)
                    fill("scores")
                    act.wait_ge(pt_done, W + 3)
                    act.wait_ge(pv_done, W + 1)
                    copy(pT[:, 0, :], R[5][:])
                    copy(pT[:, 1, :], R[0][:]).then_inc(pt_read, 1)
                    fill("probs")
                    act.wait_ge(pv_done, W + 2)
                    copy(yatt[g][e * HD:e * HD + HD, :, b * BLOCK:(b + 1) * BLOCK],
                         R[1 + 2 * (w % 2)][e * HD:e * HD + HD, :].rearrange(
                             "p (h t) -> p h t", h=GROUP)).then_inc(pv_read, 1)
                act.wait_ge(pv_read, (g + 1) * UNITS + 2)
                act.dma_start(y_dram[g * GROUP:(g + 1) * GROUP].rearrange("k p t -> p k t"),
                              yatt[g][:]).then_inc(yatt_stored, 16)

            act.wait_ge(shifted, N_LOW)
            A.activation(low[0][0:DECAY_RANK, :], low[0][0:DECAY_RANK, :], ACT.Tanh)
            A.activation(low[1][:], low[1][:], ACT.Sigmoid)
            A.activation(low[2][:], low[2][:], ACT.Sigmoid).then_inc(low_ready, 1)

            act.wait_ge(rw_loaded, 48)
            with act.Fori(0, PAIRS // 2) as i:
                for u in range(2):
                    p = i * 2 + u
                    c = cp[u]

                    def front_tile(j):
                        split(index(i, 2 * RW_TILES, RW0 + u * RW_TILES + j + 2))

                    def gate_step(tile, k):
                        if k < KD - 1:
                            return
                        n, s, _ = index(i, 2 * RW_TILES, RW0 + u * RW_TILES + 3 + tile)
                        split(index(i, 2 * RW_TILES, RW0 + u * RW_TILES + 3 + tile + 2))
                        act.wait_ge(evacuated, n + 3)
                        A.activation(gout[tile % 2][:], gout[tile % 2][:], ACT.Sigmoid
                                     ).then_inc(gate_ready, 1)
                        act.wait_ge(gate_ready, p * 4 + tile + 1)
                        act.dma_start(gates_dram[p * 4 + tile], gout[tile % 2][:]
                                      ).then_inc(gate_stored[tile % 2], 16)

                    fill = Fill(gate_step)
                    front_tile(0)
                    act.wait_ge(cp_ready, p + 1)
                    act.wait_ge(ups_done, p + 3)
                    A.activation(grow[:], R[0][:], ACT.Sigmoid, bias=c[:, C_DB:C_DB + 1]
                                 ).then_inc(up_read, 1)
                    A.activation(icl[:], R[1][:], ACT.Sigmoid, bias=c[:, C_IB:C_IB + 1]
                                 ).then_inc(up_read, 1)
                    copy(gbuf[:], R[2][:]).then_inc(up_read, 1)
                    act.wait_ge(cum_ready, p + 1)
                    A.activation(a_in[:], csum[:], ACT.Exp, scale=-LAMBDA)
                    A.activation(zq[:, :, 0, :], zq[:, :, 0, :], ACT.Exp, scale=-LAMBDA)
                    A.activation(grow[:], csum[:], ACT.Exp, scale=LAMBDA).then_inc(exps_ready, 1)
                    front_tile(1)
                    act.wait_ge(kn_read, p + 1)
                    A.activation(tmp1[:], tmp1[:], ACT.Sqrt).then_inc(kn_root, 1)
                    front_tile(2)
                    fill("prep")
                    for bank, dst, count in ((R[1], btok, 1), (R[2], ktok, 2), (R[0], vtk, 3)):
                        act.wait_ge(tok_done, p * 3 + count)
                        copy(dst[:], by_block(bank[:])).then_inc(tok_read, 1)
                    fill("tok")
                    for e in range(2):
                        act.wait_ge(ln_done, p * 2 + e + 1)
                        copy(Ln[:, e], by_block(R[1 + e][:])).then_inc(ln_read, 1)
                    fill("solve")
                    act.wait_ge(lv_done, p + 1)
                    copy(lv[:], by_block(R[1][:])).then_inc(lv_read, 1)
                    for level in range(LEVELS):
                        for e in range(2):
                            act.wait_ge(x_done, p * (2 * LEVELS) + 2 * level + e + 1)
                            copy(Xi[:, e], by_block(RA[e][:])).then_inc(x_read, 1)
                            act.wait_ge(w1_done, p * (2 * LEVELS) + 2 * level + e + 1)
                            copy(W1[:, e], R_half(RB[e])).then_inc(w1_read, 1)
                        fill("level_a")
                        fill("level_b")
                    for n in range(CHUNKS):
                        t, lo = n // 2, CHUNK * (n % 2)
                        if n + 1 < CHUNKS:
                            end = n * CHUNK + CHUNK - 1
                            act.wait_ge(s_ready, p * CHUNKS + n + 1)
                            copy(SA[:], S[:], a_in[:, end:end + 1]).then_inc(sa_ready, 1)
                        act.wait_ge(m2_done, p * CHUNKS + n + 1)
                        copy(utok[lo:lo + CHUNK, t, :], R[3][lo:lo + CHUNK, 0:P]).then_inc(u_ready, 1)
                        if n:
                            fill("u")
                            fill("state")
                        fill("rhs")
                    fill("u")
                    fill("state")
                    act.wait_ge(y_done, p + 1)
                    copy(csum[:], R[5][:]).then_inc(y_ready, 1)
                    fill("y")
                    act.wait_ge(cen_done, p + 1)
                    copy(kkbuf[:], R[0][:])
                    A.activation(tmp1[:], R[0][:], ACT.Square).then_inc(cen_read, 1)
                    fill("center")
                    act.wait_ge(var_read, p + 2)
                    A.activation(tmp2[:], tmp2[:], ACT.Sqrt).then_inc(var_root, 1)
                    act.wait_ge(y_fin, p + 1)
                    act.dma_start(y_dram[p + PAIRS], bonus[:]).then_inc(y_stored, 16)

            for h in range(PAIRS):
                act.wait_ge(ystage_loaded[h % 2], 16 * (h // 2 + 1))
                copy(H_hi[:, 2 * h:2 * h + 2, :], ystage[h % 2][:]).then_inc(yb_hi, 1)

            with act.Fori(0, KD // 2) as i:
                for u in range(2):
                    m = i * 2 + u
                    split(index(i, 2, MERGE0 + u + 2))
                    act.wait_ge(mrg_ready, m + 1)
                    copy(tile_of(M_hi, m), mrg[u][:]).then_inc(m_hi_ready, 1)

            with act.Fori(0, KD // 2) as i:
                for u in range(2):
                    m = i * 2 + u
                    split(index(i, 2, OUT0 + u + 2))
                    act.wait_ge(x2_ready, m + 1)
                    act.dma_start(x2_dram[m], x2[u][:]).then_inc(x2_stored[u], 16)
                    act.wait_ge(acc_ready, m + 1)
                    A.activation(sqx[:], x2[u][:], ACT.Square).then_inc(x2sq_ready, 1)
                    copy(tile_of(H_hi, m), x2[u][:], norm_g[:, 1, bass.ds(m, 1)]).then_inc(x2_hi, 1)
            act.wait_ge(ms2_ready, 1)
            A.activation(rstd[:], rstd[:], ACT.Sqrt).then_inc(rms2_ready, 1)

            def hidden(g, t, cols):
                for u in range(2):
                    if u == 1:
                        hn = g * FG + t
                        act.wait_ge(gate_n_ready, hn + 1)
                        A.activation(gate_s[:], gate_n[:], ACT.Silu).then_inc(silu_ready, 1)
                    split(ffn_index(g, t, u + 2), cols)
                    if u == 1:
                        act.wait_ge(hid_ready, hn + 1)
                        copy(tile_of(G_hi, t), hid[:]).then_inc(g_hi_ready, 1)

            def last_square(m):
                act.wait_ge(fin_ready, m + 1)
                act.wait_ge(acc_ready, m + KD + 1)
                A.activation(fsq[:], tile_of(resid, m), ACT.Square).then_inc(fsq_ready, 1)

            def hidden_tiles(g):
                with act.Fori(0, FG - 1) as t:
                    hidden(g, t, SLOT)
                hidden(g, FG - 1, DSLOT)

            with act.Fori(0, GROUPS_F - 1) as g:
                hidden_tiles(g)
                with act.Fori(0, KD // 2 - 1) as i:
                    for u in range(2):
                        split(ffn_index(g, i, 2 * FG + u + 2), DSLOT)
                for u in range(2):
                    split(ffn_index(g, 0, FGRP + u))
            hidden_tiles(GROUPS_F - 1)
            with act.Fori(0, KD // 2 - 1) as i:
                for u in range(2):
                    split(ffn_index(GROUPS_F - 1, i, 2 * FG + u + 2), DSLOT)
                    last_square(i * 2 + u)
            for m in (KD - 2, KD - 1):
                last_square(m)
            act.wait_ge(ms2_ready, 2)
            A.activation(rstd[:], rstd[:], ACT.Sqrt).then_inc(rms2_ready, 1)

        @block.vector
        def _(dve):
            dve.sem_inc(var_read, 1)
            dve.sem_inc(bank_read, 2)
            dve.sem_inc(acc_ready, 1)

            def fence():
                V.drain()

            V.memset(proj[:, 0:1], 0.0)
            V.drain().then_inc(zeroed, 1)

            dve.wait_ge(norms_loaded, 16)
            V.memset(sqsum[0][:], 0.0)
            for k in range(KD):
                dve.wait_ge(h_hi_ready, k + 1)
                V.scalar_tensor_tensor(H_lo[:, k, :], X[:, k, :], norm_g[:, 0, k:k + 1],
                                       H_hi[:, k, :].bitcast(f32), MUL, SUB).then_inc(h_lo_ready, 1)
                if k == 1:
                    dve.wait_ge(hi_ready, 1)
                    V.tensor_tensor(wlo[0][:], raw[0][:], whi[0][:].bitcast(f32), SUB
                                    ).then_inc(lo_ready, 1)
                if k % 2:
                    dve.wait_ge(sq_ready, k)
                    fence()
                    V.tensor_tensor(sqsum[0][:], sqsum[0][:], sq[(k - 1) % 4][:], ADD
                                    ).then_inc(sq_used[0], 1)
            dve.wait_ge(ss_done, 1)
            V.tensor_scalar(rstd1[:], R[0][:], 1.0 / D_MODEL, NORM_EPS, MUL, ADD).then_inc(ms_ready, 1)
            for g in range(STAGES):
                V.memset(kT[g][:, 0:BLOCK], 0.0)
                V.memset(vtok[g][:, 0, :], 0.0)
            V.drain().then_inc(zeroed, 1)
            dve.wait_ge(rms_ready, 1)
            V.reciprocal(rstd1[:], rstd1[:])
            fence()
            dve.wait_ge(evacuated, 4)
            V.tensor_tensor(kT[0][:, BLOCK:BLOCK + T_SEQ], kT[0][:, BLOCK:BLOCK + T_SEQ], rstd1[:], MUL)
            V.tensor_tensor(vT[0][:], vT[0][:], rstd1[:], MUL)

            def evacuate(dst, n, s):
                dve.wait_ge(tile_done, n + 1)
                V.tensor_tensor(dst, rstd1[:], dense[s][:], MUL).then_inc(evacuated, 1)

            def evacuate_qkv(g, j):
                n = g * ATT_TILES + j
                if j == 0:
                    evacuate(kT[g][:, BLOCK:BLOCK + T_SEQ], n, n % 2)
                elif j == 1:
                    evacuate(vT[g][:], n, n % 2)
                else:
                    dve.wait_ge(tile_done, n + 1)
                    V.scalar_tensor_tensor(qT[g][:, j - 2, :], dense[n % 2][:], HD ** -0.5, rstd1[:],
                                           MUL, MUL).then_inc(evacuated, 1)

            def shift(dst, mu, scratch=tmp1):
                fence()
                cur, prev = proj[:, 1:T_SEQ + 1], proj[:, 0:T_SEQ]
                V.tensor_tensor(scratch[:], prev, cur, SUB)
                fence()
                V.scalar_tensor_tensor(dst, scratch[:], mu, cur, MUL, ADD).then_inc(shifted, 1)

            for j in range(2, ATT_TILES):
                evacuate_qkv(0, j)

            dve.wait_ge(att_loaded, 48)
            for g in range(STAGES):
                def next_tile(tile, k):
                    if k < KD - 1:
                        return
                    if g + 1 < STAGES:
                        evacuate_qkv(g + 1, tile)
                    else:
                        evacuate(proj[:, 1:T_SEQ + 1], LOW0 + tile, tile % 2)
                        shift(low[tile][:], lowmu[:, tile:tile + 1])

                fill = Fill(next_tile, ATT_FILL[g])

                def stats(w):
                    e, b = w // NB, w % NB
                    W = g * UNITS + w
                    s = w % 2
                    head0 = (2 * g + e) * GROUP
                    dve.wait_ge(scores_done, W + 1)
                    dve.wait_ge(pt_done, W + 1)
                    for h in range(GROUP):
                        V.scalar_tensor_tensor(
                            probs[s][:, h, :], dist[:, min(b, 1), :],
                            slopes[:, head0 + h:head0 + h + 1],
                            R[1 + 2 * s + h // 2][:, (h % 2) * 2 * BLOCK:(h % 2 + 1) * 2 * BLOCK],
                            MUL, ADD)
                    fence()
                    V.tensor_reduce(rowmax[s][:], probs[s][:], AX, ALU.max)
                    fence()
                    sinks_e = sink[:, head0:head0 + GROUP]
                    V.tensor_tensor(rowmax[s][:], rowmax[s][:], sinks_e, ALU.max)
                    fence()
                    V.tensor_scalar(negmax[s][:], rowmax[s][:], -1.0, None, MUL)
                    V.tensor_tensor(sinkexp[s][:], sinks_e, rowmax[s][:], SUB).then_inc(stats_ready, 1)

                def normalise(w):
                    s = w % 2
                    dve.wait_ge(exp_done, g * UNITS + w + 1)
                    V.tensor_tensor(rowsum[s][:], rowsum[s][:], sinkexp[s][:], ADD)
                    fence()
                    V.reciprocal(rowinv[s][:], rowsum[s][:])
                    fence()
                    for h in range(GROUP):
                        last = V.tensor_scalar(probs[s][:, h, :], probs[s][:, h, :],
                                               rowinv[s][:, h:h + 1], None, MUL)
                    last.then_inc(probs_ready, 1)

                stats(0)
                for w in range(UNITS):
                    if w + 1 < UNITS:
                        stats(w + 1)
                    normalise(w)
                    fill("scores")
                    fill("probs")

            dve.wait_ge(rw_loaded, 48)
            V.tensor_copy(masks[:], masks_f32)
            V.memset(rhs[:], 0.0)
            V.memset(utok[:], 0.0)
            fence()
            with dve.Fori(0, PAIRS // 2) as i:
                for u in range(2):
                    p = i * 2 + u
                    n0 = i * (2 * RW_TILES) + RW0 + u * RW_TILES
                    c = cp[u]
                    col = lambda k: c[:, k:k + 1]
                    s0 = (RW0 + u * RW_TILES) % 2

                    def gate_step(tile, k):
                        if k < KD - 1:
                            return
                        dve.wait_ge(gate_stored[tile % 2], (p * 2 + tile // 2) * 16 + 16)
                        evacuate(gout[tile % 2][:], n0 + 3 + tile, (s0 + 3 + tile) % 2)

                    fill = Fill(gate_step)
                    zn, q = zq[:, :, 0, :], zq[:, :, 1, :]

                    V.tensor_copy(c[:], tile_of(cp_all, p))
                    V.drain().then_inc(cp_ready, 1)
                    evacuate(proj[:, 1:T_SEQ + 1], n0, s0)
                    shift(kbuf[:], col(C_MUK))
                    fence()
                    V.tensor_scalar(kkbuf[:], kbuf[:], col(C_KK), None, MUL)
                    fence()
                    V.tensor_tensor(tmp1[:], kkbuf[:], kkbuf[:], MUL).then_inc(ksq_ready, 1)
                    dve.wait_ge(up_read, p * 3 + 3)
                    V.tensor_tensor_scan(csum[:], scan_mask, grow[:], 0.0, MUL, ADD)
                    fence()
                    V.tensor_tensor(zn, by_block(csum[:]), by_block(grow[:]), SUB).then_inc(cum_ready, 1)
                    V.tensor_scalar(tmp2[:], icl[:], 1.0, col(C_KA), SUB, MUL)
                    fence()
                    V.scalar_tensor_tensor(kbuf[:], tmp2[:], 1.0, kbuf[:], ADD, MUL)
                    fence()
                    dve.wait_ge(exps_ready, p + 1)
                    V.tensor_tensor(kap[:], kbuf[:], grow[:], MUL)
                    evacuate(proj[:, 1:T_SEQ + 1], n0 + 1, 1 - s0)
                    shift(rbuf[:], col(C_MUR), csum)
                    dve.wait_ge(kn_done, p + 1)
                    V.tensor_scalar(tmp1[:], R[3][:], 1e-24, None, ALU.max).then_inc(kn_read, 1)
                    fence()
                    V.tensor_tensor(q, by_block(rbuf[:]), by_block(a_in[:]), MUL)
                    V.scalar_tensor_tensor(tmp2[:], rbuf[:], col(C_RK), kbuf[:], MUL, MUL)
                    dve.wait_ge(kn_root, p + 1)
                    V.reciprocal(tmp1[:], tmp1[:])
                    fence()
                    V.scalar_tensor_tensor(kkbuf[:], kkbuf[:], -1.0, tmp1[:], MUL, MUL)
                    fence()
                    V.tensor_tensor(zn, zn, by_block(kkbuf[:]), MUL)
                    V.scalar_tensor_tensor(tmp1[:], icl[:], -1.0, kkbuf[:], MUL, MUL)
                    fence()
                    V.tensor_tensor(icl[:], tmp1[:], grow[:], MUL).then_inc(prep_ready, 1)
                    evacuate(proj[:, 1:T_SEQ + 1], n0 + 2, s0)
                    shift(vbuf[:], col(C_MUV))
                    V.tensor_copy(Y[:].rearrange("p e t n -> p (e t) n"), wide(ident, 2 * NB))
                    fence()
                    dve.wait_ge(bonus_done, p + 1)
                    dve.wait_ge(y_stored, p * 16 + 16)
                    V.tensor_tensor(bonus[:], vbuf[:], R[3][:], MUL).then_inc(bonus_read, 1)
                    fill("prep")
                    fill("tok")
                    for t in range(NB):
                        for e in range(2):
                            bank = ((R[3], R[4]), (R[5], R[0]))[e][t % 2]
                            dve.wait_ge(g_done, p * (2 * NB) + 2 * t + e + 1)
                            V.tensor_tensor(lq[:, e, t].rearrange("p a b -> p (a b)"),
                                            bank[:, P:4 * P], lq_mask, MUL)
                            V.copy_predicated(Y[:, e, t, :], masks[:, 0:P], bank[:, 0:P]
                                              ).then_inc(g_read, 1)
                    fill("solve")
                    for level in range(LEVELS):
                        fill("level_a")
                        for e in range(2):
                            dve.wait_ge(p2_done, p * (2 * LEVELS) + 2 * level + e + 1)
                            dve.sem_inc(p2_seen, 1)
                            mask = masks[:, P + level * HALF:P + (level + 1) * HALF]
                            V.copy_predicated(
                                second_halves(Y[:, e], level),
                                wide(mask, NB).rearrange("p t (g n) -> p t g n", n=2 << level),
                                R_half(RA[e]).rearrange("p t (g n) -> p t g n", n=2 << level)
                            ).then_inc(p2_read, 1)
                        fill("level_b")
                    V.memset(S[:], 0.0).then_inc(s_ready, 1)
                    for n in range(CHUNKS):
                        t, lo = n // 2, CHUNK * (n % 2)
                        dve.wait_ge(m1_done, p * CHUNKS + n + 1)
                        if n == 0:
                            dve.wait_ge(lv_read, p + 1)
                        V.tensor_tensor(rhs[lo:lo + CHUNK, t, :], lv[lo:lo + CHUNK, t, :],
                                        R[2][lo:lo + CHUNK, 0:P], ADD).then_inc(rhs_ready, 1)
                        if n:
                            fill("u")
                            fill("state")
                        fill("rhs")
                        if n + 1 < CHUNKS:
                            end = n * CHUNK + CHUNK - 1
                            dve.wait_ge(m3_done, p * (CHUNKS - 1) + n + 1)
                            dve.wait_ge(sa_ready, p * (CHUNKS - 1) + n + 1)
                            for e in range(2):
                                d = slice(e * HD, e * HD + HD)
                                last = V.scalar_tensor_tensor(S[d, d], R[4][d, d], a_in[d, end:end + 1],
                                                              SA[d, d], MUL, ADD)
                            last.then_inc(s_ready, 1)
                    for place in ("u", "state", "y", "center"):
                        fill(place)
                    dve.wait_ge(var_done, p + 1)
                    V.tensor_scalar(tmp2[:], R[1][:], LNX_EPS, None, ADD).then_inc(var_read, 1)
                    dve.wait_ge(var_root, p + 1)
                    V.reciprocal(tmp1[:], tmp2[:])
                    fence()
                    V.tensor_tensor(kkbuf[:], kkbuf[:], tmp1[:], MUL)
                    fence()
                    V.tensor_scalar(kkbuf[:], kkbuf[:], col(C_LW), col(C_LB), MUL, ADD)
                    fence()
                    V.tensor_tensor(kkbuf[:], kkbuf[:], bonus[:], ADD)
                    fence()
                    V.tensor_tensor(bonus[:], kkbuf[:], gbuf[:], MUL).then_inc(y_fin, 1)

            for h in range(PAIRS):
                dve.wait_ge(yb_hi, h + 1)
                V.tensor_tensor(H_lo[:, 2 * h:2 * h + 2, :], ystage[h % 2][:],
                                H_hi[:, 2 * h:2 * h + 2, :].bitcast(f32), SUB).then_inc(yb_lo, 1)

            with dve.Fori(0, KD // 2) as i:
                for u in range(2):
                    m = i * 2 + u
                    a_bank, b_bank = (dense[1], dense[0]) if u == 0 else (R[0], R[1])
                    dve.wait_ge(gin_loaded[u], i * 16 + 16)
                    dve.wait_ge(attn_half, m + 1)
                    V.tensor_tensor(mtmp[:], gin[u][:, 0, :], a_bank[:], MUL)
                    dve.wait_ge(tile_done, m + MERGE0 + 1)
                    V.tensor_tensor(mrg[u][:], gin[u][:, 1, :], b_bank[:], MUL).then_inc(merge_read, 1)
                    fence()
                    V.tensor_tensor(mrg[u][:], mrg[u][:], mtmp[:], ADD).then_inc(mrg_ready, 1)
                    dve.wait_ge(m_hi_ready, m + 1)
                    V.tensor_tensor(tile_of(M_lo, m), mrg[u][:], tile_of(M_hi, m).bitcast(f32), SUB
                                    ).then_inc(m_lo_ready, 1)

            V.memset(sqacc[:], 0.0)
            with dve.Fori(0, KD // 2) as i:
                for u in range(2):
                    m = i * 2 + u
                    bank = dense[(OUT0 + u) % 2]
                    dve.wait_ge(xin_loaded[u], i * 16 + 16)
                    dve.wait_ge(x2_stored[u], i * 16 + 16)
                    dve.wait_ge(tile_done, m + OUT0 + 1)
                    V.tensor_tensor(x2[u][:], xin[u][:], bank[:], ADD).then_inc(bank_read, 1)
                    V.drain().then_inc(x2_ready, 1)
                    dve.wait_ge(x2sq_ready, m + 1)
                    V.tensor_tensor(sqacc[:], sqacc[:], sqx[:], ADD).then_inc(acc_ready, 1)
                    dve.wait_ge(x2_hi, m + 1)
                    V.scalar_tensor_tensor(tile_of(H_lo, m), x2[u][:], norm_g[:, 1, bass.ds(m, 1)],
                                           tile_of(H_hi, m).bitcast(f32), MUL, SUB
                                           ).then_inc(x2_lo, 1)
            dve.wait_ge(ss2_done, 1)
            V.tensor_scalar(rstd[:], R[2][:], 1.0 / D_MODEL, NORM_EPS, MUL, ADD).then_inc(ms2_ready, 1)
            dve.wait_ge(rms2_ready, 1)
            V.reciprocal(rstd[:], rstd[:])
            fence()

            def hidden_tiles(g):
                with dve.Fori(0, FG) as t:
                    n, s, _ = ffn_index(g, t, 0)
                    hn = g * FG + t
                    dve.wait_ge(tile_done, n + 1)
                    V.tensor_tensor(gate_n[:], rstd[:], dense[s][:], MUL).then_inc(bank_read, 1)
                    V.drain().then_inc(gate_n_ready, 1)
                    dve.wait_ge(tile_done, n + 2)
                    V.tensor_tensor(hid[:], rstd[:], dense[1 - s][:], MUL).then_inc(bank_read, 1)
                    fence()
                    dve.wait_ge(silu_ready, hn + 1)
                    V.tensor_tensor(hid[:], hid[:], gate_s[:], MUL).then_inc(hid_ready, 1)
                    dve.wait_ge(g_hi_ready, hn + 1)
                    V.tensor_tensor(tile_of(G_lo, t), hid[:], tile_of(G_hi, t).bitcast(f32), SUB
                                    ).then_inc(g_lo_ready, 1)

            def down_tile(g, i, u):
                n, s, _ = ffn_index(g, i, 2 * FG + u)
                m = i * 2 + u
                dve.wait_ge(tile_done, n + 1)
                V.tensor_tensor(tile_of(resid, m), tile_of(resid, m), dense[s][:], ADD
                                ).then_inc(bank_read, 1)

            with dve.Fori(0, GROUPS_F - 1) as g:
                hidden_tiles(g)
                dve.wait_ge(resid_loaded, 64)
                with dve.Fori(0, KD // 2) as i:
                    for u in range(2):
                        down_tile(g, i, u)
            hidden_tiles(GROUPS_F - 1)
            V.memset(facc[:], 0.0)
            fence()
            with dve.Fori(0, KD // 2) as i:
                for u in range(2):
                    m = i * 2 + u
                    down_tile(GROUPS_F - 1, i, u)
                    V.drain().then_inc(fin_ready, 1)
                    dve.wait_ge(fsq_ready, m + 1)
                    V.tensor_tensor(facc[:], facc[:], fsq[:], ADD).then_inc(acc_ready, 1)
            dve.wait_ge(ss2_done, 2)
            V.tensor_scalar(rstd[:], R[2][:], 1.0 / D_MODEL, NORM_EPS, MUL, ADD).then_inc(ms2_ready, 1)
            dve.wait_ge(rms2_ready, 2)
            V.reciprocal(rstd[:], rstd[:])
            fence()
            for m in range(KD):
                V.scalar_tensor_tensor(resid[:, m, :], resid[:, m, :], norm_g[:, 2, m:m + 1], rstd[:],
                                       MUL, MUL).then_inc(out_ready, 1)

        @block.tensor
        def _(pe):
            pe.sem_inc(pt_done, 2)
            pe.sem_inc(pv_done, 1)
            pe.sem_inc(ups_done, 2)

            def steps(s, bank, ks, first, last, hi=H_hi, lo=H_lo, w0=0):
                for k in ks:
                    wk = slice((k - w0) * P, (k - w0 + 1) * P)
                    PE.matmul(bank[:], whi[s][:, wk], hi[:, k, :], start=(k == first), stop=False)
                    PE.matmul(bank[:], whi[s][:, wk], lo[:, k, :], start=False, stop=False)
                    done = PE.matmul(bank[:], wlo[s][:, wk], hi[:, k, :], start=False, stop=(k == last))
                return done

            def front_tile(ix):
                n, s, _ = ix
                pe.wait_ge(lo_ready, n + 1)
                pe.wait_ge(evacuated, n + 1)
                steps(s, dense[s], range(KD), 0, KD - 1).then_inc(tile_done, 1)

            lag = 4
            for k in range(KD + lag):
                for s, ks in ((1, k - lag), (0, k)):
                    if not 0 <= ks < KD:
                        continue
                    if ks == 0:
                        pe.wait_ge(lo_ready, s + 1)
                    if s == 0:
                        pe.wait_ge(h_lo_ready, ks + 1)
                    done = steps(s, dense[s], [ks], 0, KD - 1)
                    if ks == KD - 1:
                        done.then_inc(tile_done, 1)
            pe.wait_ge(cst_loaded, 16)
            for j in range(2):
                pe.wait_ge(sq_used[j], KD // 2)
                done = PE.matmul(R[0][:], ones, sqsum[j][:], start=(j == 0), stop=(j == 1))
            done.then_inc(ss_done, 1)
            for n in range(2, ATT_TILES):
                front_tile(index(0, 2, n))

            pe.wait_ge(zeroed, 2)
            for g in range(STAGES):
                def next_tile(tile, k):
                    n, s, _ = index(0, 2, FILL_TILE0[g] + tile)
                    if k == 0:
                        pe.wait_ge(lo_ready, n + 1)
                        pe.wait_ge(evacuated, n + 1)
                    done = steps(s, dense[s], [k], 0, KD - 1)
                    if k == KD - 1:
                        done.then_inc(tile_done, 1)

                fill = Fill(next_tile, ATT_FILL[g])

                def scores(w):
                    e, b = w // NB, w % NB
                    pe.wait_ge(pv_read, g * UNITS + w + 1)
                    rows = slice(e * HD, e * HD + HD)
                    for h in range(GROUP):
                        done = PE.matmul(
                            R[1 + 2 * (w % 2) + h // 2][:, (h % 2) * 2 * BLOCK:(h % 2 + 1) * 2 * BLOCK],
                            qT[g][rows, h, b * BLOCK:(b + 1) * BLOCK],
                            kT[g][rows, b * BLOCK:(b + 2) * BLOCK], start=True, stop=True)
                    done.then_inc(scores_done, 1)

                pe.wait_ge(evacuated, (g + 1) * ATT_TILES + 2)
                scores(0)
                pe.wait_ge(pt_read, g * UNITS + 1)
                for t in range(NB):
                    done = PE.transpose(R[0][:, t * P:(t + 1) * P], vT[g][:, t * P:(t + 1) * P], ident)
                done.then_inc(vt_done, 1)
                for w in range(UNITS):
                    e, b = w // NB, w % NB
                    W = g * UNITS + w
                    if w + 1 < UNITS:
                        scores(w + 1)
                    fill("scores")
                    pe.wait_ge(probs_ready, W + 1)
                    pe.wait_ge(pt_read, W + 1)
                    if w == 0:
                        pe.wait_ge(vtok_ready, g + 1)
                    for half, bank in enumerate((R[5], R[0])):
                        for h in range(GROUP):
                            done = PE.transpose(bank[:, h * BLOCK:(h + 1) * BLOCK],
                                                probs[w % 2][:, h, half * BLOCK:(half + 1) * BLOCK],
                                                ident)
                    done.then_inc(pt_done, 1)
                    fill("probs")
                    pe.wait_ge(pt_read, W + 2)
                    cols = slice(e * HD, e * HD + HD)
                    for half in range(2):
                        done = PE.matmul(R[1 + 2 * (w % 2)][cols, :], vtok[g][:, b + half, cols],
                                         pT[:, half, :], start=(half == 0), stop=(half == 1))
                    done.then_inc(pv_done, 1)

            with pe.Fori(0, PAIRS // 2) as i:
                for u in range(2):
                    p = i * 2 + u
                    heads = [slice(e * HD, e * HD + HD) for e in range(2)]

                    def tile_ix(j):
                        return index(i, 2 * RW_TILES, RW0 + u * RW_TILES + j)

                    def gate_step(tile, k):
                        n, s, _ = tile_ix(3 + tile)
                        if k == 0:
                            pe.wait_ge(lo_ready, n + 1)
                            pe.wait_ge(evacuated, n + 1)
                        done = steps(s, dense[s], [k], 0, KD - 1)
                        if k == KD - 1:
                            done.then_inc(tile_done, 1)

                    fill = Fill(gate_step)
                    front_tile(tile_ix(0))
                    pe.wait_ge(low_ready, 1)
                    pe.wait_ge(pv_read, 2 + STAGES * UNITS)
                    pe.wait_ge(ups_loaded[u], i * 16 + 16)
                    pe.wait_ge(cen_read, p + 1)
                    pe.wait_ge(var_read, p + 1)
                    up = ups[u]
                    PE.matmul(R[0][:], up[0:64, 0, :], low[0][0:64, :], start=True, stop=True)
                    PE.matmul(R[1][:], up[64:128, 0, :], low[0][64:128, :], start=True, stop=True)
                    PE.matmul(R[2][:], up[:, 1, :], low[1][:], start=True, stop=False)
                    rest = GATE_RANK - P
                    PE.matmul(R[2][:], up[0:rest, 2, :], low[2][0:rest, :], start=False, stop=True
                              ).then_inc(ups_done, 1)
                    front_tile(tile_ix(1))
                    pe.wait_ge(ksq_ready, p + 1)
                    PE.matmul(R[3][:], head_ones, tmp1[:], start=True, stop=True).then_inc(kn_done, 1)
                    front_tile(tile_ix(2))
                    fill("prep")
                    pe.wait_ge(prep_ready, p + 1)
                    PE.matmul(R[3][:], head_ones, tmp2[:], start=True, stop=True).then_inc(bonus_done, 1)
                    for bank, src in ((R[1], icl), (R[2], kap), (R[0], vbuf)):
                        if src is vbuf:
                            pe.wait_ge(shifted, p * 3 + N_LOW + 3)
                        for t in range(NB):
                            done = PE.transpose(bank[:, t * P:(t + 1) * P], src[:, t * P:(t + 1) * P],
                                                ident)
                        done.then_inc(tok_done, 1)
                    fill("tok")
                    pe.wait_ge(bonus_read, p + 1)
                    pe.wait_ge(tok_read, p * 3 + 3)
                    for t in range(NB):
                        for e in range(2):
                            w = 2 * t + e
                            bank = ((R[3], R[4]), (R[5], R[0]))[e][t % 2]
                            if w >= 4:
                                pe.wait_ge(g_read, p * (2 * NB) + w - 3)
                            tok = slice(t * P, (t + 1) * P)
                            both = zq[heads[e], t].rearrange("p a n -> p (a n)")
                            PE.matmul(bank[:, 0:2 * P], icl[heads[e], tok], both, start=True, stop=True)
                            PE.matmul(bank[:, 2 * P:4 * P], kap[heads[e], tok], both,
                                      start=True, stop=True).then_inc(g_done, 1)
                    for e in range(2):
                        for t in range(NB):
                            tok = slice(t * P, (t + 1) * P)
                            done = PE.matmul(R[1 + e][:, tok], zq[heads[e], t, 0, :], icl[heads[e], tok],
                                             start=True, stop=True)
                        done.then_inc(ln_done, 1)
                    fill("solve")
                    pe.wait_ge(g_read, (p + 1) * (2 * NB))
                    pe.wait_ge(ln_read, p * 2 + 2)
                    for t in range(NB):
                        for e in range(2):
                            done = PE.matmul(R[1][:, t * P + e * HD:t * P + e * HD + HD],
                                             lq[:, e, t, 1, :], vtk[:, t, heads[e]],
                                             start=True, stop=True)
                    done.then_inc(lv_done, 1)
                    for level in range(LEVELS):
                        done_l = p * (2 * LEVELS) + 2 * level
                        for e in range(2):
                            if level:
                                pe.wait_ge(p2_read, done_l - 2 + e + 1)
                            for t in range(NB):
                                done = PE.transpose(RA[e][:, t * P:(t + 1) * P], Y[:, e, t, :], ident)
                            done.then_inc(x_done, 1)
                            for t in range(NB):
                                done = PE.matmul(RB[e][:, t * HALF:(t + 1) * HALF], Ln[:, e, t, :],
                                                 second_halves(Y[:, e, t, :], level),
                                                 start=True, stop=True)
                            done.then_inc(w1_done, 1)
                        fill("level_a")
                        for e in range(2):
                            pe.wait_ge(x_read, done_l + e + 1)
                            pe.wait_ge(w1_read, done_l + e + 1)
                            for t in range(NB):
                                done = PE.matmul(RA[e][:, t * HALF:(t + 1) * HALF], Xi[:, e, t, :],
                                                 W1[:, e, t, :], start=True, stop=True)
                            done.then_inc(p2_done, 1)
                        fill("level_b")
                    pe.wait_ge(p2_read, (p + 1) * (2 * LEVELS))
                    for n in range(CHUNKS):
                        t, lo = n // 2, CHUNK * (n % 2)
                        here = slice(lo, lo + CHUNK)
                        pe.wait_ge(s_ready, p * CHUNKS + n + 1)
                        PE.matmul(R[2][:, 0:P], zq[:, t, 0, :], S[:], start=True, stop=True
                                  ).then_inc(m1_done, 1)
                        PE.matmul(R[5][:, t * P + lo:t * P + lo + CHUNK], S[:], zq[:, t, 1, here],
                                  start=(n % 2 == 0), stop=False, skip_group_check=True)
                        fill("rhs")
                        pe.wait_ge(rhs_ready, p * CHUNKS + n + 1)
                        for e in range(2):
                            done = PE.matmul(R[3][:, heads[e]], Y[:, e, t, :], rhs[:, t, heads[e]],
                                             start=True, stop=True)
                        done.then_inc(m2_done, 1)
                        fill("u")
                        pe.wait_ge(u_ready, p * CHUNKS + n + 1)
                        if n + 1 < CHUNKS:
                            PE.matmul(R[4][:, 0:P], btok[here, t, :], utok[here, t, :],
                                      start=True, stop=False)
                            PE.matmul(R[4][:, 0:P], ktok[here, t, :], vtk[here, t, :],
                                      start=False, stop=True).then_inc(m3_done, 1)
                        if n % 2:
                            for e in range(2):
                                dst = R[5][heads[e], t * P:(t + 1) * P]
                                PE.matmul(dst, utok[:, t, heads[e]], lq[:, e, t, 0, :],
                                          start=False, stop=False, skip_group_check=True)
                                done = PE.matmul(dst, vtk[:, t, heads[e]], lq[:, e, t, 2, :],
                                                 start=False, stop=True, skip_group_check=True)
                            if n + 1 == CHUNKS:
                                done.then_inc(y_done, 1)
                        fill("state")
                    fill("y")
                    pe.wait_ge(y_ready, p + 1)
                    PE.matmul(R[0][:], head_center, csum[:], start=True, stop=True).then_inc(cen_done, 1)
                    fill("center")
                    pe.wait_ge(cen_read, p + 2)
                    PE.matmul(R[1][:], head_mean, tmp1[:], start=True, stop=True).then_inc(var_done, 1)

            pe.wait_ge(evacuated, MERGE0 + 2)
            pe.wait_ge(cen_read, PAIRS + 1)
            pe.wait_ge(var_read, PAIRS + 1)

            def merge_tile(i, u, first):
                n, s, _ = index(i, 2, MERGE0 + u)
                a_bank, b_bank = (dense[1], dense[0]) if u == 0 else (R[0], R[1])
                pe.wait_ge(lo_ready, n + 1)
                if not first:
                    pe.wait_ge(merge_read, n - MERGE0 - 1)
                for half, bank, flag in ((0, a_bank, attn_half), (1, b_bank, tile_done)):
                    ks = range(half * PAIRS, (half + 1) * PAIRS)
                    for k in ks:
                        if first and k % 2 == 0:
                            pe.wait_ge(yb_lo, k // 2 + 1)
                        done = steps(s, bank, [k], ks[0], ks[-1])
                    done.then_inc(flag, 1)

            for u in range(2):
                merge_tile(0, u, True)
            with pe.Fori(1, KD // 2) as i:
                for u in range(2):
                    merge_tile(i, u, False)

            def later_tile(ix, ks=KD, hi=H_hi, lo=H_lo):
                n, s, _ = ix
                pe.wait_ge(lo_ready, n + 1)
                pe.wait_ge(bank_read, n - OUT0 + 1)
                steps(s, dense[s], range(ks), 0, ks - 1, hi, lo).then_inc(tile_done, 1)

            pe.wait_ge(m_lo_ready, KD)
            with pe.Fori(0, KD // 2) as i:
                for u in range(2):
                    later_tile(index(i, 2, OUT0 + u), KD, M_hi, M_lo)
            pe.wait_ge(x2_lo, KD)
            PE.matmul(R[2][:], ones, sqacc[:], start=True, stop=True).then_inc(ss2_done, 1)
            with pe.Fori(0, GROUPS_F) as g:
                with pe.Fori(0, FG) as t:
                    for u in range(2):
                        later_tile(ffn_index(g, t, u))
                for u in range(2):
                    n, s, _ = ffn_index(g, 0, 2 * FG + u)
                    if u == 0:
                        pe.wait_ge(lo_ready, n + 1)
                        pe.wait_ge(bank_read, n - OUT0 + 1)
                        steps(s, dense[s], range(FG - 1), 0, FG - 1, G_hi, G_lo)
                        pe.wait_ge(g_lo_ready, g * FG + FG)
                        steps(s, dense[s], [FG - 1], 0, FG - 1, G_hi, G_lo).then_inc(tile_done, 1)
                    else:
                        later_tile((n, s, None), FG, G_hi, G_lo)
                with pe.Fori(1, KD // 2) as i:
                    for u in range(2):
                        later_tile(ffn_index(g, i, 2 * FG + u), FG, G_hi, G_lo)
            pe.wait_ge(acc_ready, 2 * KD + 1)
            PE.matmul(R[2][:], ones, facc[:], start=True, stop=True).then_inc(ss2_done, 1)


def _tiles(w):
    k, n = w.shape
    return np.ascontiguousarray(w.reshape(k // P, P, n // P, P).transpose(2, 1, 0, 3)).reshape(n // P, P, k)


def _shape_constants():
    i = np.arange(P)
    eye = np.eye(P, dtype=np.float32)
    head = (i[:, None] // HD == i[None, :] // HD).astype(np.float32)
    consts = np.stack([eye, np.ones((P, P), np.float32), head, head / HD, eye - head / HD], 1)
    s, t = i[:, None], i[None, :]
    same = s // CHUNK == t // CHUNK
    lq_mask = np.stack([same & (t >= s), same & (t > s), same & (t >= s)], 1).astype(np.float32)
    scan = np.broadcast_to((np.arange(T_SEQ) % CHUNK != 0).astype(np.float32), (P, T_SEQ))
    scan_lq = np.concatenate([scan, lq_mask.reshape(P, 3 * P)], 1)
    levels = []
    for l in range(LEVELS + 1):
        cols = t[:, (i >> l) % 2 == 1] if l else t
        levels.append((s // (2 << l) == cols // (2 << l)) & ((s >> l) % 2 == 0)
                      & ((cols >> l) % 2 == 1))
    levels = np.concatenate(levels, 1).astype(np.float32)
    q, k = np.arange(BLOCK)[:, None], np.arange(2 * BLOCK)[None, :]
    d = BLOCK + q - k
    valid = (d >= 0) & (d < BLOCK)
    masked = np.float32(-1e30)
    dist = np.stack([np.where(valid & (k >= BLOCK), -d, masked), np.where(valid, -d, masked)], 1)
    slopes = np.broadcast_to(2.0 ** (-8.0 * np.arange(1, HEADS + 1) / HEADS), (P, HEADS))
    att = np.concatenate([dist.reshape(P, -1), slopes], 1).astype(np.float32)
    return consts, np.ascontiguousarray(scan_lq), levels, np.ascontiguousarray(att)


def kernel(**inputs):
    import concourse.bacc as _bacc
    from concourse.bass_utils import run_bass_kernel_spmd as _run

    a = {k: np.asarray(v) for k, v in inputs.items()}
    w_in = a["w_in"][0]
    at = np.cumsum([0, WIDTH, KV_WIDTH, KV_WIDTH, WIDTH, WIDTH, WIDTH, DECAY_RANK, ICLR_RANK,
                    GATE_RANK, D_MODEL, D_MODEL])
    wq, wk, wv, wr, wrk, wrv, wdw, wda, wdg, wga, wgb = (
        w_in[:, at[j]:at[j + 1]] for j in range(11))
    order = []
    for gp in range(KV_HEADS // 2):
        order += [wk[:, gp * P:(gp + 1) * P], wv[:, gp * P:(gp + 1) * P]]
        for h in range(GROUP):
            for e in range(2):
                head = (2 * gp + e) * GROUP + h
                order.append(wq[:, head * HD:(head + 1) * HD])
    order += [wdw, wda, wdg, np.zeros((D_MODEL, 2 * P - GATE_RANK), np.float32)]
    for p in range(PAIRS):
        c = slice(p * P, (p + 1) * P)
        order += [wrk[:, c], wr[:, c], wrv[:, c]]
        for m in (2 * p, 2 * p + 1):
            order += [wga[:, m * P:(m + 1) * P], wgb[:, m * P:(m + 1) * P]]
    w_front = _tiles(np.concatenate(order, 1))

    gate_up = np.concatenate([a["gate_up"][0], np.zeros((2 * P - GATE_RANK, WIDTH), np.float32)], 0)
    ups = np.concatenate([a["decay_up"][0], a["iclr_up"][0], gate_up], 0)
    w_ups = np.ascontiguousarray(ups.reshape(3, P, PAIRS, P).transpose(2, 1, 0, 3))

    wba = a["w_branch_attn"][0].reshape(KV_HEADS // 2, 2, GROUP, HD, D_MODEL).transpose(0, 2, 1, 3, 4)
    w_branch = _tiles(np.concatenate([wba.reshape(WIDTH, D_MODEL), a["w_branch_rwkv"][0]], 0))
    w_slots = np.concatenate([w_front, w_branch, _tiles(a["w_out"][0])], 0)
    gt, ut = _tiles(a["ffn_gate"][0]), _tiles(a["ffn_up"][0])
    w_gu = np.ascontiguousarray(np.stack([gt, ut], 1)).reshape(2 * gt.shape[0], P, SLOT)
    down = a["ffn_down"][0].reshape(GROUPS_F, DSLOT, D_MODEL)
    w_down = np.concatenate([_tiles(down[g]) for g in range(GROUPS_F)], 0)

    norms = np.ascontiguousarray(np.stack(
        [a["norm_mix"][0], a["norm_ffn"][0], a["norm_final"]], 0).reshape(3, KD, P).transpose(2, 0, 1))
    mu = a["tshift_mix"][0]
    mu_r, mu_k, mu_v, mu_low = mu[:WIDTH], mu[WIDTH:2 * WIDTH], mu[2 * WIDTH:3 * WIDTH], mu[3 * WIDTH:]
    pair_cst = np.stack([mu_k, mu_r, mu_v, a["decay_bias"][0], a["iclr_bias"][0], a["k_k"][0],
                         a["k_a"][0], a["r_k"][0].reshape(WIDTH), a["lnx_w"][0], a["lnx_b"][0]], 0)
    pair_cst = np.ascontiguousarray(pair_cst.reshape(NCST, PAIRS, P).transpose(2, 1, 0))
    low_mu = np.concatenate([mu_low, np.zeros(3 * P - mu_low.shape[0], np.float32)])
    low_mu = np.ascontiguousarray(low_mu.reshape(3, P).T)
    sinks = np.ascontiguousarray(np.broadcast_to(a["attn_sinks"][0], (P, HEADS)))
    consts, scan_lq, levels, att_cst = _shape_constants()

    arrays = {
        "xT": np.ascontiguousarray(a["x"][0].T).reshape(KD, P, T_SEQ), "w_slots": w_slots,
        "w_ups": w_ups, "w_gu": w_gu, "w_down": w_down,
        "norms": norms, "pair_cst": pair_cst, "low_mu": low_mu, "sinks": sinks, "consts": consts,
        "scan_lq": scan_lq, "level_masks": levels, "att_cst": att_cst}
    nc = _bacc.Bacc("TRN2", target_bir_lowering=False, num_devices=1)
    args = {n: nc.dram_tensor(n, v.shape, mybir.dt.from_np(v.dtype), kind="ExternalInput").ap()
            for n, v in arrays.items()}
    out = nc.dram_tensor("out", (KD, P, T_SEQ), mybir.dt.float32, kind="ExternalOutput").ap()
    build_layer(nc, out=out, **args)
    r = _run(nc, [arrays], core_ids=[0])
    return np.ascontiguousarray(r.results[0]["out"].reshape(D_MODEL, T_SEQ).T)[None]
```

```python
import math
from contextlib import ExitStack

import numpy as np
import concourse.bass as bass
from concourse import mybir

P = 128
D_MODEL, T_SEQ = 2048, 512
KD = D_MODEL // P
HEADS, HD = 16, 64
KV_HEADS = 4
GROUP = HEADS // KV_HEADS
WIDTH = HEADS * HD
KV_WIDTH = KV_HEADS * HD
PAIRS = WIDTH // P
BLOCK = 128
NB = T_SEQ // BLOCK
CHUNK = 64
CHUNKS = T_SEQ // CHUNK
LEVELS = 5
HALF = P // 2
LAMBDA = math.exp(-0.5)
DECAY_RANK, ICLR_RANK, GATE_RANK = 64, 64, 160
FFN_HIDDEN = -(-8 * D_MODEL // (3 * 256)) * 256
GROUPS_F = 4
FG = FFN_HIDDEN // P // GROUPS_F
NORM_EPS, LNX_EPS = 1e-5, 64e-5
OUT_PARTS = (1, 1, 2, 4, 4, 4)
assert sum(OUT_PARTS) == KD
SLOT = KD * P
DSLOT = FG * P

STAGES = KV_HEADS // 2
ATT_TILES = 2 + GROUP
LOW0 = STAGES * ATT_TILES
N_LOW = 3
RW0 = LOW0 + N_LOW
RW_TILES = 7
MERGE0 = RW0 + PAIRS * RW_TILES
OUT0 = MERGE0 + KD
FFN0 = OUT0 + KD
FGRP = 2 * FG + KD
C_MUK, C_MUR, C_MUV, C_DB, C_IB, C_KK, C_KA, C_RK, C_LW, C_LB = range(10)
NCST = 10

UNITS = 2 * NB
ATT_FILL = ({"first": 0, "scores": 6, "probs": 4, "out": 2},
            {"first": 8, "scores": 2, "probs": 1, "out": 2})
FILL_TILE0 = (ATT_TILES, LOW0, RW0)
for _g in range(STAGES):
    assert (UNITS * (sum(ATT_FILL[_g].values()) - ATT_FILL[_g]["first"]) + ATT_FILL[_g]["first"]
            == (FILL_TILE0[_g + 1] - FILL_TILE0[_g]) * KD)
FILL = {"prep": 2, "tok": 2, "solve": 2, "level_a": 2, "level_b": 1, "rhs": 2, "u": 2, "state": 1,
        "y": 1, "center": 2}
assert (FILL["prep"] + FILL["tok"] + FILL["solve"] + LEVELS * (FILL["level_a"] + FILL["level_b"])
        + CHUNKS * (FILL["rhs"] + FILL["u"] + FILL["state"]) + FILL["y"] + FILL["center"]) == 4 * KD


def index(i, per, off):
    return i * per + off, off % 2, i * (per // 2) + off // 2


def ffn_index(g, i, off):
    off += FFN0
    return g * FGRP + i * 2 + off, off % 2, g * (FGRP // 2) + i + off // 2


class Arena:

    def __init__(self, nc, at):
        self.nc, self.at = nc, at

    def __call__(self, name, shape, dt=mybir.dt.float32):
        size = int(np.prod(shape)) * (1 if dt == mybir.dt.uint8 else 4)
        t = self.nc.alloc_sbuf_tensor_at(name, [P] + list(shape), dt, offset=self.at)
        self.at += -(-size // 32) * 32
        return t


def build_layer(nc, xT, w_slots, w_ups, w_gu, w_down, norms, pair_cst, low_mu,
                sinks, consts, scan_lq, level_masks, att_cst, out):
    f32, f32r, u8 = mybir.dt.float32, mybir.dt.float32r, mybir.dt.uint8
    ALU, ACT = mybir.AluOpType, mybir.ActivationFunctionType
    AX = mybir.AxisListType.X
    MUL, ADD, SUB = ALU.mult, ALU.add, ALU.subtract
    V, A, PE = nc.vector, nc.scalar, nc.tensor

    gates_dram = nc.dram_tensor("gates_dram", (4 * PAIRS, P, T_SEQ), f32, kind="Internal").ap()
    y_dram = nc.dram_tensor("y_dram", (2 * PAIRS, P, T_SEQ), f32, kind="Internal").ap()
    x2_dram = nc.dram_tensor("x2_dram", (KD, P, T_SEQ), f32, kind="Internal").ap()

    keep = Arena(nc, -(-nc.sbuf_base // 64) * 64)
    raw = [keep(f"raw{s}", [SLOT]) for s in range(2)]
    whi = [keep(f"whi{s}", [SLOT], f32r) for s in range(2)]
    wlo = [keep(f"wlo{s}", [SLOT], f32r) for s in range(2)]
    H_hi = keep("H_hi", [KD, T_SEQ], f32r)
    H_lo = keep("H_lo", [KD, T_SEQ], f32r)
    cst = keep("cst", [5, P])
    ident, ones, head_ones, head_mean, head_center = (cst[:, i, :] for i in range(5))
    norm_g = keep("norm_g", [3, KD])

    front = Arena(nc, keep.at)
    low = [front(f"low{i}", [T_SEQ]) for i in range(3)]
    lowmu = front("lowmu", [3])
    rstd1 = front("rstd1", [T_SEQ])
    proj = front("proj", [T_SEQ + 1])
    tmp1 = front("tmp1", [T_SEQ])
    ups = [front(f"ups{i}", [3, P]) for i in range(2)]

    start = Arena(nc, front.at)
    X = start("X", [KD, T_SEQ])
    sq = [start(f"sq{i}", [T_SEQ]) for i in range(4)]
    sqsum = [start(f"sqsum{i}", [T_SEQ]) for i in range(2)]

    qkv = Arena(nc, front.at)
    qT = [qkv(f"qT{g}", [GROUP, T_SEQ]) for g in range(STAGES)]
    kT = [qkv(f"kT{g}", [T_SEQ]) for g in range(STAGES)]
    vT = [qkv(f"vT{g}", [T_SEQ]) for g in range(STAGES)]
    vtok = [qkv(f"vtok{g}", [NB, P]) for g in range(STAGES)]
    assert qkv.at <= start.at
    att = Arena(nc, start.at)
    probs = [att(f"probs{i}", [GROUP, 2 * BLOCK]) for i in range(2)]
    pT = att("pT", [2, T_SEQ])
    yatt = [att(f"yatt{g}", [GROUP, T_SEQ]) for g in range(STAGES)]
    att_const = att("att_const", [2 * BLOCK + HEADS])
    dist = att_const[:, 0:2 * BLOCK]
    slopes = att_const[:, 2 * BLOCK:2 * BLOCK + HEADS]
    sink = att("sink", [HEADS])
    rowmax, negmax, rowsum, sinkexp, rowinv = (
        [att(f"{n}{i}", [GROUP]) for i in range(2)]
        for n in ("rowmax", "negmax", "rowsum", "sinkexp", "rowinv"))

    rw = Arena(nc, front.at)
    scanlq = rw("scanlq", [T_SEQ + 3 * P])
    scan_mask = scanlq[:, 0:T_SEQ]
    lq_mask = scanlq[:, T_SEQ:T_SEQ + 3 * P]
    masks = rw("masks", [P + LEVELS * HALF], u8)
    cp_all = rw("cp_all", [PAIRS, NCST])
    cp = [rw(f"cp{i}", [NCST]) for i in range(2)]
    kbuf, rbuf, vbuf = (rw(n, [T_SEQ]) for n in ("kbuf", "rbuf", "vbuf"))
    grow, csum, a_in, icl = (rw(n, [T_SEQ]) for n in ("grow", "csum", "a_in", "icl"))
    kkbuf, kap, tmp2, gbuf, bonus = (
        rw(n, [T_SEQ]) for n in ("kkbuf", "kap", "tmp2", "gbuf", "bonus"))
    scratch_end = rw.at
    zq = rw("zq", [NB, 2, P])
    lq = rw("lq", [2, NB, 3, P])
    Lt = rw("Lt", [2, NB, P])
    Ln = rw("Ln", [2, NB, CHUNK])
    Y = rw("Y", [2, NB, P])
    masks_f32 = Y[:].rearrange("p e t n -> p (e t n)")[:, 0:P + LEVELS * HALF]
    Xc = Lt[:, 0]
    W1 = rw("W1", [NB, HALF])
    btok, ktok, vtk = (rw(n, [NB, P]) for n in ("btok", "ktok", "vtk"))
    lv, rhs, utok = (rw(n, [NB, P]) for n in ("lv", "rhs", "utok"))
    S, SA = rw("S", [P]), rw("SA", [P])
    gout = [rw(f"gout{i}", [T_SEQ]) for i in range(2)]

    back = Arena(nc, keep.at)
    M_hi, M_lo = back("M_hi", [KD, T_SEQ], f32r), back("M_lo", [KD, T_SEQ], f32r)
    late = Arena(nc, back.at)
    rstd = late("rstd", [T_SEQ])
    early = Arena(nc, scratch_end)
    ystage = early("ystage", [KD, T_SEQ])
    gin = [early(f"gin{i}", [2, T_SEQ]) for i in range(2)]
    mrg = [early(f"mrg{i}", [T_SEQ]) for i in range(2)]
    mtmp = early("mtmp", [T_SEQ])
    xin = [late(f"xin{i}", [T_SEQ]) for i in range(2)]
    x2 = [late(f"x2_{i}", [T_SEQ]) for i in range(2)]
    sqacc, sqx = late("sqacc", [T_SEQ]), late("sqx", [T_SEQ])

    ffn = Arena(nc, keep.at)
    resid = ffn("resid", [KD, T_SEQ])
    G_hi = ffn("G_hi", [FG, T_SEQ], f32r)
    gate_n, gate_s, hid = (ffn(n, [T_SEQ]) for n in ("gate_n", "gate_s", "hid"))
    merged_end = keep.at + 2 * KD * T_SEQ * 4
    fend = Arena(nc, merged_end + T_SEQ * 4)
    G_lo = fend("G_lo", [FG, T_SEQ], f32r)
    facc, fsq = fend("facc", [T_SEQ]), fend("fsq", [T_SEQ])
    assert ffn.at <= merged_end
    assert max(rw.at, att.at, early.at, late.at, fend.at) <= nc.sbuf_usable_end

    with ExitStack() as ctx:
        def sem(name):
            return ctx.enter_context(nc.semaphore(name))

        dense = [ctx.enter_context(nc.psum_tensor(f"dense{i}", [P, T_SEQ], f32)) for i in range(2)]
        R = [ctx.enter_context(nc.psum_tensor(f"work{i}", [P, T_SEQ], f32)) for i in range(6)]
        RX, RW, RP = (R[3], R[2]), R[4], (R[5], R[0])
        RL = (R[2], R[0])

        raw_loaded = [sem(f"raw_loaded{s}") for s in range(2)]
        hi_ready, lo_ready = sem("hi_ready"), sem("lo_ready")
        tile_done = sem("tile_done")
        evacuated = sem("evacuated")
        cst_loaded, att_loaded, rw_loaded = sem("cst_loaded"), sem("att_loaded"), sem("rw_loaded")
        norms_loaded = sem("norms_loaded")
        x_loaded = [sem(f"x_loaded{g}") for g in range(KD // 2)]
        sq_ready, ss_done = sem("sq_ready"), sem("ss_done")
        sq_used = [sem("sq_used_even"), sem("sq_used_odd")]
        ms_ready, rms_ready = sem("ms_ready"), sem("rms_ready")
        h_hi_ready, h_lo_ready = sem("h_hi_ready"), sem("h_lo_ready")
        low_ready, shifted = sem("low_ready"), sem("shifted")
        vt_done, vtok_ready = sem("vt_done"), sem("vtok_ready")
        scores_done, stats_ready, exp_done = sem("scores_done"), sem("stats_ready"), sem("exp_done")
        probs_ready, pt_done, pt_read = sem("probs_ready"), sem("pt_done"), sem("pt_read")
        pv_done, pv_read = sem("pv_done"), sem("pv_read")
        yatt_stored = sem("yatt_stored")
        ups_loaded = [sem(f"ups_loaded{s}") for s in range(2)]
        cp_ready, ups_done, up_read = sem("cp_ready"), sem("ups_done"), sem("up_read")
        cum_ready, exps_ready = sem("cum_ready"), sem("exps_ready")
        ksq_ready, kn_done, kn_read, kn_root = (
            sem("ksq_ready"), sem("kn_done"), sem("kn_read"), sem("kn_root"))
        prep_ready, bonus_done, bonus_read = sem("prep_ready"), sem("bonus_done"), sem("bonus_read")
        tok_done, tok_read, g_done, g_read = (
            sem("tok_done"), sem("tok_read"), sem("g_done"), sem("g_read"))
        xb_read = sem("xb_read")
        l_read = sem("l_read")
        ln_done, ln_read, lv_done, lv_read = (
            sem("ln_done"), sem("ln_read"), sem("lv_done"), sem("lv_read"))
        x_done, x_read, w1_done, w1_read = (
            sem("x_done"), sem("x_read"), sem("w1_done"), sem("w1_read"))
        p2_done, p2_seen, p2_read = sem("p2_done"), sem("p2_seen"), sem("p2_read")
        m1_done, rhs_ready, m2_done, u_ready = (
            sem("m1_done"), sem("rhs_ready"), sem("m2_done"), sem("u_ready"))
        m3_done, s_ready, sa_ready = sem("m3_done"), sem("s_ready"), sem("sa_ready")
        y_done, y_ready = sem("y_done"), sem("y_ready")
        cen_done, cen_read = sem("cen_done"), sem("cen_read")
        var_done, var_read, var_root = sem("var_done"), sem("var_read"), sem("var_root")
        y_fin, y_stored = sem("y_fin"), sem("y_stored")
        gate_ready, gate_stored = sem("gate_ready"), [sem(f"gate_stored{s}") for s in range(2)]
        ystage_loaded = [sem(f"ystage_loaded{h}") for h in range(PAIRS)]
        yb_hi, attn_lo, rwkv_lo = sem("yb_hi"), sem("attn_lo"), sem("rwkv_lo")
        gin_loaded = [sem(f"gin_loaded{s}") for s in range(2)]
        attn_half, merge_read = sem("attn_half"), sem("merge_read")
        mrg_ready, m_hi_ready, m_lo_ready = sem("mrg_ready"), sem("m_hi_ready"), sem("m_lo_ready")
        xin_loaded = [sem(f"xin_loaded{s}") for s in range(2)]
        bank_read = sem("bank_read")
        x2_ready, x2sq_ready, x2_hi, x2_lo, acc_ready = (
            sem("x2_ready"), sem("x2sq_ready"), sem("x2_hi"), sem("x2_lo"), sem("acc_ready"))
        x2_stored = [sem(f"x2_stored{s}") for s in range(2)]
        ss2_done, ms2_ready, rms2_ready = sem("ss2_done"), sem("ms2_ready"), sem("rms2_ready")
        resid_loaded = sem("resid_loaded")
        gate_n_ready, silu_ready, hid_ready, g_hi_ready, g_lo_ready = (
            sem("gate_n_ready"), sem("silu_ready"), sem("hid_ready"), sem("g_hi_ready"),
            sem("g_lo_ready"))
        fin_ready, fsq_ready, out_ready, out_stored = (
            sem("fin_ready"), sem("fsq_ready"), sem("out_ready"), sem("out_stored"))

        heads = [slice(e * HD, e * HD + HD) for e in range(2)]
        assert HD == CHUNK

        def first_key(b):
            return 0 if b else BLOCK

        def g_bank(w):
            return ((R[3], R[4]), (R[5], R[0]))[w % 2][w // 2 % 2]

        def by_block(ap):
            return ap.rearrange("p (t n) -> p t n", t=NB)

        def of_head(bank, e):
            return bank[0:CHUNK, e * NB * CHUNK:(e + 1) * NB * CHUNK].rearrange(
                "p (t n) -> p t n", t=NB)

        def R_half(bank):
            return bank[:, 0:NB * HALF].rearrange("p (t n) -> p t n", t=NB)

        def second_halves(ap, level):
            dims = "p t" if len(ap.shape) == 3 else "p"
            split = ap.rearrange(f"{dims} (g two n) -> {dims} g two n", two=2, n=2 << level)
            return split[:, :, :, 1, :] if len(ap.shape) == 3 else split[:, :, 1, :]

        def wide(ap, n):
            return ap.unsqueeze(1).to_broadcast([P, n, ap.shape[-1]])

        def tile_of(buf, m):
            return buf[:, m, :] if isinstance(m, int) else buf[:, bass.ds(m, 1), :].rearrange(
                "p a n -> p (a n)")

        class Fill:

            def __init__(self, step, counts=FILL):
                self.pos, self.step, self.counts = 0, step, counts

            def __call__(self, place):
                for _ in range(self.counts[place]):
                    self.step(self.pos // KD, self.pos % KD)
                    self.pos += 1

        block = ctx.enter_context(nc.Block())

        @block.sync
        def _(sp):
            def load(ix, src=None, cols=SLOT):
                n, s, _ = ix
                src = w_slots[n] if src is None else src
                if not (isinstance(n, int) and n < 2):
                    sp.wait_ge(lo_ready, n - 1)
                sp.dma_start(raw[s][:, 0:cols], src).then_inc(raw_loaded[s], 16)

            sp.dma_start(norm_g[:], norms).then_inc(norms_loaded, 16)
            for g in range(KD // 2):
                if g == 1:
                    load(index(0, 2, 0))
                    load(index(0, 2, 1))
                sp.dma_start(X[:, 2 * g:2 * g + 2, :],
                             xT[2 * g:2 * g + 2].rearrange("k p t -> p k t")).then_inc(x_loaded[g], 16)
            sp.dma_start(cst[:], consts).then_inc(cst_loaded, 16)
            load(index(0, 2, 2))
            sp.dma_start(lowmu[:], low_mu).then_inc(att_loaded, 16)
            sp.dma_start(att_const[:], att_cst).then_inc(att_loaded, 16)
            sp.dma_start(sink[:], sinks).then_inc(att_loaded, 16)
            for n in range(3, RW0 + 2):
                load(index(0, 2, n))

            sp.wait_ge(pv_read, 2 + STAGES * UNITS)
            sp.wait_ge(yatt_stored, 16 * STAGES)
            sp.dma_start(scanlq[:], scan_lq).then_inc(rw_loaded, 16)
            sp.dma_start(masks_f32, level_masks).then_inc(rw_loaded, 16)
            sp.dma_start(cp_all[:], pair_cst).then_inc(rw_loaded, 16)
            def load_pair(i, u, store=True):
                p = i * 2 + u
                sp.wait_ge(ups_done, p + 1)
                sp.dma_start(ups[u % 2][:], w_ups[p]).then_inc(ups_loaded[u % 2], 16)
                for j in range(RW_TILES):
                    load(index(i, 2 * RW_TILES, RW0 + 2 + u * RW_TILES + j))
                    if j == 0 and store:
                        sp.wait_ge(y_fin, p)
                        sp.dma_start(y_dram[p + PAIRS - 1], bonus[:]).then_inc(y_stored, 16)

            load_pair(0, 0, False)
            with sp.Fori(0, PAIRS // 2 - 1) as i:
                load_pair(i, 1)
                load_pair(i, 2)
            load_pair(PAIRS // 2 - 1, 1)

            sp.wait_ge(y_stored, 16 * PAIRS)
            sp.wait_ge(y_done, PAIRS)
            for h in range(PAIRS):
                end = min(2 * h + 2, KD - 1)
                sp.dma_start(ystage[:, 2 * h:end, :], y_dram[2 * h:end].rearrange("k p t -> p k t")
                             ).then_inc(ystage_loaded[h], 16)
            for s in range(2):
                sp.wait_ge(gate_stored[s], 16 * (2 * PAIRS + 1))
            for m in range(2):
                sp.dma_start(gin[m][:], gates_dram[2 * m:2 * m + 2].rearrange("k p t -> p k t")
                             ).then_inc(gin_loaded[m], 16)
            with sp.Fori(1, KD // 2) as i:
                for u in range(2):
                    m = i * 2 + u
                    load(index(i, 2, MERGE0 + u))
                    sp.wait_ge(merge_read, m - 1)
                    sp.dma_start(gin[u][:], gates_dram[bass.ds(m * 2, 2)].rearrange("k p t -> p k t")
                                 ).then_inc(gin_loaded[u], 16)

            for s in range(2):
                load(index(0, 2, OUT0 + s))
            sp.wait_ge(m_lo_ready, KD)
            for m in range(2):
                sp.dma_start(xin[m][:], xT[m]).then_inc(xin_loaded[m], 16)
            with sp.Fori(1, KD // 2) as i:
                for u in range(2):
                    m = i * 2 + u
                    load(index(i, 2, OUT0 + u))
                    sp.wait_ge(x2_ready, m - 1)
                    sp.dma_start(xin[u][:], xT[m]).then_inc(xin_loaded[u], 16)

            for s in range(2):
                load(ffn_index(0, 0, s), w_gu[s])
            for s in range(2):
                sp.wait_ge(x2_stored[s], 16 * (KD // 2 + 1))

            def load_down(g):
                with sp.Fori(0, KD // 2) as i:
                    for u in range(2):
                        load(ffn_index(g, i, 2 * FG + u), w_down[g * KD + i * 2 + u], DSLOT)

            for t in range(1, 5):
                for u in range(2):
                    load(ffn_index(0, t, u), w_gu[t * 2 + u])
                if t == 1:
                    sp.wait_ge(tile_done, FFN0)
                m = slice(4 * (t - 1), 4 * t)
                sp.dma_start(resid[:, m, :], x2_dram[m].rearrange("k p t -> p k t")
                             ).then_inc(resid_loaded, 16)
            with sp.Fori(5, FG) as t:
                for u in range(2):
                    load(ffn_index(0, t, u), w_gu[t * 2 + u])
            load_down(0)
            with sp.Fori(1, GROUPS_F) as g:
                with sp.Fori(0, FG) as t:
                    for u in range(2):
                        load(ffn_index(g, t, u), w_gu[g * (2 * FG) + t * 2 + u])
                load_down(g)

            m = 0
            for count in OUT_PARTS:
                sp.wait_ge(out_ready, m + count)
                sp.dma_start(out[m:m + count].rearrange("k p t -> p k t"), resid[:, m:m + count, :]
                             ).then_inc(out_stored, 16)
                m += count
            sp.wait_ge(out_stored, 16 * len(OUT_PARTS))

        @block.gpsimd
        def _(pool):
            def low_part(ix, cols=SLOT):
                n, s, _ = ix
                pool.wait_ge(hi_ready, n + 1)
                nc.gpsimd.tensor_tensor(wlo[s][:, 0:cols], raw[s][:, 0:cols],
                                        whi[s][:, 0:cols].bitcast(f32), SUB).then_inc(lo_ready, 1)

            pool.wait_ge(lo_ready, 1)
            low_part(index(0, 2, 1))
            nc.gpsimd.memset(sqsum[1][:], 0.0)
            for k in range(1, KD, 2):
                pool.wait_ge(sq_ready, k + 1)
                nc.gpsimd.drain()
                nc.gpsimd.tensor_tensor(sqsum[1][:], sqsum[1][:], sq[k % 4][:], ADD
                                        ).then_inc(sq_used[1], 1)
            low_part(index(0, 2, 2))
            with pool.Fori(1, MERGE0 // 2) as i:
                for u in range(2):
                    low_part(index(i, 2, 1 + u))
            assert MERGE0 % 2
            low_part(index(0, 2, MERGE0))
            low_part(index(0, 2, MERGE0 + 1))
            for k in range(PAIRS):
                pool.wait_ge(yb_hi, k + 1)
                nc.gpsimd.tensor_tensor(H_lo[:, k, :], ystage[:, k, :], H_hi[:, k, :].bitcast(f32), SUB
                                        ).then_inc(attn_lo, 1)
            with pool.Fori(1, (FFN0 - MERGE0) // 2) as i:
                for u in range(2):
                    low_part(index(i, 2, MERGE0 + u))
            with pool.Fori(0, GROUPS_F) as g:
                with pool.Fori(0, FG) as t:
                    for u in range(2):
                        low_part(ffn_index(g, t, u))
                with pool.Fori(0, KD // 2) as i:
                    for u in range(2):
                        low_part(ffn_index(g, i, 2 * FG + u), DSLOT)

        @block.scalar
        def _(act):
            act.sem_inc(evacuated, 2)
            act.sem_inc(pt_read, 1)
            act.sem_inc(pv_read, 2)
            act.sem_inc(cen_read, 1)
            act.sem_inc(y_stored, 16)
            for s in range(2):
                act.sem_inc(gate_stored[s], 16)
                act.sem_inc(x2_stored[s], 16)

            def copy(dst, src, scale=1.0):
                return A.activation(dst, src, ACT.Copy, scale=scale)

            def split(ix, cols=SLOT):
                n, s, h = ix
                act.wait_ge(raw_loaded[s], h * 16 + 16)
                if not (isinstance(n, int) and n < 2):
                    act.wait_ge(tile_done, n - 1)
                copy(whi[s][:, 0:cols], raw[s][:, 0:cols]).then_inc(hi_ready, 1)

            act.wait_ge(norms_loaded, 16)
            def hi_part(k):
                act.wait_ge(x_loaded[k // 2], 16)
                copy(H_hi[:, k, :], X[:, k, :], norm_g[:, 0, k:k + 1]).then_inc(h_hi_ready, 1)

            def square(k):
                if k >= 4:
                    act.wait_ge(sq_used[k % 2], k // 2 - 1)
                A.activation(sq[k % 4][:], X[:, k, :], ACT.Square).then_inc(sq_ready, 1)

            hi_part(0)
            hi_part(1)
            split(index(0, 2, 0))
            square(0)
            square(1)
            split(index(0, 2, 1))
            for k in range(2, KD):
                hi_part(k)
                square(k)

            act.wait_ge(tile_done, 1)
            copy(kT[0][:], dense[0][:]).then_inc(evacuated, 1)
            split(index(0, 2, 2))
            act.wait_ge(tile_done, 2)
            copy(vT[0][:], dense[1][:]).then_inc(evacuated, 1)
            act.wait_ge(ms_ready, 1)
            A.activation(rstd1[:], rstd1[:], ACT.Sqrt).then_inc(rms_ready, 1)
            for n in range(1, ATT_TILES):
                split(index(0, 2, n + 2))

            for g in range(STAGES):
                def next_tile(tile, k):
                    if k == KD - 1:
                        split(index(0, 2, FILL_TILE0[g] + tile + 2))

                fill = Fill(next_tile, ATT_FILL[g])

                def exps(w):
                    act.wait_ge(stats_ready, g * UNITS + w + 1)
                    for h in range(GROUP):
                        p_h = probs[w % 2][:, h, first_key(w % NB):2 * BLOCK]
                        A.activation(p_h, p_h, ACT.Exp,
                                     bias=negmax[w % 2][:, h:h + 1],
                                     accum_out=rowsum[w % 2][:, h:h + 1])
                    A.activation(sinkexp[w % 2][:], sinkexp[w % 2][:], ACT.Exp).then_inc(exp_done, 1)

                act.wait_ge(vt_done, g + 1)
                copy(vtok[g][:], by_block(R[0][:])).then_inc(vtok_ready, 1)
                exps(0)
                fill("first")
                for w in range(UNITS):
                    e, b = w // NB, w % NB
                    W = g * UNITS + w
                    fill("scores")
                    act.wait_ge(pt_done, W + 3)
                    act.wait_ge(pv_done, W + 1)
                    if b:
                        copy(pT[:, 0, :], R[5][:])
                    copy(pT[:, 1, :], R[0][:]).then_inc(pt_read, 1)
                    if w + 1 < UNITS:
                        exps(w + 1)
                    fill("probs")
                    act.wait_ge(pv_done, W + 2)
                    copy(yatt[g][e * HD:e * HD + HD, :, b * BLOCK:(b + 1) * BLOCK],
                         R[1 + 2 * (w % 2)][e * HD:e * HD + HD, :].rearrange(
                             "p (h t) -> p h t", h=GROUP)).then_inc(pv_read, 1)
                    fill("out")
                act.wait_ge(pv_read, (g + 1) * UNITS + 2)
                act.dma_start(y_dram[g * GROUP:(g + 1) * GROUP].rearrange("k p t -> p k t"),
                              yatt[g][:]).then_inc(yatt_stored, 16)

            act.wait_ge(shifted, N_LOW)
            A.activation(low[0][0:DECAY_RANK, :], low[0][0:DECAY_RANK, :], ACT.Tanh)
            A.activation(low[1][:], low[1][:], ACT.Sigmoid)
            A.activation(low[2][:], low[2][:], ACT.Sigmoid).then_inc(low_ready, 1)

            act.wait_ge(rw_loaded, 48)
            with act.Fori(0, PAIRS // 2) as i:
                for u in range(2):
                    p = i * 2 + u
                    c = cp[u]

                    def front_tile(j):
                        split(index(i, 2 * RW_TILES, RW0 + u * RW_TILES + j + 2))

                    def gate_step(tile, k):
                        if k < KD - 1:
                            return
                        n, s, _ = index(i, 2 * RW_TILES, RW0 + u * RW_TILES + 3 + tile)
                        split(index(i, 2 * RW_TILES, RW0 + u * RW_TILES + 3 + tile + 2))
                        act.wait_ge(evacuated, n + 3)
                        A.activation(gout[tile % 2][:], gout[tile % 2][:], ACT.Sigmoid
                                     ).then_inc(gate_ready, 1)
                        act.wait_ge(gate_ready, p * 4 + tile + 1)
                        act.dma_start(gates_dram[p * 4 + tile], gout[tile % 2][:]
                                      ).then_inc(gate_stored[tile % 2], 16)

                    fill = Fill(gate_step)
                    front_tile(0)
                    act.wait_ge(cp_ready, p + 1)
                    act.wait_ge(ups_done, p + 3)
                    A.activation(grow[:], R[0][:], ACT.Sigmoid, bias=c[:, C_DB:C_DB + 1]
                                 ).then_inc(up_read, 1)
                    A.activation(icl[:], R[1][:], ACT.Sigmoid, bias=c[:, C_IB:C_IB + 1]
                                 ).then_inc(up_read, 1)
                    copy(gbuf[:], R[2][:]).then_inc(up_read, 1)
                    act.wait_ge(cum_ready, p + 1)
                    A.activation(a_in[:], csum[:], ACT.Exp, scale=-LAMBDA)
                    A.activation(zq[:, :, 0, :], zq[:, :, 0, :], ACT.Exp, scale=-LAMBDA)
                    A.activation(grow[:], csum[:], ACT.Exp, scale=LAMBDA).then_inc(exps_ready, 1)
                    front_tile(1)
                    act.wait_ge(kn_read, p + 1)
                    A.activation(tmp1[:], tmp1[:], ACT.Sqrt).then_inc(kn_root, 1)
                    front_tile(2)
                    fill("prep")
                    for bank, dst, count in ((R[1], btok, 1), (R[2], ktok, 2), (R[0], vtk, 3)):
                        act.wait_ge(tok_done, p * 3 + count)
                        copy(dst[:], by_block(bank[:])).then_inc(tok_read, 1)
                    fill("tok")
                    for w in range(2 * NB):
                        act.wait_ge(g_read, p * (2 * NB) + w + 1)
                        copy(Lt[:, w % 2, w // 2, :], g_bank(w)[:, 0:P]).then_inc(l_read, 1)
                    fill("solve")
                    for e in range(2):
                        act.wait_ge(ln_done, p * 2 + e + 1)
                        for c in heads:
                            done = copy(Ln[c, e], by_block(RL[e][c, :])[:, :, c])
                        done.then_inc(ln_read, 1)
                    act.wait_ge(lv_done, p + 1)
                    copy(lv[:], by_block(R[1][:])).then_inc(lv_read, 1)
                    for level in range(LEVELS):
                        act.wait_ge(w1_done, p * LEVELS + level + 1)
                        copy(W1[:], R_half(RW)).then_inc(w1_read, 1)
                        act.wait_ge(x_done, p * LEVELS + level + 1)
                        for e in range(2):
                            done = copy(Xc[heads[e], :, heads[0]], of_head(RX[0], e))
                        done.then_inc(x_read, 1)
                        fill("level_a")
                        fill("level_b")
                    for n in range(CHUNKS):
                        t, lo = n // 2, CHUNK * (n % 2)
                        if n + 1 < CHUNKS:
                            end = n * CHUNK + CHUNK - 1
                            act.wait_ge(s_ready, p * CHUNKS + n + 1)
                            copy(SA[:], S[:], a_in[:, end:end + 1]).then_inc(sa_ready, 1)
                        act.wait_ge(m2_done, p * CHUNKS + n + 1)
                        copy(utok[lo:lo + CHUNK, t, :], R[3][lo:lo + CHUNK, 0:P]).then_inc(u_ready, 1)
                        if n:
                            fill("u")
                            fill("state")
                        fill("rhs")
                    fill("u")
                    fill("state")
                    act.wait_ge(y_done, p + 1)
                    copy(csum[:], R[5][:]).then_inc(y_ready, 1)
                    fill("y")
                    act.wait_ge(cen_done, p + 1)
                    copy(kkbuf[:], R[0][:])
                    A.activation(tmp1[:], R[0][:], ACT.Square).then_inc(cen_read, 1)
                    fill("center")
                    act.wait_ge(var_read, p + 2)
                    A.activation(tmp2[:], tmp2[:], ACT.Sqrt).then_inc(var_root, 1)

            act.wait_ge(tile_done, MERGE0)
            for k in range(KD - 1):
                act.wait_ge(ystage_loaded[k // 2], 16)
                copy(H_hi[:, k, :], ystage[:, k, :]).then_inc(yb_hi, 1)
            act.wait_ge(y_fin, PAIRS)
            copy(H_hi[:, KD - 1, :], bonus[:]).then_inc(yb_hi, 1)

            with act.Fori(0, KD // 2) as i:
                for u in range(2):
                    m = i * 2 + u
                    split(index(i, 2, MERGE0 + u + 2))
                    act.wait_ge(mrg_ready, m + 1)
                    copy(tile_of(M_hi, m), mrg[u][:]).then_inc(m_hi_ready, 1)

            with act.Fori(0, KD // 2) as i:
                for u in range(2):
                    m = i * 2 + u
                    split(index(i, 2, OUT0 + u + 2))
                    act.wait_ge(x2_ready, m + 1)
                    act.dma_start(x2_dram[m], x2[u][:]).then_inc(x2_stored[u], 16)
                    act.wait_ge(acc_ready, m + 1)
                    A.activation(sqx[:], x2[u][:], ACT.Square).then_inc(x2sq_ready, 1)
                    copy(tile_of(H_hi, m), x2[u][:], norm_g[:, 1, bass.ds(m, 1)]).then_inc(x2_hi, 1)
            act.wait_ge(ms2_ready, 1)
            A.activation(rstd[:], rstd[:], ACT.Sqrt).then_inc(rms2_ready, 1)

            def hidden(g, t, cols):
                for u in range(2):
                    if u == 1:
                        hn = g * FG + t
                        act.wait_ge(gate_n_ready, hn + 1)
                        A.activation(gate_s[:], gate_n[:], ACT.Silu).then_inc(silu_ready, 1)
                    split(ffn_index(g, t, u + 2), cols)
                    if u == 1:
                        act.wait_ge(hid_ready, hn + 1)
                        copy(tile_of(G_hi, t), hid[:]).then_inc(g_hi_ready, 1)

            def last_square(m):
                act.wait_ge(fin_ready, m + 1)
                act.wait_ge(acc_ready, m + KD + 1)
                A.activation(fsq[:], tile_of(resid, m), ACT.Square).then_inc(fsq_ready, 1)

            def hidden_tiles(g):
                with act.Fori(0, FG - 1) as t:
                    hidden(g, t, SLOT)
                hidden(g, FG - 1, DSLOT)

            with act.Fori(0, GROUPS_F - 1) as g:
                hidden_tiles(g)
                with act.Fori(0, KD // 2 - 1) as i:
                    for u in range(2):
                        split(ffn_index(g, i, 2 * FG + u + 2), DSLOT)
                for u in range(2):
                    split(ffn_index(g, 0, FGRP + u))
            hidden_tiles(GROUPS_F - 1)
            with act.Fori(0, KD // 2 - 1) as i:
                for u in range(2):
                    split(ffn_index(GROUPS_F - 1, i, 2 * FG + u + 2), DSLOT)
                    last_square(i * 2 + u)
            for m in (KD - 2, KD - 1):
                last_square(m)
            act.wait_ge(ms2_ready, 2)
            A.activation(rstd[:], rstd[:], ACT.Sqrt).then_inc(rms2_ready, 1)

        @block.vector
        def _(dve):
            dve.sem_inc(var_read, 1)
            dve.sem_inc(bank_read, 2)
            dve.sem_inc(acc_ready, 1)

            def fence():
                V.drain()

            V.memset(proj[:, 0:1], 0.0)

            dve.wait_ge(norms_loaded, 16)
            V.memset(sqsum[0][:], 0.0)
            for k in range(KD):
                dve.wait_ge(h_hi_ready, k + 1)
                V.scalar_tensor_tensor(H_lo[:, k, :], X[:, k, :], norm_g[:, 0, k:k + 1],
                                       H_hi[:, k, :].bitcast(f32), MUL, SUB).then_inc(h_lo_ready, 1)
                if k == 1:
                    dve.wait_ge(hi_ready, 1)
                    V.tensor_tensor(wlo[0][:], raw[0][:], whi[0][:].bitcast(f32), SUB
                                    ).then_inc(lo_ready, 1)
                if k % 2:
                    dve.wait_ge(sq_ready, k)
                    fence()
                    V.tensor_tensor(sqsum[0][:], sqsum[0][:], sq[(k - 1) % 4][:], ADD
                                    ).then_inc(sq_used[0], 1)
            dve.wait_ge(ss_done, 1)
            V.tensor_scalar(rstd1[:], R[0][:], 1.0 / D_MODEL, NORM_EPS, MUL, ADD).then_inc(ms_ready, 1)
            dve.wait_ge(rms_ready, 1)
            V.reciprocal(rstd1[:], rstd1[:])
            fence()
            dve.wait_ge(evacuated, 4)
            V.tensor_tensor(kT[0][:], kT[0][:], rstd1[:], MUL)
            V.tensor_tensor(vT[0][:], vT[0][:], rstd1[:], MUL)

            def evacuate(dst, n, s):
                dve.wait_ge(tile_done, n + 1)
                V.tensor_tensor(dst, rstd1[:], dense[s][:], MUL).then_inc(evacuated, 1)

            def evacuate_qkv(g, j):
                n = g * ATT_TILES + j
                if j == 0:
                    evacuate(kT[g][:], n, n % 2)
                elif j == 1:
                    evacuate(vT[g][:], n, n % 2)
                else:
                    dve.wait_ge(tile_done, n + 1)
                    V.scalar_tensor_tensor(qT[g][:, j - 2, :], dense[n % 2][:], HD ** -0.5, rstd1[:],
                                           MUL, MUL).then_inc(evacuated, 1)

            def shift(dst, mu, scratch=tmp1):
                fence()
                cur, prev = proj[:, 1:T_SEQ + 1], proj[:, 0:T_SEQ]
                V.tensor_tensor(scratch[:], prev, cur, SUB)
                fence()
                V.scalar_tensor_tensor(dst, scratch[:], mu, cur, MUL, ADD).then_inc(shifted, 1)

            for j in range(2, ATT_TILES):
                evacuate_qkv(0, j)

            dve.wait_ge(att_loaded, 48)
            for g in range(STAGES):
                def next_tile(tile, k):
                    if k < KD - 1:
                        return
                    if g + 1 < STAGES:
                        evacuate_qkv(g + 1, tile)
                    else:
                        evacuate(proj[:, 1:T_SEQ + 1], LOW0 + tile, tile % 2)
                        shift(low[tile][:], lowmu[:, tile:tile + 1])

                fill = Fill(next_tile, ATT_FILL[g])

                def stats(w):
                    e, b = w // NB, w % NB
                    W = g * UNITS + w
                    s = w % 2
                    head0 = (2 * g + e) * GROUP
                    dve.wait_ge(scores_done, W + 1)
                    dve.wait_ge(pt_done, W + 1)
                    k0 = first_key(b)
                    for h in range(GROUP):
                        V.scalar_tensor_tensor(
                            probs[s][:, h, k0:2 * BLOCK], dist[:, k0:2 * BLOCK],
                            slopes[:, head0 + h:head0 + h + 1],
                            R[1 + 2 * s + h // 2][:, (h % 2) * 2 * BLOCK + k0:(h % 2 + 1) * 2 * BLOCK],
                            MUL, ADD)
                    fence()
                    V.tensor_reduce(rowmax[s][:], probs[s][:, :, k0:2 * BLOCK], AX, ALU.max)
                    fence()
                    sinks_e = sink[:, head0:head0 + GROUP]
                    V.tensor_tensor(rowmax[s][:], rowmax[s][:], sinks_e, ALU.max)
                    fence()
                    V.tensor_scalar(negmax[s][:], rowmax[s][:], -1.0, None, MUL)
                    V.tensor_tensor(sinkexp[s][:], sinks_e, rowmax[s][:], SUB).then_inc(stats_ready, 1)

                def normalise(w):
                    s = w % 2
                    dve.wait_ge(exp_done, g * UNITS + w + 1)
                    V.tensor_tensor(rowsum[s][:], rowsum[s][:], sinkexp[s][:], ADD)
                    fence()
                    V.reciprocal(rowinv[s][:], rowsum[s][:])
                    fence()
                    k0 = first_key(w % NB)
                    for h in range(GROUP):
                        p_h = probs[s][:, h, k0:2 * BLOCK]
                        last = V.tensor_scalar(p_h, p_h,
                                               rowinv[s][:, h:h + 1], None, MUL)
                    last.then_inc(probs_ready, 1)

                stats(0)
                fill("first")
                for w in range(UNITS):
                    normalise(w)
                    if w + 1 < UNITS:
                        stats(w + 1)
                    for place in ("scores", "probs", "out"):
                        fill(place)

            dve.wait_ge(rw_loaded, 48)
            V.tensor_copy(masks[:], masks_f32)
            V.memset(rhs[:], 0.0)
            V.memset(utok[:], 0.0)
            fence()
            with dve.Fori(0, PAIRS // 2) as i:
                for u in range(2):
                    p = i * 2 + u
                    n0 = i * (2 * RW_TILES) + RW0 + u * RW_TILES
                    c = cp[u]
                    col = lambda k: c[:, k:k + 1]
                    s0 = (RW0 + u * RW_TILES) % 2

                    def gate_step(tile, k):
                        if k < KD - 1:
                            return
                        dve.wait_ge(gate_stored[tile % 2], (p * 2 + tile // 2) * 16 + 16)
                        evacuate(gout[tile % 2][:], n0 + 3 + tile, (s0 + 3 + tile) % 2)

                    fill = Fill(gate_step)
                    zn, q = zq[:, :, 0, :], zq[:, :, 1, :]

                    V.tensor_copy(c[:], tile_of(cp_all, p))
                    V.drain().then_inc(cp_ready, 1)
                    evacuate(proj[:, 1:T_SEQ + 1], n0, s0)
                    shift(kbuf[:], col(C_MUK))
                    fence()
                    V.tensor_scalar(kkbuf[:], kbuf[:], col(C_KK), None, MUL)
                    fence()
                    V.tensor_tensor(tmp1[:], kkbuf[:], kkbuf[:], MUL).then_inc(ksq_ready, 1)
                    dve.wait_ge(up_read, p * 3 + 3)
                    V.tensor_tensor_scan(csum[:], scan_mask, grow[:], 0.0, MUL, ADD)
                    fence()
                    V.tensor_tensor(zn, by_block(csum[:]), by_block(grow[:]), SUB).then_inc(cum_ready, 1)
                    V.tensor_scalar(tmp2[:], icl[:], 1.0, col(C_KA), SUB, MUL)
                    fence()
                    V.scalar_tensor_tensor(kbuf[:], tmp2[:], 1.0, kbuf[:], ADD, MUL)
                    fence()
                    dve.wait_ge(exps_ready, p + 1)
                    V.tensor_tensor(kap[:], kbuf[:], grow[:], MUL)
                    evacuate(proj[:, 1:T_SEQ + 1], n0 + 1, 1 - s0)
                    shift(rbuf[:], col(C_MUR), csum)
                    dve.wait_ge(kn_done, p + 1)
                    V.tensor_scalar(tmp1[:], R[3][:], 1e-24, None, ALU.max).then_inc(kn_read, 1)
                    fence()
                    V.tensor_tensor(q, by_block(rbuf[:]), by_block(a_in[:]), MUL)
                    V.scalar_tensor_tensor(tmp2[:], rbuf[:], col(C_RK), kbuf[:], MUL, MUL)
                    dve.wait_ge(kn_root, p + 1)
                    V.reciprocal(tmp1[:], tmp1[:])
                    fence()
                    V.scalar_tensor_tensor(kkbuf[:], kkbuf[:], -1.0, tmp1[:], MUL, MUL)
                    fence()
                    V.tensor_tensor(zn, zn, by_block(kkbuf[:]), MUL)
                    V.scalar_tensor_tensor(tmp1[:], icl[:], -1.0, kkbuf[:], MUL, MUL)
                    fence()
                    V.tensor_tensor(icl[:], tmp1[:], grow[:], MUL).then_inc(prep_ready, 1)
                    evacuate(proj[:, 1:T_SEQ + 1], n0 + 2, s0)
                    shift(vbuf[:], col(C_MUV))
                    V.tensor_copy(Y[:].rearrange("p e t n -> p (e t) n"), wide(ident, 2 * NB))
                    fence()
                    dve.wait_ge(bonus_done, p + 1)
                    dve.wait_ge(y_stored, p * 16 + 16)
                    V.tensor_tensor(bonus[:], vbuf[:], R[3][:], MUL).then_inc(bonus_read, 1)
                    fill("prep")
                    fill("tok")
                    for t in range(NB):
                        for e in range(2):
                            bank = g_bank(2 * t + e)
                            dve.wait_ge(g_done, p * (2 * NB) + 2 * t + e + 1)
                            V.tensor_tensor(lq[:, e, t].rearrange("p a b -> p (a b)"),
                                            bank[:, P:4 * P], lq_mask, MUL)
                            V.copy_predicated(Y[:, e, t, :], masks[:, 0:P], bank[:, 0:P]
                                              ).then_inc(g_read, 1)
                    fill("solve")
                    for level in range(LEVELS):
                        dve.wait_ge(x_done, p * LEVELS + level + 1)
                        for e in range(2):
                            done = V.tensor_copy(Xc[heads[e], :, heads[1]], of_head(RX[1], e))
                        done.then_inc(xb_read, 1)
                        fill("level_a")
                        for e in range(2):
                            dve.wait_ge(p2_done, p * (2 * LEVELS) + 2 * level + e + 1)
                            dve.sem_inc(p2_seen, 1)
                            mask = masks[:, P + level * HALF:P + (level + 1) * HALF]
                            V.copy_predicated(
                                second_halves(Y[:, e], level),
                                wide(mask, NB).rearrange("p t (g n) -> p t g n", n=2 << level),
                                R_half(RP[e]).rearrange("p t (g n) -> p t g n", n=2 << level)
                            ).then_inc(p2_read, 1)
                        fill("level_b")
                    V.memset(S[:], 0.0).then_inc(s_ready, 1)
                    for n in range(CHUNKS):
                        t, lo = n // 2, CHUNK * (n % 2)
                        dve.wait_ge(m1_done, p * CHUNKS + n + 1)
                        if n == 0:
                            dve.wait_ge(lv_read, p + 1)
                        V.tensor_tensor(rhs[lo:lo + CHUNK, t, :], lv[lo:lo + CHUNK, t, :],
                                        R[2][lo:lo + CHUNK, 0:P], ADD).then_inc(rhs_ready, 1)
                        if n:
                            fill("u")
                            fill("state")
                        fill("rhs")
                        if n + 1 < CHUNKS:
                            end = n * CHUNK + CHUNK - 1
                            dve.wait_ge(m3_done, p * (CHUNKS - 1) + n + 1)
                            dve.wait_ge(sa_ready, p * (CHUNKS - 1) + n + 1)
                            for e in range(2):
                                d = slice(e * HD, e * HD + HD)
                                last = V.scalar_tensor_tensor(S[d, d], R[4][d, d], a_in[d, end:end + 1],
                                                              SA[d, d], MUL, ADD)
                            last.then_inc(s_ready, 1)
                    for place in ("u", "state", "y", "center"):
                        fill(place)
                    dve.wait_ge(var_done, p + 1)
                    V.tensor_scalar(tmp2[:], R[1][:], LNX_EPS, None, ADD).then_inc(var_read, 1)
                    dve.wait_ge(var_root, p + 1)
                    V.reciprocal(tmp1[:], tmp2[:])
                    fence()
                    V.tensor_tensor(kkbuf[:], kkbuf[:], tmp1[:], MUL)
                    fence()
                    V.tensor_scalar(kkbuf[:], kkbuf[:], col(C_LW), col(C_LB), MUL, ADD)
                    fence()
                    V.tensor_tensor(kkbuf[:], kkbuf[:], bonus[:], ADD)
                    fence()
                    V.tensor_tensor(bonus[:], kkbuf[:], gbuf[:], MUL).then_inc(y_fin, 1)

            for k in range(PAIRS, KD):
                dve.wait_ge(yb_hi, k + 1)
                V.tensor_tensor(H_lo[:, k, :], ystage[:, k, :] if k < KD - 1 else bonus[:],
                                H_hi[:, k, :].bitcast(f32), SUB).then_inc(rwkv_lo, 1)

            with dve.Fori(0, KD // 2) as i:
                for u in range(2):
                    m = i * 2 + u
                    a_bank, b_bank = (dense[1], dense[0]) if u == 0 else (R[0], R[1])
                    dve.wait_ge(gin_loaded[u], i * 16 + 16)
                    dve.wait_ge(attn_half, m + 1)
                    V.tensor_tensor(mtmp[:], gin[u][:, 0, :], a_bank[:], MUL)
                    dve.wait_ge(tile_done, m + MERGE0 + 1)
                    V.tensor_tensor(mrg[u][:], gin[u][:, 1, :], b_bank[:], MUL).then_inc(merge_read, 1)
                    fence()
                    V.tensor_tensor(mrg[u][:], mrg[u][:], mtmp[:], ADD).then_inc(mrg_ready, 1)
                    dve.wait_ge(m_hi_ready, m + 1)
                    V.tensor_tensor(tile_of(M_lo, m), mrg[u][:], tile_of(M_hi, m).bitcast(f32), SUB
                                    ).then_inc(m_lo_ready, 1)

            V.memset(sqacc[:], 0.0)
            with dve.Fori(0, KD // 2) as i:
                for u in range(2):
                    m = i * 2 + u
                    bank = dense[(OUT0 + u) % 2]
                    dve.wait_ge(xin_loaded[u], i * 16 + 16)
                    dve.wait_ge(x2_stored[u], i * 16 + 16)
                    dve.wait_ge(tile_done, m + OUT0 + 1)
                    V.tensor_tensor(x2[u][:], xin[u][:], bank[:], ADD).then_inc(bank_read, 1)
                    V.drain().then_inc(x2_ready, 1)
                    dve.wait_ge(x2sq_ready, m + 1)
                    V.tensor_tensor(sqacc[:], sqacc[:], sqx[:], ADD).then_inc(acc_ready, 1)
                    dve.wait_ge(x2_hi, m + 1)
                    V.scalar_tensor_tensor(tile_of(H_lo, m), x2[u][:], norm_g[:, 1, bass.ds(m, 1)],
                                           tile_of(H_hi, m).bitcast(f32), MUL, SUB
                                           ).then_inc(x2_lo, 1)
            dve.wait_ge(ss2_done, 1)
            V.tensor_scalar(rstd[:], R[2][:], 1.0 / D_MODEL, NORM_EPS, MUL, ADD).then_inc(ms2_ready, 1)
            dve.wait_ge(rms2_ready, 1)
            V.reciprocal(rstd[:], rstd[:])
            fence()

            def hidden_tiles(g):
                with dve.Fori(0, FG) as t:
                    n, s, _ = ffn_index(g, t, 0)
                    hn = g * FG + t
                    dve.wait_ge(tile_done, n + 1)
                    V.tensor_tensor(gate_n[:], rstd[:], dense[s][:], MUL).then_inc(bank_read, 1)
                    V.drain().then_inc(gate_n_ready, 1)
                    dve.wait_ge(tile_done, n + 2)
                    V.tensor_tensor(hid[:], rstd[:], dense[1 - s][:], MUL).then_inc(bank_read, 1)
                    fence()
                    dve.wait_ge(silu_ready, hn + 1)
                    V.tensor_tensor(hid[:], hid[:], gate_s[:], MUL).then_inc(hid_ready, 1)
                    dve.wait_ge(g_hi_ready, hn + 1)
                    V.tensor_tensor(tile_of(G_lo, t), hid[:], tile_of(G_hi, t).bitcast(f32), SUB
                                    ).then_inc(g_lo_ready, 1)

            def down_tile(g, i, u):
                n, s, _ = ffn_index(g, i, 2 * FG + u)
                m = i * 2 + u
                dve.wait_ge(tile_done, n + 1)
                V.tensor_tensor(tile_of(resid, m), tile_of(resid, m), dense[s][:], ADD
                                ).then_inc(bank_read, 1)

            with dve.Fori(0, GROUPS_F - 1) as g:
                hidden_tiles(g)
                dve.wait_ge(resid_loaded, 64)
                with dve.Fori(0, KD // 2) as i:
                    for u in range(2):
                        down_tile(g, i, u)
            hidden_tiles(GROUPS_F - 1)
            V.memset(facc[:], 0.0)
            fence()

            def last_down(i, u, add=True):
                down_tile(GROUPS_F - 1, i, u)
                V.drain().then_inc(fin_ready, 1)
                if add:
                    dve.wait_ge(fsq_ready, i * 2 + u + 1)
                    V.tensor_tensor(facc[:], facc[:], fsq[:], ADD).then_inc(acc_ready, 1)

            with dve.Fori(0, KD // 2 - 1) as i:
                for u in range(2):
                    last_down(i, u)
            last_down(KD // 2 - 1, 0)
            last_down(KD // 2 - 1, 1, False)
            dve.wait_ge(ss2_done, 2)
            V.tensor_scalar(rstd[:], R[2][:], 1.0 / D_MODEL, NORM_EPS, MUL, ADD).then_inc(ms2_ready, 1)
            dve.wait_ge(rms2_ready, 2)
            V.reciprocal(rstd[:], rstd[:])
            fence()
            for m in range(KD):
                V.scalar_tensor_tensor(resid[:, m, :], resid[:, m, :], norm_g[:, 2, m:m + 1], rstd[:],
                                       MUL, MUL).then_inc(out_ready, 1)

        @block.tensor
        def _(pe):
            pe.sem_inc(pt_done, 2)
            pe.sem_inc(pv_done, 1)
            pe.sem_inc(ups_done, 2)

            def steps(s, bank, ks, first, last, hi=H_hi, lo=H_lo, w0=0):
                for k in ks:
                    wk = slice((k - w0) * P, (k - w0 + 1) * P)
                    PE.matmul(bank[:], whi[s][:, wk], hi[:, k, :], start=(k == first), stop=False)
                    PE.matmul(bank[:], whi[s][:, wk], lo[:, k, :], start=False, stop=False)
                    done = PE.matmul(bank[:], wlo[s][:, wk], hi[:, k, :], start=False, stop=(k == last))
                return done

            def front_tile(ix):
                n, s, _ = ix
                pe.wait_ge(lo_ready, n + 1)
                pe.wait_ge(evacuated, n + 1)
                steps(s, dense[s], range(KD), 0, KD - 1).then_inc(tile_done, 1)

            ahead, together = 4, 9
            order = [(0, k) for k in range(ahead)]
            for k in range(together):
                order += [(1, k), (0, k + ahead)]
            order += [(0, k) for k in range(together + ahead, KD)]
            order += [(1, k) for k in range(together, KD)]
            for s, k in order:
                if k == 0:
                    pe.wait_ge(lo_ready, s + 1)
                if s == 0:
                    pe.wait_ge(h_lo_ready, k + 1)
                done = steps(s, dense[s], [k], 0, KD - 1)
                if k == KD - 1:
                    done.then_inc(tile_done, 1)
            pe.wait_ge(cst_loaded, 16)
            for j in range(2):
                pe.wait_ge(sq_used[j], KD // 2)
                done = PE.matmul(R[0][:], ones, sqsum[j][:], start=(j == 0), stop=(j == 1))
            done.then_inc(ss_done, 1)
            for n in range(2, ATT_TILES):
                front_tile(index(0, 2, n))

            for g in range(STAGES):
                def next_tile(tile, k):
                    n, s, _ = index(0, 2, FILL_TILE0[g] + tile)
                    if k == 0:
                        pe.wait_ge(lo_ready, n + 1)
                        pe.wait_ge(evacuated, n + 1)
                    done = steps(s, dense[s], [k], 0, KD - 1)
                    if k == KD - 1:
                        done.then_inc(tile_done, 1)

                fill = Fill(next_tile, ATT_FILL[g])

                def scores(w):
                    e, b = w // NB, w % NB
                    pe.wait_ge(pv_read, g * UNITS + w + 1)
                    rows = slice(e * HD, e * HD + HD)
                    k0 = first_key(b)
                    for h in range(GROUP):
                        done = PE.matmul(
                            R[1 + 2 * (w % 2) + h // 2][:, (h % 2) * 2 * BLOCK + k0:(h % 2 + 1) * 2 * BLOCK],
                            qT[g][rows, h, b * BLOCK:(b + 1) * BLOCK],
                            kT[g][rows, (b - 1) * BLOCK + k0:(b + 1) * BLOCK], start=True, stop=True)
                    done.then_inc(scores_done, 1)

                pe.wait_ge(evacuated, (g + 1) * ATT_TILES + 2)
                scores(0)
                pe.wait_ge(pt_read, g * UNITS + 1)
                for t in range(NB):
                    done = PE.transpose(R[0][:, t * P:(t + 1) * P], vT[g][:, t * P:(t + 1) * P], ident)
                done.then_inc(vt_done, 1)
                fill("first")
                for w in range(UNITS):
                    e, b = w // NB, w % NB
                    W = g * UNITS + w
                    if w + 1 < UNITS:
                        scores(w + 1)
                    fill("scores")
                    pe.wait_ge(probs_ready, W + 1)
                    pe.wait_ge(pt_read, W + 1)
                    if w == 0:
                        pe.wait_ge(vtok_ready, g + 1)
                    seen = range(0 if b else 1, 2)
                    for half in seen:
                        bank = (R[5], R[0])[half]
                        for h in range(GROUP):
                            done = PE.transpose(bank[:, h * BLOCK:(h + 1) * BLOCK],
                                                probs[w % 2][:, h, half * BLOCK:(half + 1) * BLOCK],
                                                ident)
                    done.then_inc(pt_done, 1)
                    fill("probs")
                    pe.wait_ge(pt_read, W + 2)
                    cols = slice(e * HD, e * HD + HD)
                    for half in seen:
                        done = PE.matmul(R[1 + 2 * (w % 2)][cols, :], vtok[g][:, b - 1 + half, cols],
                                         pT[:, half, :], start=(half == seen[0]), stop=(half == 1))
                    done.then_inc(pv_done, 1)
                    fill("out")

            with pe.Fori(0, PAIRS // 2) as i:
                for u in range(2):
                    p = i * 2 + u

                    def tile_ix(j):
                        return index(i, 2 * RW_TILES, RW0 + u * RW_TILES + j)

                    def gate_step(tile, k):
                        n, s, _ = tile_ix(3 + tile)
                        if k == 0:
                            pe.wait_ge(lo_ready, n + 1)
                            pe.wait_ge(evacuated, n + 1)
                        done = steps(s, dense[s], [k], 0, KD - 1)
                        if k == KD - 1:
                            done.then_inc(tile_done, 1)

                    fill = Fill(gate_step)
                    front_tile(tile_ix(0))
                    pe.wait_ge(low_ready, 1)
                    pe.wait_ge(pv_read, 2 + STAGES * UNITS)
                    pe.wait_ge(ups_loaded[u], i * 16 + 16)
                    pe.wait_ge(cen_read, p + 1)
                    pe.wait_ge(var_read, p + 1)
                    up = ups[u]
                    PE.matmul(R[0][:], up[0:64, 0, :], low[0][0:64, :], start=True, stop=True)
                    PE.matmul(R[1][:], up[64:128, 0, :], low[0][64:128, :], start=True, stop=True)
                    PE.matmul(R[2][:], up[:, 1, :], low[1][:], start=True, stop=False)
                    rest = GATE_RANK - P
                    PE.matmul(R[2][:], up[0:rest, 2, :], low[2][0:rest, :], start=False, stop=True
                              ).then_inc(ups_done, 1)
                    front_tile(tile_ix(1))
                    pe.wait_ge(ksq_ready, p + 1)
                    PE.matmul(R[3][:], head_ones, tmp1[:], start=True, stop=True).then_inc(kn_done, 1)
                    front_tile(tile_ix(2))
                    fill("prep")
                    pe.wait_ge(prep_ready, p + 1)
                    PE.matmul(R[3][:], head_ones, tmp2[:], start=True, stop=True).then_inc(bonus_done, 1)
                    for bank, src in ((R[1], icl), (R[2], kap), (R[0], vbuf)):
                        if src is vbuf:
                            pe.wait_ge(shifted, p * 3 + N_LOW + 3)
                        for t in range(NB):
                            done = PE.transpose(bank[:, t * P:(t + 1) * P], src[:, t * P:(t + 1) * P],
                                                ident)
                        done.then_inc(tok_done, 1)
                    fill("tok")
                    pe.wait_ge(bonus_read, p + 1)
                    pe.wait_ge(tok_read, p * 3 + 3)
                    for t in range(NB):
                        for e in range(2):
                            w = 2 * t + e
                            bank = g_bank(w)
                            if w >= 4:
                                pe.wait_ge(l_read, p * (2 * NB) + w - 3)
                            tok = slice(t * P, (t + 1) * P)
                            both = zq[heads[e], t].rearrange("p a n -> p (a n)")
                            PE.matmul(bank[:, 0:2 * P], icl[heads[e], tok], both, start=True, stop=True)
                            PE.matmul(bank[:, 2 * P:4 * P], kap[heads[e], tok], both,
                                      start=True, stop=True).then_inc(g_done, 1)
                    fill("solve")
                    pe.wait_ge(g_read, (p + 1) * (2 * NB))
                    pe.wait_ge(l_read, (p + 1) * (2 * NB))
                    for e in range(2):
                        for t in range(NB):
                            done = PE.transpose(RL[e][:, t * P:(t + 1) * P], Lt[:, e, t, :], ident)
                        done.then_inc(ln_done, 1)
                    for t in range(NB):
                        for e in range(2):
                            done = PE.matmul(R[1][:, t * P + e * HD:t * P + e * HD + HD],
                                             lq[:, e, t, 1, :], vtk[:, t, heads[e]],
                                             start=True, stop=True)
                    done.then_inc(lv_done, 1)
                    pe.wait_ge(ln_read, (p + 1) * 2)
                    for level in range(LEVELS):
                        for e in range(2):
                            if level:
                                pe.wait_ge(p2_read, p * (2 * LEVELS) + 2 * level - 1 + e)
                            for t in range(NB):
                                done = PE.matmul(RW[heads[e], t * HALF:(t + 1) * HALF], Ln[:, e, t, :],
                                                 second_halves(Y[:, e, t, :], level),
                                                 start=True, stop=True)
                            if e:
                                done.then_inc(w1_done, 1)
                            for t in range(NB):
                                at = (e * NB + t) * CHUNK
                                for c in range(2):
                                    rows = heads[c]
                                    done = PE.transpose(RX[c][0:CHUNK, at:at + CHUNK],
                                                        Y[rows, e, t, rows], ident[rows, rows])
                        done.then_inc(x_done, 1)
                        fill("level_a")
                        pe.wait_ge(x_read, p * LEVELS + level + 1)
                        pe.wait_ge(xb_read, p * LEVELS + level + 1)
                        pe.wait_ge(w1_read, p * LEVELS + level + 1)
                        for e in range(2):
                            for t in range(NB):
                                if level < LEVELS - 1 or e + t == 0:
                                    done = PE.matmul(RP[e][:, t * HALF:(t + 1) * HALF],
                                                     Xc[heads[e], t, :], W1[heads[e], t, :],
                                                     start=True, stop=True)
                                    continue
                                for lo in (0, CHUNK):
                                    mid, c0 = lo + CHUNK // 2, t * HALF + lo // 2
                                    done = PE.matmul(RP[e][lo:mid, c0:c0 + CHUNK // 2],
                                                     Xc[heads[e], t, lo:mid],
                                                     W1[heads[e], t, lo // 2:mid - lo // 2],
                                                     start=True, stop=True)
                            done.then_inc(p2_done, 1)
                        fill("level_b")
                    pe.wait_ge(p2_read, (p + 1) * (2 * LEVELS))
                    for n in range(CHUNKS):
                        t, lo = n // 2, CHUNK * (n % 2)
                        here = slice(lo, lo + CHUNK)
                        pe.wait_ge(s_ready, p * CHUNKS + n + 1)
                        PE.matmul(R[2][here, 0:P], zq[:, t, 0, here], S[:], start=True, stop=True
                                  ).then_inc(m1_done, 1)
                        PE.matmul(R[5][:, t * P + lo:t * P + lo + CHUNK], S[:], zq[:, t, 1, here],
                                  start=(n % 2 == 0), stop=False, skip_group_check=True)
                        fill("rhs")
                        pe.wait_ge(rhs_ready, p * CHUNKS + n + 1)
                        for e in range(2):
                            done = PE.matmul(R[3][here, heads[e]], Y[:, e, t, here],
                                             rhs[:, t, heads[e]], start=True, stop=True)
                        done.then_inc(m2_done, 1)
                        fill("u")
                        pe.wait_ge(u_ready, p * CHUNKS + n + 1)
                        if n + 1 < CHUNKS:
                            PE.matmul(R[4][:, 0:P], btok[here, t, :], utok[here, t, :],
                                      start=True, stop=False)
                            PE.matmul(R[4][:, 0:P], ktok[here, t, :], vtk[here, t, :],
                                      start=False, stop=True).then_inc(m3_done, 1)
                        if n % 2:
                            for e in range(2):
                                dst = R[5][heads[e], t * P:(t + 1) * P]
                                PE.matmul(dst, utok[:, t, heads[e]], lq[:, e, t, 0, :],
                                          start=False, stop=False, skip_group_check=True)
                                done = PE.matmul(dst, vtk[:, t, heads[e]], lq[:, e, t, 2, :],
                                                 start=False, stop=True, skip_group_check=True)
                            if n + 1 == CHUNKS:
                                done.then_inc(y_done, 1)
                        fill("state")
                    fill("y")
                    pe.wait_ge(y_ready, p + 1)
                    PE.matmul(R[0][:], head_center, csum[:], start=True, stop=True).then_inc(cen_done, 1)
                    fill("center")
                    pe.wait_ge(cen_read, p + 2)
                    PE.matmul(R[1][:], head_mean, tmp1[:], start=True, stop=True).then_inc(var_done, 1)

            pe.wait_ge(evacuated, MERGE0 + 2)
            pe.wait_ge(cen_read, PAIRS + 1)
            pe.wait_ge(var_read, PAIRS + 1)

            halves = ((dense[1], dense[0]), (R[0], R[1]))
            for s in range(2):
                pe.wait_ge(lo_ready, MERGE0 + s + 1)
            def merge_steps(u, half, ks):
                lo_done, flag = ((attn_lo, attn_half), (rwkv_lo, tile_done))[half]
                for k in ks:
                    pe.wait_ge(lo_done, k + 1)
                    done = steps((MERGE0 + u) % 2, halves[u][half], [half * PAIRS + k],
                                 half * PAIRS, half * PAIRS + PAIRS - 1)
                    if k == PAIRS - 1:
                        done.then_inc(flag, 1)

            for k in range(PAIRS):
                for u in range(2):
                    merge_steps(u, 0, [k])
            for u in range(2):
                merge_steps(u, 1, range(PAIRS))
            with pe.Fori(1, KD // 2) as i:
                for u in range(2):
                    n, s, _ = index(i, 2, MERGE0 + u)
                    pe.wait_ge(lo_ready, n + 1)
                    pe.wait_ge(merge_read, n - MERGE0 - 1)
                    for half, flag in ((0, attn_half), (1, tile_done)):
                        ks = range(half * PAIRS, (half + 1) * PAIRS)
                        steps(s, halves[u][half], ks, ks[0], ks[-1]).then_inc(flag, 1)

            def later_tile(ix, ks=KD, hi=H_hi, lo=H_lo):
                n, s, _ = ix
                pe.wait_ge(lo_ready, n + 1)
                pe.wait_ge(bank_read, n - OUT0 + 1)
                steps(s, dense[s], range(ks), 0, ks - 1, hi, lo).then_inc(tile_done, 1)

            def tile_as_ready(ix, ready, count, depth=KD, hi=H_hi, lo=H_lo):
                n, s, _ = ix
                pe.wait_ge(lo_ready, n + 1)
                pe.wait_ge(bank_read, n - OUT0 + 1)
                pe.wait_ge(ready, count - 1)
                steps(s, dense[s], range(depth - 1), 0, depth - 1, hi, lo)
                pe.wait_ge(ready, count)
                steps(s, dense[s], [depth - 1], 0, depth - 1, hi, lo).then_inc(tile_done, 1)

            tile_as_ready(index(0, 2, OUT0), m_lo_ready, KD, KD, M_hi, M_lo)
            later_tile(index(0, 2, OUT0 + 1), KD, M_hi, M_lo)
            with pe.Fori(1, KD // 2) as i:
                for u in range(2):
                    later_tile(index(i, 2, OUT0 + u), KD, M_hi, M_lo)

            def down_tiles(g):
                tile_as_ready(ffn_index(g, 0, 2 * FG), g_lo_ready, g * FG + FG, FG, G_hi, G_lo)
                later_tile(ffn_index(g, 0, 2 * FG + 1), FG, G_hi, G_lo)
                with pe.Fori(1, KD // 2) as i:
                    for u in range(2):
                        later_tile(ffn_index(g, i, 2 * FG + u), FG, G_hi, G_lo)

            tile_as_ready(ffn_index(0, 0, 0), x2_lo, KD)
            PE.matmul(R[2][:], ones, sqacc[:], start=True, stop=True).then_inc(ss2_done, 1)
            later_tile(ffn_index(0, 0, 1))
            with pe.Fori(1, FG) as t:
                for u in range(2):
                    later_tile(ffn_index(0, t, u))
            down_tiles(0)
            with pe.Fori(1, GROUPS_F) as g:
                with pe.Fori(0, FG) as t:
                    for u in range(2):
                        later_tile(ffn_index(g, t, u))
                down_tiles(g)
            pe.wait_ge(acc_ready, 2 * KD)
            PE.matmul(R[2][:], ones, facc[:], start=True, stop=False)
            pe.wait_ge(fsq_ready, KD)
            PE.matmul(R[2][:], ones, fsq[:], start=False, stop=True).then_inc(ss2_done, 1)


def _tiles(w):
    k, n = w.shape
    return np.ascontiguousarray(w.reshape(k // P, P, n // P, P).transpose(2, 1, 0, 3)).reshape(n // P, P, k)


def _shape_constants():
    i = np.arange(P)
    eye = np.eye(P, dtype=np.float32)
    head = (i[:, None] // HD == i[None, :] // HD).astype(np.float32)
    consts = np.stack([eye, np.ones((P, P), np.float32), head, head / HD, eye - head / HD], 1)
    s, t = i[:, None], i[None, :]
    same = s // CHUNK == t // CHUNK
    lq_mask = np.stack([same & (t >= s), same & (t > s), same & (t >= s)], 1).astype(np.float32)
    scan = np.broadcast_to((np.arange(T_SEQ) % CHUNK != 0).astype(np.float32), (P, T_SEQ))
    scan_lq = np.concatenate([scan, lq_mask.reshape(P, 3 * P)], 1)
    levels = []
    for l in range(LEVELS + 1):
        cols = t[:, (i >> l) % 2 == 1] if l else t
        levels.append((s // (2 << l) == cols // (2 << l)) & ((s >> l) % 2 == 0)
                      & ((cols >> l) % 2 == 1))
    levels = np.concatenate(levels, 1).astype(np.float32)
    q, k = np.arange(BLOCK)[:, None], np.arange(2 * BLOCK)[None, :]
    d = BLOCK + q - k
    valid = (d >= 0) & (d < BLOCK)
    masked = np.float32(-1e30)
    dist = np.where(valid, -d, masked)
    slopes = np.broadcast_to(2.0 ** (-8.0 * np.arange(1, HEADS + 1) / HEADS), (P, HEADS))
    att = np.concatenate([dist, slopes], 1).astype(np.float32)
    return consts, np.ascontiguousarray(scan_lq), levels, np.ascontiguousarray(att)


def kernel(**inputs):
    import concourse.bacc as _bacc
    from concourse.bass_utils import run_bass_kernel_spmd as _run

    a = {k: np.asarray(v) for k, v in inputs.items()}
    w_in = a["w_in"][0]
    at = np.cumsum([0, WIDTH, KV_WIDTH, KV_WIDTH, WIDTH, WIDTH, WIDTH, DECAY_RANK, ICLR_RANK,
                    GATE_RANK, D_MODEL, D_MODEL])
    wq, wk, wv, wr, wrk, wrv, wdw, wda, wdg, wga, wgb = (
        w_in[:, at[j]:at[j + 1]] for j in range(11))
    order = []
    for gp in range(KV_HEADS // 2):
        order += [wk[:, gp * P:(gp + 1) * P], wv[:, gp * P:(gp + 1) * P]]
        for h in range(GROUP):
            for e in range(2):
                head = (2 * gp + e) * GROUP + h
                order.append(wq[:, head * HD:(head + 1) * HD])
    order += [wdw, wda, wdg, np.zeros((D_MODEL, 2 * P - GATE_RANK), np.float32)]
    for p in range(PAIRS):
        c = slice(p * P, (p + 1) * P)
        order += [wrk[:, c], wr[:, c], wrv[:, c]]
        for m in (2 * p, 2 * p + 1):
            order += [wga[:, m * P:(m + 1) * P], wgb[:, m * P:(m + 1) * P]]
    w_front = _tiles(np.concatenate(order, 1))

    gate_up = np.concatenate([a["gate_up"][0], np.zeros((2 * P - GATE_RANK, WIDTH), np.float32)], 0)
    ups = np.concatenate([a["decay_up"][0], a["iclr_up"][0], gate_up], 0)
    w_ups = np.ascontiguousarray(ups.reshape(3, P, PAIRS, P).transpose(2, 1, 0, 3))

    wba = a["w_branch_attn"][0].reshape(KV_HEADS // 2, 2, GROUP, HD, D_MODEL).transpose(0, 2, 1, 3, 4)
    w_branch = _tiles(np.concatenate([wba.reshape(WIDTH, D_MODEL), a["w_branch_rwkv"][0]], 0))
    w_slots = np.concatenate([w_front, w_branch, _tiles(a["w_out"][0])], 0)
    gt, ut = _tiles(a["ffn_gate"][0]), _tiles(a["ffn_up"][0])
    w_gu = np.ascontiguousarray(np.stack([gt, ut], 1)).reshape(2 * gt.shape[0], P, SLOT)
    down = a["ffn_down"][0].reshape(GROUPS_F, DSLOT, D_MODEL)
    w_down = np.concatenate([_tiles(down[g]) for g in range(GROUPS_F)], 0)

    norms = np.ascontiguousarray(np.stack(
        [a["norm_mix"][0], a["norm_ffn"][0], a["norm_final"]], 0).reshape(3, KD, P).transpose(2, 0, 1))
    mu = a["tshift_mix"][0]
    mu_r, mu_k, mu_v, mu_low = mu[:WIDTH], mu[WIDTH:2 * WIDTH], mu[2 * WIDTH:3 * WIDTH], mu[3 * WIDTH:]
    pair_cst = np.stack([mu_k, mu_r, mu_v, a["decay_bias"][0], a["iclr_bias"][0], a["k_k"][0],
                         a["k_a"][0], a["r_k"][0].reshape(WIDTH), a["lnx_w"][0], a["lnx_b"][0]], 0)
    pair_cst = np.ascontiguousarray(pair_cst.reshape(NCST, PAIRS, P).transpose(2, 1, 0))
    low_mu = np.concatenate([mu_low, np.zeros(3 * P - mu_low.shape[0], np.float32)])
    low_mu = np.ascontiguousarray(low_mu.reshape(3, P).T)
    sinks = np.ascontiguousarray(np.broadcast_to(a["attn_sinks"][0], (P, HEADS)))
    consts, scan_lq, levels, att_cst = _shape_constants()

    arrays = {
        "xT": np.ascontiguousarray(a["x"][0].T).reshape(KD, P, T_SEQ), "w_slots": w_slots,
        "w_ups": w_ups, "w_gu": w_gu, "w_down": w_down,
        "norms": norms, "pair_cst": pair_cst, "low_mu": low_mu, "sinks": sinks, "consts": consts,
        "scan_lq": scan_lq, "level_masks": levels, "att_cst": att_cst}
    nc = _bacc.Bacc("TRN2", target_bir_lowering=False, num_devices=1)
    args = {n: nc.dram_tensor(n, v.shape, mybir.dt.from_np(v.dtype), kind="ExternalInput").ap()
            for n, v in arrays.items()}
    out = nc.dram_tensor("out", (KD, P, T_SEQ), mybir.dt.float32, kind="ExternalOutput").ap()
    build_layer(nc, out=out, **args)
    r = _run(nc, [arrays], core_ids=[0])
    return np.ascontiguousarray(r.results[0]["out"].reshape(D_MODEL, T_SEQ).T)[None]
```
